# Optimizing a Trainium2 kernel written in Bass

```python
import jax, jax.numpy as jnp
from jax import lax
import numpy as np

D_MODEL = 2048
BATCH = 1
SEQ = 256
DEPTH = 1
DEC_BATCH = 8
DEC_SEQ = 4
PAST_LEN = 2048
PAGE_SIZE = 128

MIX_WIDTH = D_MODEL
N_HEADS = 8
QK_NOPE = 128
QK_ROPE = 64
QK_HEAD = QK_NOPE + QK_ROPE
V_HEAD = 128
ATTN_WIDTH = N_HEADS * V_HEAD
Q_LORA = 512
KV_LORA = 256
POOL_WIDTH = MIX_WIDTH - ATTN_WIDTH
POOL_WINDOWS = (2, 4, 8, 16)
N_POOL_GROUPS = len(POOL_WINDOWS)
POOL_GROUP = POOL_WIDTH // N_POOL_GROUPS
POOL_HIST = max(POOL_WINDOWS) - 1
IN_WIDTH = Q_LORA + KV_LORA + QK_ROPE + POOL_WIDTH
SPLITS = (Q_LORA, Q_LORA + KV_LORA, Q_LORA + KV_LORA + QK_ROPE)
D_FF = ((8 * D_MODEL + 3 * 256 - 1) // (3 * 256)) * 256
ROPE_THETA = 10000.0
EPS = 1e-6
Q_BLOCK = 128
SCALE = QK_HEAD ** -0.5

kernel_name = "hymba_mla_multiscale_pool_adaln_step"

def rms_norm(x, w):
    xf = x.astype(jnp.float32)
    y = xf * lax.rsqrt(jnp.mean(xf * xf, axis=-1, keepdims=True) + EPS)
    return (y * w.astype(jnp.float32)).astype(x.dtype)

def rope_tables(pos):
    inv = 1.0 / (ROPE_THETA ** (jnp.arange(0, QK_ROPE, 2, dtype=jnp.float32) / QK_ROPE))
    ang = pos.astype(jnp.float32)[:, None] * inv[None, :]
    return jnp.cos(ang), jnp.sin(ang)

def apply_rope(x, cos, sin):
    x1, x2 = jnp.split(x.astype(jnp.float32), 2, axis=-1)
    return jnp.concatenate([x1 * cos - x2 * sin, x1 * sin + x2 * cos], axis=-1).astype(x.dtype)

def qk_gain(g_nope, g_rope_half):
    return jnp.concatenate([g_nope, g_rope_half, g_rope_half], axis=-1)

def mixer_inputs(x, c, pos, w_mod, b_mod, norm1, w_in, q_a_norm, w_q_b, kv_a_norm, q_gain):
    B, T, _ = x.shape
    mod = jax.nn.silu(c) @ w_mod + b_mod
    sh1, sc1, g1, sh2, sc2, g2 = jnp.split(mod[:, None, :], 6, axis=-1)
    h = rms_norm(x, norm1) * (1.0 + sc1) + sh1
    z = h @ w_in
    c_q, c_kv, k_r, u = jnp.split(z, SPLITS, axis=-1)
    cos, sin = rope_tables(pos)
    q = (rms_norm(c_q, q_a_norm) @ w_q_b).reshape(B, T, N_HEADS, QK_HEAD)
    q = jnp.concatenate([q[..., :QK_NOPE], apply_rope(q[..., QK_NOPE:], cos[:, None], sin[:, None])], axis=-1)
    q = rms_norm(q, q_gain)
    lat = rms_norm(c_kv, kv_a_norm)
    k_r = apply_rope(k_r, cos, sin)
    return q, lat, k_r, u, (g1, sh2, sc2, g2)

def expand_kv(lat, k_rope, w_kv_b, k_gain):
    kv = (lat @ w_kv_b).reshape(lat.shape[:-1] + (N_HEADS, QK_NOPE + V_HEAD))
    k_nope, v = jnp.split(kv, [QK_NOPE], axis=-1)
    k_r = jnp.broadcast_to(k_rope[..., None, :], k_nope.shape[:-1] + (QK_ROPE,))
    k = rms_norm(jnp.concatenate([k_nope, k_r], axis=-1), k_gain)
    return k, v

def attend(q, k, v, q_pos, k_pos):
    s = jnp.einsum('bqhd,bkhd->bhqk', q, k, preferred_element_type=jnp.float32) * SCALE
    s = jnp.where(k_pos[None, :] <= q_pos[:, None], s, -jnp.inf)
    p = jax.nn.softmax(s, axis=-1).astype(v.dtype)
    return jnp.einsum('bhqk,bkhd->bqhd', p, v)

def prompt_attention(q, k, v):
    B, S = q.shape[0], q.shape[1]
    nb = S // Q_BLOCK
    qb = q.reshape(B, nb, Q_BLOCK, N_HEADS, QK_HEAD).transpose(1, 0, 2, 3, 4)
    k_pos = jnp.arange(S)

    def one_block(args):
        i, qi = args
        return attend(qi, k, v, i * Q_BLOCK + jnp.arange(Q_BLOCK), k_pos)

    o = lax.map(one_block, (jnp.arange(nb), qb))
    return o.transpose(1, 0, 2, 3, 4).reshape(B, S, ATTN_WIDTH)

def sample_attention(q, lat_new, kr_new, cache_lat, cache_kr, page_table, w_kv_b, k_gain):
    Bd, T = q.shape[0], q.shape[1]
    past = page_table.shape[1] * cache_lat.shape[1]
    k_pos = jnp.arange(past + T)
    q_pos = past + jnp.arange(T)

    def one_seq(args):
        pt, qi, ln, kn = args
        lat = jnp.concatenate([cache_lat[pt].reshape(past, KV_LORA), ln], axis=0)
        kr = jnp.concatenate([cache_kr[pt].reshape(past, QK_ROPE), kn], axis=0)
        k, v = expand_kv(lat, kr, w_kv_b, k_gain)
        return attend(qi[None], k[None], v[None], q_pos, k_pos)[0]

    o = lax.map(one_seq, (page_table, q, lat_new, kr_new))
    return o.reshape(Bd, T, ATTN_WIDTH)

def pool_mix(u, hist, first_pos, w_pool, b_pool, pool_scale):
    B, T, _ = u.shape
    full = jnp.concatenate([hist, u], axis=1)
    cs = jnp.cumsum(full.astype(jnp.float32), axis=1)
    cs = jnp.concatenate([jnp.zeros_like(cs[:, :1]), cs], axis=1)
    pos = first_pos + jnp.arange(T)
    end = POOL_HIST + 1
    means = []
    for g, w in enumerate(POOL_WINDOWS):
        ch = slice(g * POOL_GROUP, (g + 1) * POOL_GROUP)
        s = cs[:, end:end + T, ch] - cs[:, end - w:end - w + T, ch]
        cnt = jnp.minimum(pos + 1, w).astype(jnp.float32)
        means.append(s / cnt[None, :, None])
    d = (jnp.concatenate(means, axis=-1) - u.astype(jnp.float32)).reshape(B, T, N_POOL_GROUPS, POOL_GROUP)
    o = jnp.einsum('btgc,gcd->btgd', d, w_pool.astype(jnp.float32)) + b_pool
    o = (o.reshape(B, T, POOL_WIDTH) * pool_scale).astype(u.dtype)
    return o, full[:, -POOL_HIST:]

def layer_out(x, attn_o, pool_o, mods, w_out, norm2, w_gate, w_up, w_down):
    g1, sh2, sc2, g2 = mods
    x = x + g1 * (jnp.concatenate([attn_o, pool_o], axis=-1) @ w_out)
    h = rms_norm(x, norm2) * (1.0 + sc2) + sh2
    f = (jax.nn.silu(h @ w_gate) * (h @ w_up)) @ w_down
    return x + g2 * f

def setup_inputs(seed: int = 0) -> dict:
    key = jax.random.key(seed)
    keys = iter(jax.random.split(key, 40))

    def normal(shape, scale):
        return scale * jax.random.normal(next(keys), shape, jnp.float32)

    def gain(shape):
        return 1.0 + 0.1 * jax.random.normal(next(keys), shape, jnp.float32)

    L = DEPTH
    n_pages = PAST_LEN // PAGE_SIZE
    n_used = DEC_BATCH * n_pages
    n_phys = (n_used * 5) // 4
    page_table = jax.random.permutation(next(keys), n_phys)[:n_used].reshape(DEC_BATCH, n_pages).astype(jnp.int32)
    return {
        'x_prompt': normal((BATCH, SEQ, D_MODEL), 1.0),
        'x_sample': normal((DEC_BATCH, DEC_SEQ, D_MODEL), 1.0),
        'cache_kv_latent': normal((L, n_phys, PAGE_SIZE, KV_LORA), 1.0),
        'cache_k_rope': normal((L, n_phys, PAGE_SIZE, QK_ROPE), 1.0),
        'state_pool': normal((L, DEC_BATCH, POOL_HIST, POOL_WIDTH), 1.0),
        'page_table': page_table,
        'c_prompt': normal((BATCH, D_MODEL), 1.0),
        'c_sample': normal((DEC_BATCH, D_MODEL), 1.0),
        'w_mod': normal((L, D_MODEL, 6 * D_MODEL), 0.5 * D_MODEL ** -0.5),
        'b_mod': normal((L, 6 * D_MODEL), 0.01),
        'norm1': gain((L, D_MODEL)),
        'w_in': normal((L, D_MODEL, IN_WIDTH), D_MODEL ** -0.5),
        'q_a_norm': gain((L, Q_LORA)),
        'w_q_b': normal((L, Q_LORA, N_HEADS * QK_HEAD), Q_LORA ** -0.5),
        'kv_a_norm': gain((L, KV_LORA)),
        'w_kv_b': normal((L, KV_LORA, N_HEADS * (QK_NOPE + V_HEAD)), KV_LORA ** -0.5),
        'q_norm_nope': gain((L, QK_NOPE)),
        'q_norm_rope': gain((L, QK_ROPE // 2)),
        'k_norm_nope': gain((L, QK_NOPE)),
        'k_norm_rope': gain((L, QK_ROPE // 2)),
        'w_pool': normal((L, N_POOL_GROUPS, POOL_GROUP, POOL_GROUP), POOL_GROUP ** -0.5),
        'b_pool': normal((L, N_POOL_GROUPS, POOL_GROUP), 0.01),
        'pool_scale': gain((L, POOL_WIDTH)),
        'w_out': normal((L, MIX_WIDTH, D_MODEL), MIX_WIDTH ** -0.5),
        'norm2': gain((L, D_MODEL)),
        'w_gate': normal((L, D_MODEL, D_FF), D_MODEL ** -0.5),
        'w_up': normal((L, D_MODEL, D_FF), D_MODEL ** -0.5),
        'w_down': normal((L, D_FF, D_MODEL), D_FF ** -0.5),
    }

def reference(x_prompt, x_sample, cache_kv_latent, cache_k_rope, state_pool, page_table, c_prompt, c_sample,
              w_mod, b_mod, norm1, w_in, q_a_norm, w_q_b, kv_a_norm, w_kv_b,
              q_norm_nope, q_norm_rope, k_norm_nope, k_norm_rope,
              w_pool, b_pool, pool_scale, w_out, norm2, w_gate, w_up, w_down):
    S = x_prompt.shape[1]
    T = x_sample.shape[1]
    past = page_table.shape[1] * cache_kv_latent.shape[2]
    pos_p = jnp.arange(S)
    pos_s = past + jnp.arange(T)
    yp, ys = x_prompt, x_sample
    lat_p_all, kr_p_all, pool_p_all = [], [], []
    lat_s_all, kr_s_all, pool_s_all = [], [], []
    for l in range(DEPTH):
        q_gain = qk_gain(q_norm_nope[l], q_norm_rope[l])
        k_gain = qk_gain(k_norm_nope[l], k_norm_rope[l])
        qp, latp, krp, up, modp = mixer_inputs(yp, c_prompt, pos_p, w_mod[l], b_mod[l], norm1[l], w_in[l],
                                               q_a_norm[l], w_q_b[l], kv_a_norm[l], q_gain)
        kp, vp = expand_kv(latp, krp, w_kv_b[l], k_gain)
        ap = prompt_attention(qp, kp, vp)
        hist0 = jnp.zeros((up.shape[0], POOL_HIST, POOL_WIDTH), up.dtype)
        pp, hp = pool_mix(up, hist0, 0, w_pool[l], b_pool[l], pool_scale[l])
        yp = layer_out(yp, ap, pp, modp, w_out[l], norm2[l], w_gate[l], w_up[l], w_down[l])
        qs, lats, krs, us, mods = mixer_inputs(ys, c_sample, pos_s, w_mod[l], b_mod[l], norm1[l], w_in[l],
                                               q_a_norm[l], w_q_b[l], kv_a_norm[l], q_gain)
        a_s = sample_attention(qs, lats, krs, cache_kv_latent[l], cache_k_rope[l], page_table, w_kv_b[l], k_gain)
        ps, hs = pool_mix(us, state_pool[l], past, w_pool[l], b_pool[l], pool_scale[l])
        ys = layer_out(ys, a_s, ps, mods, w_out[l], norm2[l], w_gate[l], w_up[l], w_down[l])
        lat_p_all.append(latp); kr_p_all.append(krp); pool_p_all.append(hp)
        lat_s_all.append(lats); kr_s_all.append(krs); pool_s_all.append(hs)
    new_lat_p = jnp.stack(lat_p_all)
    new_kr_p = jnp.stack(kr_p_all)
    new_pool_p = jnp.stack(pool_p_all)
    new_lat_s = jnp.stack(lat_s_all)
    new_kr_s = jnp.stack(kr_s_all)
    new_pool_s = jnp.stack(pool_s_all)
    return (yp, ys, new_lat_p, new_kr_p, new_pool_p, new_lat_s, new_kr_s, new_pool_s)


_drawn_inputs = setup_inputs


def setup_inputs(seed=0):
    import zlib

    import numpy as np

    out = dict(_drawn_inputs(seed))
    spreads = {}
    factors = {'cache_kv_latent': 7.335,
     'cache_k_rope': 8.0,
     'b_mod': 4.245,
     'q_a_norm': 8.0,
     'q_norm_nope': 8.0,
     'q_norm_rope': 8.0,
     'k_norm_nope': 8.0,
     'k_norm_rope': 8.0,
     'b_pool': 8.0,
     'pool_scale': 2.857}
    for name, (base, spread) in spreads.items():
        noise = np.random.default_rng([zlib.crc32(name.encode()), seed]).standard_normal(out[name].shape)
        drawn = base * np.exp(spread * noise) if base else spread * noise
        out[name] = __import__('jax').numpy.asarray(drawn.astype(out[name].dtype))
    for name, factor in factors.items():
        out[name] = (out[name] * factor).astype(out[name].dtype)
    return out
```

```python
from contextlib import ExitStack, contextmanager

import numpy as np

import concourse.bass as bass
from concourse import mybir

P = 128
F32 = mybir.dt.float32
F32R = mybir.dt.float32r
I32 = mybir.dt.int32
ALU = mybir.AluOpType
ACT = mybir.ActivationFunctionType
AX = mybir.AxisListType.X
ds = bass.ds

EPS = 1e-6
ROPE_THETA = 10000.0
POOL_WINDOWS = (2, 4, 8, 16)
NEG = -1e30


class Signal:

    def __init__(self, sem, credit=0):
        self.sem, self.credit = sem, credit

    def open(self, eng):
        if self.credit:
            eng.sem_inc(self.sem, self.credit)

    def up(self, ins):
        return ins.then_inc(self.sem, 1)

    def wait(self, eng, n):
        value = n + self.credit
        if isinstance(value, int) and value <= 0:
            return
        eng.wait_ge(self.sem, value)


class Stages:

    def __init__(self, sem, names):
        self.sem, self.at, self.n = sem, {x: i + 1 for i, x in enumerate(names)}, 0
        assert len(self.at) == len(names)

    def up(self, ins, name):
        self.n += 1
        assert self.at[name] == self.n, (name, self.n, self.at[name])
        return ins.then_inc(self.sem, 1)

    def wait(self, eng, name):
        eng.wait_ge(self.sem, self.at[name])


class Chain:

    def __init__(self, eng, sem):
        self.eng, self.sem, self.n, self.loops = eng, sem, 0, []

    def value(self):
        v = self.n
        for i, per in self.loops:
            v = i * per + v
        return v

    def link(self, ins):
        ins.then_inc(self.sem, 1)
        self.n += 1
        self.eng.wait_ge(self.sem, self.value())

    @contextmanager
    def loop(self, count, per):
        start = self.n
        with self.eng.Fori(0, count) as i:
            self.loops.append((i, per))
            yield i
            self.loops.pop()
        assert self.n - start == per, (self.n - start, per)
        self.n = start + count * per


def hybrid_step(nc, t, o):
    S = t["x_prompt"].shape[1]
    NB, NT = t["x_sample"].shape[:2]
    D = t["x_prompt"].shape[2]
    _, NPHYS, PAGE, KVL = t["cache_kv_latent"].shape
    RP = t["cache_k_rope"].shape[3]
    HALF = RP // 2
    NPG = t["page_table"].shape[1]
    QL = t["q_a_norm"].shape[1]
    NOPE = t["q_norm_nope"].shape[1]
    QKH = NOPE + RP
    H = t["w_q_b"].shape[2] // QKH
    HIST = t["state_pool"].shape[2]
    PW = t["pool_scale"].shape[1]
    FF = t["w_gate"].shape[2]
    SCALE = float(QKH) ** -0.5
    NS = NB * NT
    T = S + NS
    NV = 1 + NB
    KD = D // P
    KQ = QL // P
    KL = KVL // P
    KU = PW // P
    NG = 6
    TILES = NB * NPG
    TOK = [(0, P), (P, P), (S, NS)]
    HF = FF // P // 2
    HD = HF // 2
    EXT = HIST + S + NB * (HIST + NT)
    SEG = HIST + NT
    assert S == 2 * P and PAGE == P and NOPE == P and KL == 2 and KD == 16 and NS == 32 and NPG == 16

    with ExitStack() as ctx:
        sem = lambda name: ctx.enter_context(nc.semaphore(name))

        BASE = (nc.sbuf_base + 63) // 64 * 64
        top = [BASE]

        def region(nbytes):
            at = top[0]
            top[0] += (nbytes + 31) // 32 * 32
            assert top[0] <= nc.sbuf_usable_end, (top[0], nc.sbuf_usable_end)
            return at

        def sb(name, shape, dt, at=None):
            n = int(np.prod(shape[1:])) * 4
            if at is None:
                at = region(n)
            return nc.alloc_sbuf_tensor_at(name, shape, dt, offset=at)

        RX = region(KD * T * 4)
        RH = region(2 * KD * T * 4)
        RM = region(2 * HF * T * 4)
        RRAW = region(4 * KD * P * 4)
        RCONV = region(4 * KD * P * 4)
        RW = region(2 * KL * H * 2 * P * 4 // 2 + H * KVL * 4)
        HT_BYTES = KD * T * 4
        MIX = KU * T * 4

        xT = sb("xT", [P, KD, T], F32, RX)
        hT_hi = sb("hT_hi", [P, KD, T], F32R, RH)
        hT_lo = sb("hT_lo", [P, KD, T], F32R, RH + HT_BYTES)
        raw = [sb(f"raw{s}", [P, KD * P], F32, RRAW + s * KD * P * 4) for s in range(4)]
        conv_hi = [sb(f"conv_hi{s}", [P, KD * P], F32R, RCONV + 2 * s * KD * P * 4) for s in range(2)]
        conv_lo = [sb(f"conv_lo{s}", [P, KD * P], F32R, RCONV + (2 * s + 1) * KD * P * 4) for s in range(2)]
        wkv = sb("wkv", [P, KL, H, 2, P], F32, RW)
        wkT = sb("wkT", [P, H, KVL], F32, RW + KL * H * 2 * P * 4)
        modT = sb("modT", [P, NG, KD, NV], F32)
        rinv = sb("rinv", [P, TILES + 3, H], F32)
        krs = sb("krs", [P, TILES + 3], F32)
        ident = sb("ident", [P, P], F32)
        ones = sb("ones", [P, P], F32)
        cos = sb("cos", [P, 3, HALF], F32)
        sin = sb("sin", [P, 3, HALF], F32)
        ratio = sb("ratio", [P, 4, 16], F32)
        vecT = sb("vecT", [P, 2 * KD + KQ + 2 * KU], F32)
        gqk = sb("gqk", [P, QKH], F32)
        lattok = sb("lattok", [P, 3, KVL + RP], F32)
        stat = sb("stat", [P, 64], F32)
        pages_sb = sb("pages_sb", [1, TILES], I32)
        NVEC = 2 * KD + KQ + 2 * KU
        norm1T, norm2T = vecT[:, 0:KD], vecT[:, KD:2 * KD]
        qaT = vecT[:, 2 * KD:2 * KD + KQ]
        bpoolT = vecT[:, 2 * KD + KQ:2 * KD + KQ + KU]
        pscaleT = vecT[:, 2 * KD + KQ + KU:NVEC]
        wk_hi = sb("wk_hi", [P, KL, H * P], F32R, RM)
        wk_lo = sb("wk_lo", [P, KL, H * P], F32R, RM + 8192)
        sq = [sb(f"sq{s}", [P, H * P], F32, RM + 16384 + 4096 * s) for s in range(2)]
        sq_x = sb("sq_x", [P, D], F32, RM + 16384)
        latT_hi = [sb(f"latT_hi{s}", [P, KL, P], F32R, RM + 24576 + 2048 * s) for s in range(2)]
        latT_lo = [sb(f"latT_lo{s}", [P, KL, P], F32R, RM + 24576 + 2048 * s + 1024) for s in range(2)]
        pg = [sb(f"pg{s}", [P, KVL + RP], F32, RM + 28672 + 1280 * s) for s in range(4)]
        rxB = sb("rxB", [P, T], F32, RM + 33792)
        kvgain = sb("kvgain", [P, KVL], F32, RM + 34944)
        gk = sb("gk", [P, QKH], F32, RM + 35968)
        assert 35968 + QKH * 4 <= 4 * MIX
        hist_st = sb("hist_st", [NB * HIST, PW], F32, RH)
        cs = sb("cs", [P, KD, 32], F32, RH + 4096)
        modrow = sb("modrow", [P, 512], F32, RH + 6144)
        bmod_st = sb("bmod_st", [NG * KD, P], F32, RH + 8192)
        vec_st = sb("vec_st", [NVEC, P], F32, RH + 8704)
        bmodT = sb("bmodT", [P, NG * KD], F32, RH + 9216)
        diag_x = sb("diag_x", [P, 3, P], F32, RH + 9600)
        x_st = sb("x_st", [P, 3, D], F32, RCONV)
        c_st = sb("c_st", [NV, D], F32, RCONV + 3 * D * 4)
        kr_junk = [sb(f"kr_junk{s}", [P, RP], F32, RCONV + 2560 + 256 * s) for s in range(4)]
        h32 = [sb(f"h32_{s}", [P, T], F32, RCONV + 1152 * s) for s in range(2)]
        zT = sb("zT", [P, 7, T], F32, RM)
        sqz = sb("sqz", [P, KQ, T], F32, RM + MIX)
        sqq = sb("sqq", [P, H * QKH], F32, RM + MIX)
        kvtok = sb("kvtok", [P, 3, KVL + RP], F32, RM + 2 * MIX)
        rope_t = [sb(f"rope_t{j}", [P, H, HALF], F32, RM + 2 * MIX + 3840 + 1024 * j) for j in range(4)]
        sqk = sb("sqk", [P, H * P], F32, RM + MIX)
        sqk2 = sb("sqk2", [P, H * P], F32, RM + MIX + 4096)
        rqB = sb("rqB", [P, T], F32, RM + 3 * MIX)
        uext = sb("uext", [P, KU, EXT], F32, RM + 4 * MIX)
        wqb = sb("wqb", [P, KQ, H * QKH], F32, RRAW)
        wpool = sb("wpool", [P, 4, 2, 2 * P], F32, RRAW + 3 * KD * P * 4)
        qtok = sb("qtok", [P, 3, H, QKH], F32, RH)
        qnT = sb("qnT", [P, H, T], F32, RH + 18432)
        win = [sb(f"win{s}", [P, 2, EXT], F32, RH + 27648 + 3392 * s) for s in range(2)]
        dT = sb("dT", [P, 2, T], F32, RH + 34432)
        unew = sb("unew", [P, KU, NS], F32, RH + 27648)
        ustate = sb("ustate", [NS, PW], F32, RH + 4096)
        ustate_p = sb("ustate_p", [HIST, PW], F32, RH)
        kvjunk = sb("kvjunk", [P, KVL], F32, RM + MIX + 4608)
        ptmp = [sb(f"ptmp{s}", [P, T], F32, RM + 2 * MIX + 3840 + 1152 * s) for s in range(2)]
        qabs = sb("qabs", [P, KL, H, T], F32, RCONV)
        qrT = sb("qrT", [RP, H, T], F32, RCONV + 18432)
        latTn = sb("latTn", [P, KL, T], F32, RCONV + 27648)
        krTn = sb("krTn", [RP, T], F32, RCONV + 27648 + 2304)
        mix_hi = sb("mix_hi", [P, KD, T], F32R, RM)
        mix_lo = sb("mix_lo", [P, KD, T], F32R, RM + 2 * MIX)
        lat_pg = [[sb(f"lat_pg{a}_{j}", [P, KVL], F32, RH + (a * NPG + j) * KVL * 4) for j in range(NPG)] for a in range(2)]
        kr_pg = [sb(f"kr_pg{j}", [P, RP], F32, RH + 2 * NPG * KVL * 4 + j * RP * 4) for j in range(NPG)]
        A0 = RM + 4 * MIX
        causal = sb("causal", [P, 2 * P], F32, A0)
        newmask = sb("newmask", [NS, NS], F32, A0 + 1024)
        pT = [sb(f"pT{s}", [P, 3, P], F32, A0 + 1152 + 1536 * s) for s in range(2)]
        st = [sb(f"st{s}", [P, NPG, H * NT], F32, A0 + 4224 + 2048 * s) for s in range(2)]
        sN = sb("sN", [NS, H, NS], F32, A0 + 8320)
        pN = [sb(f"pN{s}", [NS, H * NT], F32, A0 + 9344 + 128 * s) for s in range(2)]
        olS = sb("olS", [P, KL, H, NS], F32, A0 + 9600)
        smx = [sb(f"smx{s}", [P, 32], F32, A0 + 11648 + 128 * s) for s in range(2)]
        sdg = [sb(f"sdg{s}", [32, 32], F32, A0 + 11904 + 128 * s) for s in range(2)]
        sdn = [sb(f"sdn{s}", [P, 32], F32, A0 + 12160 + 128 * s) for s in range(2)]
        srd = [sb(f"srd{s}", [P, 32], F32, A0 + 12416 + 128 * s) for s in range(2)]
        B0 = RW + KL * H * 2 * P * 4
        stp = [sb(f"stp{s}", [P, 3 * P], F32, B0 + 1536 * s) for s in range(2)]
        olp = [sb(f"olp{s}", [P, KL, 2 * P], F32, B0 + 3072 + 2048 * s) for s in range(2)]
        rdps = [sb("rdp0", [P, 2 * P], F32, B0 + 7168), sb("rdp1", [P, 2 * P], F32, RCONV + 31616)]
        mxp = sb("mxp", [P, P], F32, RCONV + 31104)
        dgp = sb("dgp", [P, 2, P], F32, A0 + 12544)
        assert 12544 + 1024 <= 2 * HF * T * 4 - 4 * MIX
        tmpC = [sb(f"tmpC{s}", [P, T], F32, RW + 1152 * s) for s in range(4)]
        rn2 = sb("rn2", [P, T], F32, RW + 4608)
        h2t = [sb(f"h2t{s}", [P, T], F32, RW + 5760 + 1152 * s) for s in range(4)]
        sg = [sb(f"sg{s}", [P, T], F32, RW + 10368 + 1152 * s) for s in range(2)]
        act32 = [sb(f"act32_{s}", [P, T], F32, RW + 12672 + 1152 * s) for s in range(2)]
        yT = [sb(f"yT{s}", [P, T], F32, RW + 18176 + 1152 * s) for s in range(2)]
        ystage = [sb(f"ystage{s}", [P, 3, P], F32, RW + 14976 + 1536 * s) for s in range(2)]
        dtmp = sb("dtmp", [P, NS], F32, RW + 18048)
        aT_hi = sb("aT_hi", [P, HF, T], F32R, RM)
        aT_lo = sb("aT_lo", [P, HF, T], F32R, RM + HF * T * 4)

        PB = [ctx.enter_context(nc.psum_tensor(f"PB{i}", [P, 512], F32)) for i in range(2)]
        PK = [ctx.enter_context(nc.psum_tensor(f"PK{i}", [P, 2, 512], F32)) for i in range(2)]
        PM = [ctx.enter_context(nc.psum_tensor(f"PM{i}", [P, 512], F32)) for i in range(2)]
        BANKS = [PB[0][:, :], PB[1][:, :], PK[0][:, 0, :], PK[0][:, 1, :], PK[1][:, 0, :], PK[1][:, 1, :], PM[0][:, :], PM[1][:, :]]

        page_lat = t["cache_kv_latent"][0]
        page_kr = t["cache_k_rope"][0]
        wmod_v = t["w_mod"][0]
        win_v = t["w_in"][0].rearrange("(k p) n -> p k n", p=P)
        wout_v = t["w_out"][0].rearrange("(k p) n -> p k n", p=P)
        gate_v = t["w_gate"][0].rearrange("(k p) n -> p k n", p=P)
        up_v = t["w_up"][0].rearrange("(k p) n -> p k n", p=P)
        down_v = t["w_down"][0].rearrange("(k p) n -> p k n", p=P)

        ZCOL = [m * P for m in range(6)] + [QL + KVL] + [QL + KVL + RP + m * P for m in range(KU)]
        ZW = [P] * 6 + [RP] + [P] * KU
        NZ = len(ZCOL)

        s_const, s_x, s_wkv, s_pt, s_small = (sem(n) for n in ("s_const", "s_x", "s_wkv", "s_pt", "s_small"))
        s_zero = sem("s_zero")
        s_setT = sem("s_setT")
        s_setE = Signal(sem("s_setE"))
        s_cs = sem("s_cs")
        s_wkhi, s_wklo = sem("s_wkhi"), sem("s_wklo")
        s_actc, s_dvec, s_poolc = sem("s_actc"), sem("s_dvec"), sem("s_poolc")
        s_ssx, s_msx, s_sdx, s_diagx, s_bx, s_rxB = (sem(n) for n in ("s_ssx", "s_msx", "s_sdx", "s_diagx", "s_bx", "s_rxB"))
        page_full = [sem(f"page_full{s}") for s in range(4)]
        raw_full = [sem(f"raw_full{s}") for s in range(4)]
        tile_turned = Signal(sem("tile_turned"), 4)
        tile_hi = Signal(sem("tile_hi"))
        tile_lo = Signal(sem("tile_lo"), 2)
        keys_done = Signal(sem("keys_done"), 2)
        sq_done = Signal(sem("sq_done"), 2)
        red_done = Signal(sem("red_done"), 2)
        krs_done = Signal(sem("krs_done"), 4)
        mod_step = Signal(sem("mod_step"), 4)
        modrow_done = Signal(sem("modrow_done"), 1)
        modrow_turned = Signal(sem("modrow_turned"), 1)
        modT_done = Signal(sem("modT_done"), 1)
        s_hT = sem("s_hT")
        w_hi = Signal(sem("w_hi"))
        w_lo = Signal(sem("w_lo"))
        piece_done = Signal(sem("piece_done"))
        piece_out = Signal(sem("piece_out"))
        s_wqb, s_wpool, s_mask = sem("s_wqb"), sem("s_wpool"), sem("s_mask")
        s_rinv0, s_rinv1 = sem("s_rinv0"), sem("s_rinv1")
        s_out = sem("s_out")

        block = ctx.enter_context(nc.Block())

        def settle(eng):
            eng.wait_ge(s_const, 16)

        def bcast(ap, n):
            return ap.unsqueeze(len(ap.shape)).to_broadcast(list(ap.shape) + [n])

        def setup_groups():
            g = [("c", [(k * NV, NV, c_st[:, k * P:(k + 1) * P], P) for k in range(KD)])]
            g.append(("vec", [(0, NG * KD, bmod_st[:, :], P), (NG * KD, NVEC, vec_st[:, :], P)]))
            for k in range(KD):
                g.append((("x", k), [(a, n, x_st[0:n, j, k * P:(k + 1) * P], P) for j, (a, n) in enumerate(TOK)]))
            for m in range(KU // 2):
                g.append((("hist", m), [(j * NB * HIST, NB * HIST, hist_st[:, (2 * m + j) * P:(2 * m + j + 1) * P], P) for j in range(2)]))
            for h in range(H):
                g.append((("wk", h), [(k * P, P, wkv[:, k, h, 0, :], P) for k in range(KL)]))
            return g

        SETUP = setup_groups()
        NSET = len(SETUP)

        N_SMALL = 2 + 5 + 5 + 6
        N_WIN = NG * KD
        N_WOUT = N_WIN + NZ
        N_FFN = N_WOUT + KD

        def raw_use(n, i=0, per=0):
            return ((n // 4) + 1 + i * (per // 4)) * 16

        NP_FF = 2 * HF + 2 * KD

        heads = range(H)
        PE_B = (["cqss"] + [f"tok{j}" for j in range(3)] + [f"q{j}{c}" for j in range(3) for c in range(3)]
                + ["latT0", "latT1", "krT"] + [f"kn{j}" for j in range(3)]
                + [f"{x}{j}{a}" for j in range(3) for x in ("qn", "qr") for a in range(2)]
                + [f"po{m}" for m in range(KU)] + [f"qabs{h}{k}" for h in heads for k in range(KL)]
                + ["up0", "up1", "us0", "us1"])
        ACT_B = (["sqz", "kvss", "kvsd", "rqsd"] + [f"q{j}{c}" for j in range(3) for c in range(3)]
                 + [f"{x}{j}" for j in range(3) for x in ("sqq", "qsd")]
                 + ["krs", "latT0", "latT1", "krT", "kn0", "kn1", "kn2"]
                 + [f"qn{j}{a}" for j in range(3) for a in range(2)] + ["rk_sd"]
                 + [f"poh{m}" for m in range(KU)] + [f"qabs{h}{k}" for h in heads for k in range(KL)])
        DVE_B = (["tok0", "tok1", "tok2", "kvms", "cqss", "cq", "lat"]
                 + [f"{x}{j}" for j in range(3) for x in ("rope", "qms", "qnorm")]
                 + ["kn0", "kn1", "kn2", "rk_ms"] + [f"qr{j}{a}" for j in range(3) for a in range(2)] + ["rinv"]
                 + [f"{x}{m}" for m in range(KU) for x in ("po", "pol")] + ["up0", "up1", "us0", "us1"])
        BY_DVE = {x for x in PE_B if x[:2] in ("cq", "to", "qr", "po", "up", "us")}
        RING_B = {}
        for x in PE_B:
            RING_B[x] = {"cqss": [6], "tok0": [0], "tok1": [1], "tok2": [7], "latT0": [0], "latT1": [1], "krT": [6],
                         "kn0": [2, 3], "kn1": [4, 5], "kn2": [2, 3]}.get(x)
        for n, x in enumerate([x for x in PE_B if RING_B[x] is None]):
            RING_B[x] = [n % 8]
        pe_b, act_b, dve_b = Stages(sem("pe_b"), PE_B), Stages(sem("act_b"), ACT_B), Stages(sem("dve_b"), DVE_B)
        pool_b = Stages(sem("pool_b"), [f"d{g}" for g in range(4)] + ["unew"])
        def piped(steps, last):
            return [(x, s - lag) for s in range(H + last) for x, lag in steps if 0 <= s - lag < H]

        PE_H = piped([("S", 0), ("T", 1), ("D", 2), ("O", 2), ("B", 1), ("V", 3)], 3)
        ACT_H = piped([("exp", 1), ("O", 2), ("hi", 3)], 3)
        DVE_H = piped([("s", 0), ("dg", 1), ("sub", 1), ("rd", 2), ("tmp", 3), ("lo", 3)], 3)
        named = lambda steps: [f"{x}{h}" for x, h in steps]
        pe_h, act_h, dve_h = (Stages(sem(n), named(x)) for n, x in (("pe_h", PE_H), ("act_h", ACT_H), ("dve_h", DVE_H)))
        seq_full = [[sem(f"seq_full{a}{j}") for j in range(4)] for a in range(2)]
        seq_begun = sem("seq_begun")
        pt_turned = Signal(sem("pt_turned"), NPG)
        pt_lat = Signal(sem("pt_lat"), 2)
        pt_kr = Signal(sem("pt_kr"), 2)
        sc_tile = Signal(sem("sc_tile"), 2)
        sq_scaled = Signal(sem("sq_scaled"), 2)
        mx_turned = Signal(sem("mx_turned"))
        mx_diag = Signal(sem("mx_diag"))
        mx_spread = Signal(sem("mx_spread"))
        sub_done = Signal(sem("sub_done"))
        exp_done = Signal(sem("exp_done"))
        sum_done = Signal(sem("sum_done"))
        pv_done = Signal(sem("pv_done"), 2)
        ol_done = Signal(sem("ol_done"), 1)
        s_nk, s_sN, s_vs, s_vhi, s_mixs = (sem(n) for n in ("s_nk", "s_sN", "s_vs", "s_vhi", "s_mixs"))
        x1_sq = Signal(sem("x1_sq"))
        x1_ss = Signal(sem("x1_ss"), 2)
        s_ms2, s_sd2, s_rn2, s_a2 = (sem(n) for n in ("s_ms2", "s_sd2", "s_rn2", "s_a2"))
        h2_t, h2_s, h2_hi, h2_lo = (Signal(sem(n)) for n in ("h2_t", "h2_s", "h2_hi", "h2_lo"))
        ff_silu = Signal(sem("ff_silu"), 2)
        ff_act = Signal(sem("ff_act"), 2)
        ff_split = Signal(sem("ff_split"), 2)
        down_out = Signal(sem("down_out"), 2)
        y_turned = Signal(sem("y_turned"), 2)
        y_out = Signal(sem("y_out"), 2)
        y_stored = [sem(f"y_stored{a}") for a in range(2)]

        def wparts(n, k, w):
            c = n - N_WIN
            view = lambda x: x[:, 0:k * w].rearrange("p (k c) -> p k c", k=k)
            return view(raw[n % 4]), view(conv_hi[c % 2]), view(conv_lo[c % 2])

        @block.sync
        def _(sp):
            sp.dma_start(ident[:, :], t["c_ident"]).then_inc(s_const, 16)
            sp.dma_start(c_st[:, :], t["c_all"]).then_inc(s_small, 16)
            sp.dma_start(bmod_st[:, :], t["b_mod"][0].rearrange("(a p) -> a p", p=P)).then_inc(s_small, 16)
            row = 0
            for name in ("norm1", "norm2", "q_a_norm", "b_pool", "pool_scale"):
                v = t[name][0]
                v = v.rearrange("g c -> (g c)") if len(v.shape) == 2 else v
                v = v.rearrange("(a p) -> a p", p=P)
                sp.dma_start(vec_st[row:row + v.shape[0], :], v).then_inc(s_small, 16)
                row += v.shape[0]
            sp.dma_start(pages_sb[:, :], t["page_table"].rearrange("b n -> (b n)").rearrange("(a n) -> a n", a=1)).then_inc(s_pt, 16)
            sp.dma_start(hist_st[:, :], t["state_pool"][0].rearrange("b n c -> (b n) c")).then_inc(s_small, 16)
            sp.dma_start(cos[:, :, :], t["c_cos"]).then_inc(s_small, 16)
            sp.dma_start(sin[:, :, :], t["c_sin"]).then_inc(s_small, 16)
            sp.dma_start(ratio[:, :, :], t["c_ratio"]).then_inc(s_small, 16)
            sp.dma_start(kvgain[:, :], t["kv_a_norm"][0].partition_broadcast(P)).then_inc(s_small, 16)
            for dst, a, b in ((gqk, "q_norm_nope", "q_norm_rope"), (gk, "k_norm_nope", "k_norm_rope")):
                sp.dma_start(dst[:, 0:NOPE], t[a][0].partition_broadcast(P)).then_inc(s_small, 16)
                for j in range(2):
                    sp.dma_start(dst[:, NOPE + j * HALF:NOPE + (j + 1) * HALF], t[b][0].partition_broadcast(P)).then_inc(s_small, 16)
            for j, (a, n) in enumerate(TOK):
                src = t["x_prompt"][0, a:a + n, :] if j < 2 else t["x_sample"].rearrange("b n d -> (b n) d")
                sp.dma_start(x_st[0:n, j, :], src).then_inc(s_x, 16)
            sp.dma_start(wkv[:, :, :, :, :].rearrange("p k h a d -> p k (h a d)"), t["w_kv_b"][0].rearrange("(k p) n -> p k n", p=P)).then_inc(s_wkv, 16)
            sp.dma_start(o["pool_s"][0, :, 0:HIST - NT, :], t["state_pool"][0, :, NT:HIST, :]).then_inc(s_out, 16)

            def load_page(i, j, base, lat, kr, full):
                settle(sp)
                page = sp.value_load(pages_sb[0:1, ds(base + j, 1)], min_val=0, max_val=NPHYS - 1)
                sp.dma_start(lat, page_lat[ds(page, 1), :, :].rearrange("a p n -> p (a n)")).then_inc(full, 16)
                sp.dma_start(kr, page_kr[ds(page, 1), :, :].rearrange("a p n -> p (a n)")).then_inc(full, 16)

            def ring_page(i, j, base):
                tile_turned.wait(sp, base + j - 3)
                settle(sp)
                krs_done.wait(sp, base + j - 3)
                load_page(i, j, base, pg[j % 4][:, 0:KVL], pg[j % 4][:, KVL:KVL + RP], page_full[j % 4])

            sp.wait_ge(s_pt, 16)
            with sp.Fori(0, NG) as g:
                for k in range(KD):
                    ring_page(g, k, g * KD)
                    mod_step.wait(sp, g * KD + k - 3)
                    settle(sp)
                    sp.dma_start(raw[k % 4][:, :], wmod_v[k * P:(k + 1) * P, ds(g * D, D)]).then_inc(raw_full[k % 4], 16)

            def load_win(m):
                n = N_WIN + m
                if m < 4:
                    mod_step.wait(sp, n - 3)
                else:
                    w_lo.wait(sp, m - 3)
                dst = raw[n % 4][:, 0:KD * ZW[m]].rearrange("p (k c) -> p k c", k=KD)
                sp.dma_start(dst, win_v[:, :, ZCOL[m]:ZCOL[m] + ZW[m]]).then_inc(raw_full[n % 4], 16)

            for m in range(3):
                load_win(m)
            left = (TILES - NG * KD) // 4
            with sp.Fori(0, left) as i:
                for j in range(4):
                    ring_page(i, j, i * 4 + NG * KD)
            for m in range(3, NZ):
                load_win(m)
            w_lo.wait(sp, NZ)
            sp.dma_start(wqb[:, :, :], t["w_q_b"][0].rearrange("(k p) n -> p k n", p=P)).then_inc(s_wqb, 16)
            sp.dma_start(wpool[:, :, :, :].rearrange("p g k n -> p (g k) n"), t["w_pool"][0].rearrange("g (k p) n -> p (g k) n", p=P)).then_inc(s_wpool, 16)
            dve_b.wait(sp, "lat")
            sp.dma_start(o["lat_p"][0, 0].rearrange("(a p) n -> p a n", p=P), lattok[:, 0:2, 0:KVL]).then_inc(s_out, 16)
            sp.dma_start(o["kr_p"][0, 0].rearrange("(a p) n -> p a n", p=P), lattok[:, 0:2, KVL:KVL + RP]).then_inc(s_out, 16)
            sp.dma_start(o["lat_s"][0].rearrange("b n c -> (b n) c"), lattok[0:NS, 2, 0:KVL]).then_inc(s_out, 16)
            sp.dma_start(o["kr_s"][0].rearrange("b n c -> (b n) c"), lattok[0:NS, 2, KVL:KVL + RP]).then_inc(s_out, 16)

            def load_wout(m, i=0):
                n = N_WOUT + m
                col = i * 4 * P + m * P
                sp.dma_start(wparts(n, KD, P)[0], wout_v[:, :, ds(col, P)]).then_inc(raw_full[n % 4], 16)

            pe_b.wait(sp, "q22")
            pe_b.wait(sp, "po7")
            for m in range(4):
                load_wout(m)
            dve_b.wait(sp, "us1")
            pool_b.wait(sp, "unew")
            sp.dma_start(o["pool_p"][0, 0], ustate_p[:, :]).then_inc(s_out, 16)
            sp.dma_start(o["pool_s"][0, :, HIST - NT:HIST, :], ustate[:, :]).then_inc(s_out, 16)
            sp.dma_start(causal[:, :], t["c_causal"]).then_inc(s_mask, 16)
            sp.dma_start(newmask[:, :], t["c_newmask"]).then_inc(s_mask, 16)
            sp.wait_ge(s_out, 16 * 7)

            def load_seq(i, a):
                pv_done.wait(sp, i + a - 1)
                sp.sem_inc(seq_begun, 1)
                for j in range(NPG):
                    pt_turned.wait(sp, (i + a - 1) * NPG + j + 1)
                    load_page(i, j, (i + a) * NPG, lat_pg[a][j][:, :], kr_pg[j][:, :], seq_full[a][j // 4])

            with sp.Fori(0, NB // 2) as i:
                for a in range(2):
                    load_seq(i * 2, a)
            w_lo.wait(sp, NZ + 1)
            with sp.Fori(0, (KD - 4) // 4) as i:
                for j in range(4):
                    w_lo.wait(sp, NZ + i * 4 + j + 1)
                    settle(sp)
                    load_wout(4 + j, i)
            for f in range(2):
                n0 = N_FFN + f * NP_FF
                with sp.Fori(0, HF // 2) as i:
                    for j in range(4):
                        w_lo.wait(sp, i * 4 + (n0 + j - 4 - N_WIN + 1))
                        settle(sp)
                        src = (gate_v, up_v)[j % 2][:, :, ds(i * 2 * P + (f * HF + j // 2) * P, P)]
                        sp.dma_start(wparts(n0 + j, KD, P)[0], src).then_inc(raw_full[(n0 + j) % 4], 16)
                n1 = n0 + 2 * HF

                def load_down(i, j):
                    w_lo.wait(sp, i * 4 + (n1 + j - 4 - N_WIN + 1))
                    settle(sp)
                    r = f * HF + (j % 2) * HD
                    src = down_v[:, r:r + HD, ds(i * 2 * P + (j // 2) * P, P)]
                    sp.dma_start(wparts(n1 + j, HD, P)[0], src).then_inc(raw_full[(n1 + j) % 4], 16)

                def store_y(i, a):
                    y_out.wait(sp, i * 2 + a + 1)
                    settle(sp)
                    col = i * 2 * P + a * P
                    sp.dma_start(o["y_p"][0, :, ds(col, P)].rearrange("(a p) n -> p a n", p=P), ystage[a][:, 0:2, :]).then_inc(y_stored[a], 16)
                    sp.dma_start(o["y_s"].rearrange("b n d -> (b n) d")[:, ds(col, P)], ystage[a][0:NS, 2, :]).then_inc(y_stored[a], 16)

                if f == 0:
                    with sp.Fori(0, KD // 2) as i:
                        for j in range(4):
                            load_down(i, j)
                else:
                    for r in range(2):
                        for j in range(4):
                            load_down(r, j)
                    with sp.Fori(0, KD // 2 - 2) as i:
                        for j in range(4):
                            load_down(i + 2, j)
                            if j % 2:
                                store_y(i, j // 2)
                    for r in range(KD // 2 - 2, KD // 2):
                        for a in range(2):
                            store_y(r, a)
            for a in range(2):
                sp.wait_ge(y_stored[a], KD * 16)
            sp.wait_ge(s_out, 16 * 7)

        @block.gpsimd
        def _(pool):
            ch = Chain(pool, s_poolc)
            pool.memset(ones[:, :], 1.0).then_inc(s_zero, 1)
            pool.memset(cs[:, :, :], 0.0).then_inc(s_zero, 1)
            pool.memset(stat[:, :], 1.0).then_inc(s_zero, 1)
            pool.memset(uext[:, :, 0:HIST], 0.0).then_inc(s_zero, 1)
            pool.memset(rinv[:, TILES:TILES + 3, :], 1.0).then_inc(s_zero, 1)
            pool.memset(krs[:, TILES:TILES + 3], 1.0).then_inc(s_zero, 1)
            modT_done.wait(pool, NG)
            pool.wait_ge(s_rxB, 1)
            s_setE.wait(pool, NSET - 1)
            sc1 = modT[:, 1, :, :]
            ch.link(pool.tensor_scalar(sc1, sc1, 1.0, None, ALU.add))
            ch.link(pool.tensor_tensor(sc1, sc1, bcast(norm1T, NV), ALU.mult))
            for k in range(KD):
                h = h32[k % 2]
                a, b = modT[:, 1, k, :], modT[:, 0, k, :]
                ch.link(pool.tensor_tensor(h[:, :], xT[:, k, :], rxB[:, :], ALU.mult))
                ch.link(pool.tensor_scalar(h[:, 0:S], h[:, 0:S], a[:, 0:1], b[:, 0:1], ALU.mult, ALU.add))
                hs = h[:, S:T].rearrange("p (b n) -> p b n", b=NB)
                ch.link(pool.tensor_tensor(hs, hs, bcast(a[:, 1:NV], NT), ALU.mult))
                ch.link(pool.tensor_tensor(hs, hs, bcast(b[:, 1:NV], NT), ALU.add))
                ch.link(pool.tensor_copy(hT_hi[:, k, :], h[:, :]))
                ins = pool.tensor_tensor(hT_lo[:, k, :], h[:, :], hT_hi[:, k, :].bitcast(F32), ALU.subtract)
                ins.then_inc(s_hT, 1)
            piece_out.wait(pool, NZ)
            for g, w in enumerate(POOL_WINDOWS):
                f = uext[:, 2 * g:2 * g + 2, :]
                s, step, n = f, 1, 0
                while step < w:
                    d = win[n % 2]
                    ch.link(pool.tensor_tensor(d[:, :, 2 * step - 1:EXT], s[:, :, 2 * step - 1:EXT], s[:, :, step - 1:EXT - step], ALU.add))
                    s, step, n = d, 2 * step, n + 1
                if g:
                    pe_b.wait(pool, f"po{2 * g - 1}")
                head = s[:, :, HIST:HIST + w - 1]
                ch.link(pool.tensor_tensor(head, head, ratio[:, g:g + 1, 0:w - 1].to_broadcast([P, 2, w - 1]), ALU.mult))
                ch.link(pool.tensor_scalar(s[:, :, HIST:EXT], s[:, :, HIST:EXT], 1.0 / w, None, ALU.mult))
                ch.link(pool.tensor_tensor(dT[:, :, 0:S], s[:, :, HIST:HIST + S], f[:, :, HIST:HIST + S], ALU.subtract))
                for a in range(2):
                    tail = lambda x: x[:, a, HIST + S:EXT].rearrange("p (b n) -> p b n", b=NB)[:, :, HIST:SEG]
                    ins = pool.tensor_tensor(dT[:, a, S:T].rearrange("p (b n) -> p b n", b=NB), tail(s), tail(f), ALU.subtract)
                    if a == 0:
                        ch.link(ins)
                pool_b.up(ins, f"d{g}")
                pool_b.wait(pool, f"d{g}")
            pool_b.up(pool.tensor_copy(unew[:, :, :].rearrange("p m (b n) -> p m b n", b=NB),
                                       uext[:, :, HIST + S:EXT].rearrange("p m (b n) -> p m b n", b=NB)[:, :, :, HIST:SEG]), "unew")
            sc2 = modT[:, 4, :, :]
            ch.link(pool.tensor_scalar(sc2, sc2, 1.0, None, ALU.add))
            pool.tensor_tensor(sc2, sc2, bcast(norm2T, NV), ALU.mult).then_inc(s_a2, 1)
            pool.wait_ge(s_a2, 1)
            for k in range(KD):
                h2_t.wait(pool, k + 1)
                hs = h2t[k % 4][:, S:T].rearrange("p (b n) -> p b n", b=NB)
                ch.link(pool.tensor_tensor(hs, hs, bcast(modT[:, 4, k, 1:NV], NT), ALU.mult))
                h2_s.up(pool.tensor_tensor(hs, hs, bcast(modT[:, 3, k, 1:NV], NT), ALU.add))
            ff_split.open(pool)
            for f in range(2):
                if f:
                    piece_done.wait(pool, N_FFN + NP_FF - N_WIN)
                with ch.loop(HF // 2, 2) as i:
                    for a in range(2):
                        ff_act.wait(pool, i * 2 + (f * HF + a + 1))
                        settle(pool)
                        ch.link(pool.tensor_copy(aT_hi[:, ds(i * 2 + a, 1), :].rearrange("p a n -> p (a n)"), act32[a][:, :]))
                        ff_split.up(pool.tensor_tensor(aT_lo[:, ds(i * 2 + a, 1), :].rearrange("p a n -> p (a n)"), act32[a][:, :],
                                                       aT_hi[:, ds(i * 2 + a, 1), :].rearrange("p a n -> p (a n)").bitcast(F32), ALU.subtract))

        @block.scalar
        def _(act):
            ch = Chain(act, s_actc)
            krs_done.open(act)
            sq_done.open(act)
            modrow_done.open(act)
            act.wait_ge(s_zero, 2)
            act.wait_ge(s_setT, 1)
            act.activation(cs[:, :, 0:NV], PB[0][:, 0:KD * NV].rearrange("p (k v) -> p k v", k=KD), ACT.Silu).then_inc(s_cs, 1)
            act.wait_ge(s_zero, 3)
            act.wait_ge(s_x, 48)
            for j, (a, n) in enumerate(TOK):
                ins = act.activation(sq_x[0:n, :], x_st[0:n, j, :], ACT.Square, accum_out=stat[0:n, j:j + 1])
                if j < 2:
                    ch.link(ins)
                else:
                    ins.then_inc(s_ssx, 1)
            act.wait_ge(s_msx, 1)
            act.activation(stat[:, 3:6], stat[:, 3:6], ACT.Sqrt).then_inc(s_sdx, 1)
            act.wait_ge(s_wkv, 16)
            act.activation(wk_hi[:, :, :].rearrange("p k (h d) -> p k h d", h=H), wkv[:, :, :, 0, :], ACT.Copy).then_inc(s_wkhi, 1)

            def tile_parts(base, j):
                i = base + j
                tile_turned.wait(act, i + 1)
                keys_done.wait(act, i - 1)
                tile_hi.up(act.activation(latT_hi[j % 2][:, :, :], PB[j % 2][:, 0:KVL].rearrange("p (k n) -> p k n", k=KL), ACT.Copy))
                settle(act)
                krs_done.up(act.activation(kr_junk[j % 4][:, :], pg[j % 4][:, KVL:KVL + RP], ACT.Square, accum_out=krs[:, ds(i, 1)]))

            def tile_squares(base, j):
                i = base + j
                keys_done.wait(act, i + 1)
                red_done.wait(act, i - 1)
                sq_done.up(act.activation(sq[j % 2][:, :].rearrange("p (a n) -> p a n", a=2), PK[j % 2][:, :, :], ACT.Square))

            act.wait_ge(s_diagx, 1)
            tile_parts(0, 0)
            with act.Fori(0, NG) as g:
                for k in range(KD):
                    tile_parts(g * KD, k + 1)
                    if k == KD - 1:
                        mod_step.wait(act, g * KD + KD)
                        modrow_turned.wait(act, g)
                        modrow_done.up(act.activation(modrow[:, :], PM[0][:, :], ACT.Copy))
                    tile_squares(g * KD, k)
            left = (TILES - NG * KD) // 4
            with act.Fori(0, left - 1) as i:
                for j in range(4):
                    tile_parts(i * 4 + NG * KD, j + 1)
                    tile_squares(i * 4 + NG * KD, j)
            for j in range(4):
                if j < 3:
                    tile_parts(TILES - 4, j + 1)
                tile_squares(TILES - 4, j)
            def weight_hi(n, k, w, i=0, r=0):
                src, hi, _ = wparts(n, k, w)
                act.wait_ge(raw_full[n % 4], i * 16 + (n // 4 + 1) * 16)
                piece_done.wait(act, i * 4 + (n - N_WIN - 1))
                w_hi.up(act.activation(hi, src, ACT.Copy))

            act.wait_ge(s_hT, KD)
            krs_done.wait(act, TILES)
            weight_hi(N_WIN, KD, ZW[0])
            for m in range(NZ):
                if m + 1 < NZ:
                    weight_hi(N_WIN + m + 1, KD, ZW[m + 1])
                piece_done.wait(act, m + 1)
                src = PB[m % 2][0:ZW[m], 0:T]
                if m < 7:
                    ins = act.activation(zT[0:ZW[m], m, :], src, ACT.Copy)
                else:
                    ch.link(act.activation(uext[:, m - 7, HIST:HIST + S], src[:, 0:S], ACT.Copy))
                    dst = uext[:, m - 7, HIST + S:EXT].rearrange("p (b n) -> p b n", b=NB)[:, :, HIST:SEG]
                    ins = act.activation(dst, src[:, S:T].rearrange("p (b n) -> p b n", b=NB), ACT.Copy)
                piece_out.up(ins)
            piece_out.wait(act, NZ)
            act_b.up(act.activation(sqz[:, :, :], zT[:, 0:KQ, :], ACT.Square), "sqz")
            dve_b.wait(act, "tok2")
            for j, (a, n) in enumerate(TOK):
                ins = act.activation(kvjunk[0:n, :], kvtok[0:n, j, 0:KVL], ACT.Square, accum_out=stat[0:n, 9 + j:10 + j])
                if j < 2:
                    ch.link(ins)
            act_b.up(ins, "kvss")
            dve_b.wait(act, "kvms")
            act_b.up(act.activation(stat[:, 12:15], stat[:, 12:15], ACT.Sqrt), "kvsd")
            dve_b.wait(act, "cqss")
            act_b.up(act.activation(rqB[:, :], rqB[:, :], ACT.Sqrt), "rqsd")
            qflat = qtok[:, :, :, :].rearrange("p j h d -> p j (h d)")
            for j, (a, n) in enumerate(TOK):
                for c in range(3):
                    pe_b.wait(act, f"q{j}{c}")
                    act_b.up(act.activation(qflat[0:n, j, 512 * c:512 * (c + 1)], BANKS[RING_B[f"q{j}{c}"][0]][0:n, :], ACT.Copy), f"q{j}{c}")
            for j, (a, n) in enumerate(TOK):
                dve_b.wait(act, f"rope{j}")
                act_b.up(act.activation(sqq[0:n, :], qflat[0:n, j, :], ACT.Square), f"sqq{j}")
                dve_b.wait(act, f"qms{j}")
                act_b.up(act.activation(stat[0:n, 16 + 8 * j:24 + 8 * j], stat[0:n, 16 + 8 * j:24 + 8 * j], ACT.Sqrt), f"qsd{j}")
            dve_b.wait(act, "lat")
            for j, (a, n) in enumerate(TOK):
                ins = act.activation(kvjunk[0:n, 0:RP], lattok[0:n, j, KVL:KVL + RP], ACT.Square, accum_out=krs[0:n, TILES + j:TILES + j + 1])
                if j < 2:
                    ch.link(ins)
            act_b.up(ins, "krs")
            for k in range(KL):
                pe_b.wait(act, f"latT{k}")
                act_b.up(act.activation(latTn[:, k, :], BANKS[RING_B[f"latT{k}"][0]][:, 0:T], ACT.Copy), f"latT{k}")
            pe_b.wait(act, "krT")
            act_b.up(act.activation(krTn[:, :], BANKS[RING_B["krT"][0]][0:RP, 0:T], ACT.Copy), "krT")
            dve_b.wait(act, "qnorm2")
            for j, (a, n) in enumerate(TOK):
                pe_b.wait(act, f"kn{j}")
                if j == 2:
                    dve_b.wait(act, "kn0")
                dst = (sqk, sqk2, sqk)[j]
                act_b.up(act.activation(dst[0:n, :].rearrange("p (a n) -> p a n", a=2), PK[j % 2][0:n, :, :], ACT.Square), f"kn{j}")
            for j, (a, n) in enumerate(TOK):
                for e in range(2):
                    pe_b.wait(act, f"qn{j}{e}")
                    src = BANKS[RING_B[f"qn{j}{e}"][0]][:, 0:4 * n].rearrange("p (h n) -> p h n", h=4)
                    act_b.up(act.activation(qnT[:, 4 * e:4 * e + 4, a:a + n], src, ACT.Copy), f"qn{j}{e}")
            dve_b.wait(act, "rk_ms")
            act_b.up(act.activation(rinv[:, :, :], rinv[:, :, :], ACT.Sqrt), "rk_sd")
            for m in range(KU):
                dve_b.wait(act, f"po{m}")
                act_b.up(act.activation(mix_hi[:, KU + m, :], ptmp[m % 2][:, :], ACT.Copy), f"poh{m}")
            for h in heads:
                for k in range(KL):
                    pe_b.wait(act, f"qabs{h}{k}")
                    act_b.up(act.activation(qabs[:, k, h, :], BANKS[RING_B[f"qabs{h}{k}"][0]][:, 0:T], ACT.Copy), f"qabs{h}{k}")
            for x, h in ACT_H:
                if x == "exp":
                    dve_h.wait(act, f"sub{h}")
                    act_h.up(act.activation(stp[h % 2][:, :], stp[h % 2][:, :], ACT.Exp), f"exp{h}")
                elif x == "O":
                    pe_h.wait(act, f"O{h}")
                    if h >= 2:
                        dve_h.wait(act, f"lo{h - 2}")
                    act_h.up(act.activation(olp[h % 2][:, :, :], BANKS[5].rearrange("p (k n) -> p k n", k=KL), ACT.Copy), f"O{h}")
                else:
                    dve_h.wait(act, f"tmp{h}")
                    act_h.up(act.activation(mix_hi[:, h, 0:S], olp[h % 2][:, 0, :], ACT.Copy), f"hi{h}")

            pt_lat.open(act)

            def seq_act(base, a, tail):
                for j in range(NPG):
                    i = (base + a) * NPG + j
                    pt_turned.wait(act, i + 1)
                    sc_tile.wait(act, i - 1)
                    pt_lat.up(act.activation(pT[j % 2][:, 0:2, :], BANKS[j % 2][:, 0:2 * P].rearrange("p (k n) -> p k n", k=2), ACT.Copy))
                    if tail and j == 7:
                        tail_act(base + a - 1, 1 - a)

            def tail_act(b, a):
                sub_done.wait(act, b + 1)
                ch.link(act.activation(st[a][:, :, :], st[a][:, :, :], ACT.Exp))
                exp_done.up(act.activation(pN[a][:, :], pN[a][:, :], ACT.Exp))

            seq_act(0, 0, False)
            with ch.loop(NB // 2 - 1, 2) as i:
                for a in (1, 0):
                    seq_act(i * 2 + (1 - a) * 2, a, True)
            seq_act(NB - 2, 1, True)
            tail_act(NB - 1, 1)
            act.wait_ge(s_vs, 1)
            act.activation(mix_hi[:, 0:H, S:T], BANKS[7][:, 0:H * NS].rearrange("p (h n) -> p h n", h=H), ACT.Copy).then_inc(s_vhi, 1)

            weight_hi(N_WOUT, KD, P)

            with act.Fori(0, KD // 4 - 1) as i:
                for j in range(4):
                    weight_hi(N_WOUT + j + 1, KD, P, i)
                    piece_out.wait(act, i * 4 + (NZ + j + 1))
                    x1_ss.wait(act, i * 4 + (j - 1))
                    settle(act)
                    x1_sq.up(act.activation(tmpC[j % 2][:, :], xT[:, ds(i * 4 + j, 1), :].rearrange("p a n -> p (a n)"), ACT.Square))
            for j in range(4):
                m = KD - 4 + j
                weight_hi(N_WOUT + m + 1, KD, P)
                piece_out.wait(act, NZ + m + 1)
                x1_ss.wait(act, m - 1)
                x1_sq.up(act.activation(tmpC[j % 2][:, :], xT[:, m, :], ACT.Square))
            act.wait_ge(s_ms2, 1)
            act.activation(rn2[:, :], rn2[:, :], ACT.Sqrt).then_inc(s_sd2, 1)
            act.wait_ge(s_a2, 1)
            for k in range(KD):
                h2_t.wait(act, k + 1)
                h = h2t[k % 4]
                ch.link(act.activation(h[:, 0:S], h[:, 0:S], ACT.Identity, scale=modT[:, 4, k, 0:1], bias=modT[:, 3, k, 0:1]))
                h2_s.wait(act, k + 1)
                h2_hi.up(act.activation(hT_hi[:, k, :], h[:, :], ACT.Copy))

            ff_silu.open(act)
            y_out.open(act)

            def silu(f, a, i=0):
                n = N_FFN + f * NP_FF + 2 * a - N_WIN
                piece_done.wait(act, i * 4 + (n + 1))
                ff_act.wait(act, i * 2 + (f * HF + a - 1))
                ff_silu.up(act.activation(sg[a][:, :], PK[0][:, a, 0:T], ACT.Silu))

            def y_rows(a, i=0, r=0):
                y_turned.wait(act, i * 2 + (2 * r + a + 1))
                if r:
                    act.wait_ge(y_stored[a], i * 32 + r * 32)
                ch.link(act.activation(ystage[a][:, 0:2, :], PM[a][:, 0:2 * P].rearrange("p (j n) -> p j n", j=2), ACT.Copy))
                y_out.up(act.activation(ystage[a][0:NS, 2, :], PM[a][0:NS, 2 * P:3 * P], ACT.Copy))

            for f in range(2):
                n0 = N_FFN + f * NP_FF
                n1 = n0 + 2 * HF
                with act.Fori(0, HF // 2 - 1) as i:
                    for j in range(4):
                        weight_hi(n0 + j + 1, KD, P, i)
                        if j % 2 == 0:
                            silu(f, j // 2, i)
                last = HF // 2 - 1
                for j in range(4):
                    n = n0 + 4 * last + j + 1
                    weight_hi(n, HD if n == n1 else KD, P)
                    if j % 2 == 0:
                        silu(f, j // 2, last)
                last = KD // 2 - 1
                if f == 0:
                    with act.Fori(0, last) as i:
                        for j in range(4):
                            weight_hi(n1 + j + 1, HD, P, i)
                    for j in range(4):
                        n = n1 + 4 * last + j + 1
                        weight_hi(n, KD if j == 3 else HD, P)
                else:
                    for j in range(4):
                        weight_hi(n1 + j + 1, HD, P)
                    for j in range(4):
                        weight_hi(n1 + 4 + j + 1, HD, P)
                        if j % 2:
                            y_rows(j // 2)
                    with ch.loop(last - 2, 2) as i:
                        for j in range(4):
                            weight_hi(n1 + 8 + j + 1, HD, P, i)
                            if j % 2:
                                y_rows(j // 2, i, 1)
                    for j in range(4):
                        if j < 3:
                            weight_hi(n1 + 4 * last + j + 1, HD, P)
                        if j % 2:
                            y_rows(j // 2, 0, last - 1)
                    for a in range(2):
                        y_rows(a, 0, last)

        @block.vector
        def _(dve):
            ch = Chain(dve, s_dvec)
            tile_lo.open(dve)
            red_done.open(dve)
            modT_done.open(dve)
            ol_done.open(dve)
            for n, (what, parts) in enumerate(SETUP):
                if n == 0:
                    continue
                dve.wait_ge(s_setT, n + 1)
                src = PB[n % 2]
                if what == "vec":
                    ch.link(dve.tensor_copy(bmodT[:, :], src[:, 0:NG * KD]))
                    ins = dve.tensor_copy(vecT[:, :], src[:, NG * KD:NG * KD + NVEC])
                elif what[0] == "x":
                    ins = dve.tensor_copy(xT[:, what[1], :], src[:, 0:T])
                elif what[0] == "hist":
                    m = 2 * what[1]
                    for j in range(2):
                        dst = uext[:, m + j, HIST + S:EXT].rearrange("p (b n) -> p b n", b=NB)[:, :, 0:HIST]
                        ins = dve.tensor_copy(dst, src[:, j * NB * HIST:(j + 1) * NB * HIST].rearrange("p (b n) -> p b n", b=NB))
                        if j == 0:
                            ch.link(ins)
                else:
                    ins = dve.tensor_copy(wkT[:, what[1], :], src[:, 0:KVL])
                s_setE.up(ins)
                if n == 1 + KD:
                    dve.wait_ge(s_ssx, 1)
                    dve.tensor_scalar(stat[:, 3:6], stat[:, 0:3], 1.0 / D, EPS, ALU.mult, ALU.add).then_inc(s_msx, 1)
            dve.wait_ge(s_sdx, 1)
            ch.link(dve.reciprocal(stat[:, 6:9], stat[:, 3:6]))
            for j in range(3):
                ins = dve.tensor_scalar(diag_x[:, j, :], ident[:, :], stat[:, 6 + j:7 + j], None, ALU.mult)
                if j < 2:
                    ch.link(ins)
                else:
                    ins.then_inc(s_diagx, 1)
            dve.wait_ge(s_wkhi, 1)
            dve.tensor_tensor(wk_lo[:, :, :].rearrange("p k (h d) -> p k h d", h=H), wkv[:, :, :, 0, :],
                              wk_hi[:, :, :].bitcast(F32).rearrange("p k (h d) -> p k h d", h=H), ALU.subtract).then_inc(s_wklo, 1)
            dve.wait_ge(s_bx, 1)
            dve.tensor_copy(rxB[:, :], PM[1][:, 0:T]).then_inc(s_rxB, 1)
            dve.wait_ge(s_small, 16 * N_SMALL)
            ch.link(dve.scalar_tensor_tensor(out=gqk[:, :], in0=gqk[:, :], scalar=SCALE, in1=gk[:, :], op0=ALU.mult, op1=ALU.mult))

            def tile_rest(base, j):
                i = base + j
                tile_hi.wait(dve, i + 1)
                tile_lo.up(dve.tensor_tensor(latT_lo[j % 2][:, :, :], PB[j % 2][:, 0:KVL].rearrange("p (k n) -> p k n", k=KL),
                                             latT_hi[j % 2][:, :, :].bitcast(F32), ALU.subtract))

            def tile_norms(base, j):
                i = base + j
                sq_done.wait(dve, i + 1)
                settle(dve)
                red_done.up(dve.tensor_reduce(rinv[:, ds(i, 1), :].rearrange("p a h -> p (a h)"), sq[j % 2][:, :].rearrange("p (h d) -> p h d", h=H), AX, ALU.add))

            tile_rest(0, 0)
            with dve.Fori(0, NG) as g:
                for k in range(KD):
                    tile_rest(g * KD, k + 1)
                    tile_norms(g * KD, k)
                    if k == KD - 1:
                        modrow_turned.wait(dve, g + 1)
                        for j in range(4):
                            src = PM[1][:, :].rearrange("p (b q) -> p b q", b=4)[:, :, 32 * j:32 * j + NV]
                            bias = bcast(bmodT[:, ds(g * KD + 4 * j, 4)], NV)
                            dst = modT[:, ds(g, 1), 4 * j:4 * j + 4, :].rearrange("p a b v -> p (a b) v")
                            ins = dve.tensor_tensor(dst, src, bias, ALU.add)
                        modT_done.up(ins)
            left = (TILES - NG * KD) // 4
            with dve.Fori(0, left - 1) as i:
                for j in range(4):
                    tile_rest(i * 4 + NG * KD, j + 1)
                    tile_norms(i * 4 + NG * KD, j)
            for j in range(4):
                if j < 3:
                    tile_rest(TILES - 4, j + 1)
                tile_norms(TILES - 4, j)
            def weight_lo(n, k, w, i=0):
                src, hi, lo = wparts(n, k, w)
                w_hi.wait(dve, i * 4 + (n - N_WIN + 1))
                w_lo.up(dve.tensor_tensor(lo, src, hi.bitcast(F32), ALU.subtract))

            for m in range(NZ):
                weight_lo(N_WIN + m, KD, ZW[m])

            def rope(x, j, n, nh, out):
                c = cos[0:n, j:j + 1, :].to_broadcast([n, nh, HALF])
                s = sin[0:n, j:j + 1, :].to_broadcast([n, nh, HALF])
                x1, x2 = x[:, :, 0:HALF], x[:, :, HALF:RP]
                r = [rope_t[q][0:n, 0:nh, :] for q in range(4)]
                for q, (u, v) in enumerate(((x1, c), (x2, s), (x1, s), (x2, c))):
                    ch.link(dve.tensor_tensor(r[q], u, v, ALU.mult))
                ch.link(dve.tensor_tensor(out[:, :, 0:HALF], r[0], r[1], ALU.subtract))
                return dve.tensor_tensor(out[:, :, HALF:RP], r[2], r[3], ALU.add)

            for j, (a, n) in enumerate(TOK):
                pe_b.wait(dve, f"tok{j}")
                dve_b.up(dve.tensor_copy(kvtok[0:n, j, :], BANKS[RING_B[f"tok{j}"][0]][0:n, 0:KVL + RP]), f"tok{j}")
            act_b.wait(dve, "kvss")
            dve_b.up(dve.tensor_scalar(stat[:, 12:15], stat[:, 9:12], 1.0 / KVL, EPS, ALU.mult, ALU.add), "kvms")
            pe_b.wait(dve, "cqss")
            dve_b.up(dve.tensor_scalar(rqB[:, :], BANKS[RING_B["cqss"][0]][:, 0:T], 1.0 / QL, EPS, ALU.mult, ALU.add), "cqss")
            act_b.wait(dve, "rqsd")
            ch.link(dve.reciprocal(rqB[:, :], rqB[:, :]))
            for k in range(KQ):
                ins = dve.scalar_tensor_tensor(out=zT[:, k, :], in0=zT[:, k, :], scalar=qaT[:, k:k + 1], in1=rqB[:, :], op0=ALU.mult, op1=ALU.mult)
            dve_b.up(ins, "cq")
            act_b.wait(dve, "kvsd")
            ch.link(dve.reciprocal(stat[:, 12:15], stat[:, 12:15]))
            for j, (a, n) in enumerate(TOK):
                ch.link(dve.scalar_tensor_tensor(out=lattok[0:n, j, 0:KVL], in0=kvtok[0:n, j, 0:KVL], scalar=stat[0:n, 12 + j:13 + j],
                                                 in1=kvgain[0:n, :], op0=ALU.mult, op1=ALU.mult))
                ins = rope(kvtok[0:n, j:j + 1, KVL:KVL + RP], j, n, 1, lattok[0:n, j:j + 1, KVL:KVL + RP])
                if j < 2:
                    ch.link(ins)
            dve_b.up(ins, "lat")
            dve_b.wait(dve, "lat")
            for j, (a, n) in enumerate(TOK):
                act_b.wait(dve, f"q{j}2")
                x = qtok[0:n, j, :, NOPE:QKH]
                dve_b.up(rope(x, j, n, H, x), f"rope{j}")
                act_b.wait(dve, f"sqq{j}")
                ms = stat[0:n, 16 + 8 * j:24 + 8 * j]
                ch.link(dve.tensor_reduce(ms, sqq[0:n, :].rearrange("p (h d) -> p h d", h=H), AX, ALU.add))
                dve_b.up(dve.tensor_scalar(ms, ms, 1.0 / QKH, EPS, ALU.mult, ALU.add), f"qms{j}")
                act_b.wait(dve, f"qsd{j}")
                ch.link(dve.reciprocal(ms, ms))
                ch.link(dve.tensor_tensor(qtok[0:n, j, :, :], qtok[0:n, j, :, :], bcast(ms, QKH), ALU.mult))
                gains = gqk[0:n, :].unsqueeze(1).to_broadcast([n, H, QKH])
                dve_b.up(dve.tensor_tensor(qtok[0:n, j, :, :], qtok[0:n, j, :, :], gains, ALU.mult), f"qnorm{j}")
            for j, (a, n) in enumerate(TOK):
                act_b.wait(dve, f"kn{j}")
                src = (sqk, sqk2, sqk)[j]
                dve_b.up(dve.tensor_reduce(rinv[0:n, TILES + j, :], src[0:n, :].rearrange("p (h d) -> p h d", h=H), AX, ALU.add), f"kn{j}")
            dve_b.wait(dve, "kn2")
            red_done.wait(dve, TILES)
            krs_done.wait(dve, TILES)
            ch.link(dve.tensor_tensor(rinv[:, :, :], rinv[:, :, :], bcast(krs[:, :], H), ALU.add))
            dve_b.up(dve.tensor_scalar(rinv[:, :, :], rinv[:, :, :], 1.0 / QKH, EPS, ALU.mult, ALU.add), "rk_ms")
            for j, (a, n) in enumerate(TOK):
                for e in range(2):
                    pe_b.wait(dve, f"qr{j}{e}")
                    src = BANKS[RING_B[f"qr{j}{e}"][0]][0:RP, 0:4 * n].rearrange("p (h n) -> p h n", h=4)
                    dve_b.up(dve.tensor_copy(qrT[:, 4 * e:4 * e + 4, a:a + n], src), f"qr{j}{e}")
            act_b.wait(dve, "rk_sd")
            dve_b.up(dve.reciprocal(rinv[:, :, :], rinv[:, :, :]), "rinv")
            for m in range(KU):
                pe_b.wait(dve, f"po{m}")
                if m >= 2:
                    dve_b.wait(dve, f"pol{m - 2}")
                dve_b.up(dve.tensor_scalar(ptmp[m % 2][:, :], BANKS[RING_B[f"po{m}"][0]][:, 0:T], bpoolT[:, m:m + 1], pscaleT[:, m:m + 1], ALU.add, ALU.mult), f"po{m}")
                act_b.wait(dve, f"poh{m}")
                dve_b.up(dve.tensor_tensor(mix_lo[:, KU + m, :], ptmp[m % 2][:, :], mix_hi[:, KU + m, :].bitcast(F32), ALU.subtract), f"pol{m}")
            for x, dst, n in (("up", ustate_p, HIST), ("us", ustate, NS)):
                for j in range(2):
                    pe_b.wait(dve, f"{x}{j}")
                    dve_b.up(dve.tensor_copy(dst[:, 512 * j:512 * (j + 1)], BANKS[RING_B[f"{x}{j}"][0]][0:n, :]), f"{x}{j}")
            dve.wait_ge(s_mask, 32)
            dve_b.wait(dve, "rinv")
            for x, h in DVE_H:
                s = stp[h % 2]
                if x == "s":
                    pe_h.wait(dve, f"S{h}")
                    if h >= 2:
                        pe_h.wait(dve, f"O{h - 2}")
                    ps = BANKS[h % 2]
                    ch.link(dve.scalar_tensor_tensor(out=s[:, 0:S], in0=ps[:, 0:S], scalar=rinv[:, TILES, h:h + 1], in1=causal[:, :], op0=ALU.mult, op1=ALU.add))
                    ch.link(dve.scalar_tensor_tensor(out=s[:, S:S + P], in0=ps[:, S:S + P], scalar=rinv[:, TILES + 1, h:h + 1], in1=causal[:, 0:P], op0=ALU.mult, op1=ALU.add))
                    if h >= 1:
                        pe_h.wait(dve, f"T{h - 1}")
                    dve_h.up(dve.tensor_tensor(mxp[:, 0:P], s[:, P:S], s[:, S:S + P], ALU.max), f"s{h}")
                elif x == "dg":
                    pe_h.wait(dve, f"T{h}")
                    if h >= 1:
                        pe_h.wait(dve, f"B{h - 1}")
                    ch.link(dve.tensor_reduce(stat[:, 40:42], BANKS[2][:, 0:S].rearrange("p (j n) -> p j n", j=2), AX, ALU.max))
                    ch.link(dve.tensor_scalar(dgp[:, 0, :], ident[:, :], stat[:, 40:41], None, ALU.mult))
                    dve_h.up(dve.tensor_scalar(dgp[:, 1, :], ident[:, :], stat[:, 41:42], None, ALU.mult), f"dg{h}")
                elif x == "sub":
                    pe_h.wait(dve, f"B{h}")
                    ch.link(dve.tensor_tensor(s[:, 0:S], s[:, 0:S], BANKS[3][:, 0:S], ALU.subtract))
                    dve_h.up(dve.tensor_tensor(s[:, S:S + P], s[:, S:S + P], BANKS[3][:, P:S], ALU.subtract), f"sub{h}")
                elif x == "rd":
                    pe_h.wait(dve, f"D{h}")
                    dve_h.up(dve.reciprocal(rdps[h % 2][:, :], BANKS[4][:, 0:S]), f"rd{h}")
                elif x == "tmp":
                    pe_h.wait(dve, f"V{h}")
                    dve_h.wait(dve, f"rd{h}")
                    dve_h.up(dve.tensor_tensor(olp[h % 2][:, 0, :], BANKS[6 + h % 2][:, 0:S], rdps[h % 2][:, :], ALU.mult), f"tmp{h}")
                else:
                    act_h.wait(dve, f"hi{h}")
                    dve_h.up(dve.tensor_tensor(mix_lo[:, h, 0:S], olp[h % 2][:, 0, :], mix_hi[:, h, 0:S].bitcast(F32), ALU.subtract), f"lo{h}")
            pt_kr.open(dve)
            sq_scaled.open(dve)
            dve.wait_ge(s_nk, 1)
            nk = BANKS[7][0:NS, 0:H * NS].rearrange("p (h n) -> p h n", h=H)
            ch.link(dve.tensor_tensor(sN[:, :, :], nk, bcast(rinv[0:NS, TILES + 2, :], NS), ALU.mult))
            dve.tensor_tensor(sN[:, :, :], sN[:, :, :], newmask[:, :].unsqueeze(1).to_broadcast([NS, H, NS]), ALU.add).then_inc(s_sN, 1)
            dve.wait_ge(s_sN, 1)

            def tail_dve(b, a, step):
                own = sN[:, :, ds(b * NT, NT)]
                if step == "scale":
                    sc_tile.wait(dve, (b + 1) * NPG)
                    r = bcast(rinv[:, ds(b * NPG, NPG), :].rearrange("p j h -> p (j h)"), NT)
                    ch.link(dve.tensor_tensor(st[a][:, :, :].rearrange("p j (h n) -> p (j h) n", h=H),
                                              BANKS[2 + a].rearrange("p (j n) -> p j n", n=NT), r, ALU.mult))
                    ch.link(dve.tensor_reduce(smx[a][:, :], st[a][:, :, :].rearrange("p j c -> p c j"), AX, ALU.max))
                    m = smx[a][0:NS, :].rearrange("p (h n) -> p h n", h=H)
                    sq_scaled.up(dve.tensor_tensor(m, m, own, ALU.max))
                elif step == "max":
                    mx_turned.wait(dve, b + 1)
                    ch.link(dve.tensor_reduce(stat[0:32, 44 + a:45 + a], BANKS[4][0:32, 0:P], AX, ALU.max))
                    mx_diag.up(dve.tensor_scalar(sdg[a][:, :], ident[0:32, 0:32], stat[0:32, 44 + a:45 + a], None, ALU.mult))
                elif step == "sub":
                    mx_spread.wait(dve, b + 1)
                    m = BANKS[4][:, P:P + 32]
                    ch.link(dve.tensor_tensor(st[a][:, :, :], st[a][:, :, :], m.unsqueeze(1).to_broadcast([P, NPG, 32]), ALU.subtract))
                    sub_done.up(dve.tensor_tensor(pN[a][:, :].rearrange("p (h n) -> p h n", h=H), own, m[0:NS, :].rearrange("p (h n) -> p h n", h=H), ALU.subtract))
                elif step == "sum":
                    exp_done.wait(dve, b + 1)
                    ch.link(dve.tensor_reduce(sdn[a][:, :], st[a][:, :, :].rearrange("p j c -> p c j"), AX, ALU.add))
                    sum_done.up(dve.tensor_tensor(sdn[a][0:NS, :], sdn[a][0:NS, :], pN[a][:, :], ALU.add))
                else:
                    pv_done.wait(dve, b + 1)
                    ch.link(dve.reciprocal(srd[a][:, :], BANKS[4][:, P + 32:P + 64]))
                    for k in range(KL):
                        ins = dve.tensor_tensor(olS[:, k, :, ds(b * NT, NT)], BANKS[4][:, P + 64 + 32 * k:P + 96 + 32 * k].rearrange("p (h n) -> p h n", h=H),
                                                srd[a][:, :].rearrange("p (h n) -> p h n", h=H), ALU.mult)
                    ol_done.up(ins)

            STEPS = {0: "scale", 4: "max", 7: "sub", 10: "sum", 15: "out"}

            def seq_dve(base, a, tail):
                for j in range(NPG):
                    i = (base + a) * NPG + j
                    pt_turned.wait(dve, i + 1)
                    sc_tile.wait(dve, i - 1)
                    pt_kr.up(dve.tensor_copy(pT[j % 2][0:RP, 2, :], BANKS[5 + j % 2][0:RP, 0:P]))
                    if tail and j in STEPS:
                        tail_dve(base + a - 1, 1 - a, STEPS[j])

            seq_dve(0, 0, False)
            with ch.loop(NB // 2 - 1, 12) as i:
                for a in (1, 0):
                    seq_dve(i * 2 + (1 - a) * 2, a, True)
            seq_dve(NB - 2, 1, True)
            for step in STEPS.values():
                tail_dve(NB - 1, 1, step)
            dve.wait_ge(s_vhi, 1)
            dve.tensor_tensor(mix_lo[:, 0:H, S:T], BANKS[7][:, 0:H * NS].rearrange("p (h n) -> p h n", h=H),
                              mix_hi[:, 0:H, S:T].bitcast(F32), ALU.subtract).then_inc(s_mixs, 1)

            def gated(dst, old, ps, g, m, up, by):
                gate = modT[:, g, ds(m, 1), :].rearrange("p a v -> p (a v)")
                seqs = lambda x: x.rearrange("p (b n) -> p b n", b=NB)
                ch.link(dve.tensor_tensor(seqs(dtmp[:, :]), seqs(ps[:, S:T]), bcast(gate[:, 1:NV], NT), ALU.mult))
                ch.link(dve.tensor_tensor(tmpC[2][:, 0:S], ps[:, 0:S], gate[:, 0:1].to_broadcast([P, S]), ALU.mult))
                ch.link(dve.tensor_tensor(dst[:, S:T], old[:, S:T], dtmp[:, :], ALU.add))
                up(dve.tensor_tensor(dst[:, 0:S], old[:, 0:S], tmpC[2][:, 0:S], ALU.add))

            weight_lo(N_WOUT, KD, P)

            def out_tile(j, i):
                piece_done.wait(dve, i * 4 + (NZ + j + 1))
                x = xT[:, ds(i * 4 + j, 1), :].rearrange("p a n -> p (a n)")
                gated(x, x, PB[(NZ + j) % 2], 2, i * 4 + j, piece_out.up, None)

            with ch.loop(KD // 4 - 1, 12) as i:
                for j in range(4):
                    weight_lo(N_WOUT + j + 1, KD, P, i)
                    out_tile(j, i)
            for j in range(4):
                weight_lo(N_WOUT + KD - 4 + j + 1, KD, P)
                out_tile(j, KD // 4 - 1)
            x1_ss.wait(dve, KD)
            dve.tensor_scalar(rn2[:, :], PM[0][:, 0:T], 1.0 / D, EPS, ALU.mult, ALU.add).then_inc(s_ms2, 1)
            dve.wait_ge(s_sd2, 1)
            dve.reciprocal(rn2[:, :], rn2[:, :]).then_inc(s_rn2, 1)
            dve.wait_ge(s_rn2, 1)
            piece_out.wait(dve, NZ + KD)

            def h2_rest(k):
                h2_hi.wait(dve, k + 1)
                h2_lo.up(dve.tensor_tensor(hT_lo[:, k, :], h2t[k % 4][:, :], hT_hi[:, k, :].bitcast(F32), ALU.subtract))

            for k in range(KD):
                if k >= 4:
                    h2_lo.wait(dve, k - 3)
                h2_t.up(dve.tensor_tensor(h2t[k % 4][:, :], xT[:, k, :], rn2[:, :], ALU.mult))
                if k >= 2:
                    h2_rest(k - 2)
            h2_rest(KD - 2)
            h2_rest(KD - 1)

            ff_act.open(dve)
            down_out.open(dve)

            def activate(f, a, i=0):
                n = N_FFN + f * NP_FF + 2 * a + 1 - N_WIN
                piece_done.wait(dve, i * 4 + (n + 1))
                ff_silu.wait(dve, i * 2 + (f * HF + a + 1))
                ff_split.wait(dve, i * 2 + (f * HF + a - 1))
                ff_act.up(dve.tensor_tensor(act32[a][:, :], sg[a][:, :], PK[1][:, a, 0:T], ALU.mult))

            def down_tile(f, a, i):
                n = N_FFN + f * NP_FF + 2 * HF + 2 * a + 1 - N_WIN
                piece_done.wait(dve, i * 4 + (n + 1))
                x = xT[:, ds(i * 2 + a, 1), :].rearrange("p a n -> p (a n)")
                if f:
                    y_turned.wait(dve, i * 2 + (a - 1))
                gated(yT[a] if f else x, x, PB[a], 5, i * 2 + a, down_out.up, None)

            for f in range(2):
                n0 = N_FFN + f * NP_FF
                n1 = n0 + 2 * HF
                with dve.Fori(0, HF // 2 - 1) as i:
                    for j in range(4):
                        weight_lo(n0 + j + 1, KD, P, i)
                        if j % 2:
                            activate(f, j // 2, i)
                last = HF // 2 - 1
                for j in range(4):
                    n = n0 + 4 * last + j + 1
                    weight_lo(n, HD if n == n1 else KD, P)
                    if j % 2:
                        activate(f, j // 2, last)
                last = KD // 2 - 1
                with ch.loop(last, 6) as i:
                    for j in range(4):
                        weight_lo(n1 + j + 1, HD, P, i)
                        if j % 2:
                            down_tile(f, j // 2, i)
                for j in range(4):
                    if f == 0 or j < 3:
                        weight_lo(n1 + 4 * last + j + 1, KD if j == 3 else HD, P)
                    if j % 2:
                        down_tile(f, j // 2, last)

        @block.tensor
        def _(pe):
            tile_turned.open(pe)
            pt_turned.open(pe)
            pv_done.open(pe)
            x1_ss.open(pe)
            keys_done.open(pe)
            mod_step.open(pe)
            modrow_turned.open(pe)
            pe.wait_ge(s_const, 16)
            for n, (what, parts) in enumerate(SETUP):
                if n == 0:
                    pe.wait_ge(s_small, 16 * N_SMALL)
                if what == ("x", 0):
                    pe.wait_ge(s_x, 48)
                if what == ("wk", 0):
                    pe.wait_ge(s_wkv, 16)
                if n == 2:
                    pe.wait_ge(s_cs, 1)
                elif n > 2:
                    s_setE.wait(pe, n - 1 - 1)
                for a, w, src, rows in parts:
                    ins = pe.transpose(PB[n % 2][0:rows, a:a + w], src, ident[0:w, 0:w])
                ins.then_inc(s_setT, 1)
            pe.wait_ge(s_diagx, 1)
            pe.wait_ge(s_zero, 1)
            for j, (a, n) in enumerate(TOK):
                ins = pe.matmul(PM[1][:, a:a + n], ones[0:n, :], diag_x[0:n, j, 0:n], start=True, stop=True)
            ins.then_inc(s_bx, 1)

            def turn(base, j):
                i = base + j
                pe.wait_ge(page_full[j % 4], (base + (j // 4) * 4) * 8 + 32)
                tile_lo.wait(pe, i - 1)
                for k in range(KL):
                    ins = pe.transpose(PB[j % 2][:, k * P:(k + 1) * P], pg[j % 4][:, k * P:(k + 1) * P], ident[:, :])
                tile_turned.up(ins)

            def mod(g, k):
                pe.wait_ge(raw_full[k % 4], (g * KD + (k // 4) * 4) * 4 + 16)
                if k == 0:
                    modrow_done.wait(pe, g)
                for j in range(4):
                    ins = pe.matmul(PM[0][32 * j:32 * j + 32, :], cs[:, k, :], raw[k % 4][:, 512 * j:512 * (j + 1)],
                                    start=(k == 0), stop=(k == KD - 1), tile_position=(0, 32 * j))
                mod_step.up(ins)

            def keys(base, j):
                i = base + j
                tile_lo.wait(pe, i + 1)
                sq_done.wait(pe, i - 1)
                for n, (L, W) in enumerate(((latT_hi, wk_hi), (latT_hi, wk_lo), (latT_lo, wk_hi))):
                    for k in range(KL):
                        for a in range(2):
                            ins = pe.matmul(PK[j % 2][:, a, :], L[j % 2][:, k, :], W[:, k, 512 * a:512 * (a + 1)],
                                            start=(n == 0 and k == 0), stop=(n == 2 and k == KL - 1))
                keys_done.up(ins)

            s_setE.wait(pe, NSET - 1)
            turn(0, 0)
            pe.wait_ge(s_wklo, 1)
            pe.wait_ge(s_cs, 1)
            pe.wait_ge(s_rxB, 1)
            with pe.Fori(0, NG) as g:
                for k in range(KD):
                    turn(g * KD, k + 1)
                    mod(g, k)
                    keys(g * KD, k)
                modrow_done.wait(pe, g + 1)
                modT_done.wait(pe, g)
                for b in range(4):
                    ins = pe.transpose(PM[1][:, b * P:(b + 1) * P], modrow[:, b * P:(b + 1) * P], ident[:, :])
                modrow_turned.up(ins)
            left = (TILES - NG * KD) // 4
            with pe.Fori(0, left - 1) as i:
                for j in range(4):
                    turn(i * 4 + NG * KD, j + 1)
                    keys(i * 4 + NG * KD, j)
            for j in range(4):
                if j < 3:
                    turn(TILES - 4, j + 1)
                keys(TILES - 4, j)
            def passes(out, n, rhs_hi, rhs_lo, k, w, first=True, last=True, ready=None, dyn=None):
                _, hi, lo = wparts(n, k, w)
                for q in range(k):
                    if ready:
                        ready(q)
                    for e, (a, b) in enumerate(((hi, rhs_hi), (hi, rhs_lo), (lo, rhs_hi))):
                        ins = pe.matmul(out, a[:, q, :], b[:, q, :], start=(first and q == 0 and e == 0), stop=(last and q == k - 1 and e == 2))
                piece_done.up(ins)

            pe.wait_ge(s_hT, KD)
            for m in range(NZ):
                w_lo.wait(pe, m + 1)
                piece_out.wait(pe, m - 1)
                passes(PB[m % 2][0:ZW[m], 0:T], N_WIN + m, hT_hi, hT_lo, KD, ZW[m])
            piece_out.wait(pe, NZ)
            sq_done.wait(pe, TILES)
            modT_done.wait(pe, NG)
            last_use = {}

            def banks(name):
                for b in RING_B[name]:
                    if b in last_use:
                        x = last_use[b]
                        (dve_b if x in BY_DVE else act_b).wait(pe, x)
                    last_use[b] = name
                return BANKS[RING_B[name][0]]

            act_b.wait(pe, "sqz")
            out = banks("cqss")
            for k in range(KQ):
                ins = pe.matmul(out[:, 0:T], ones[:, :], sqz[:, k, :], start=(k == 0), stop=(k == KQ - 1))
            pe_b.up(ins, "cqss")
            for j, (a, n) in enumerate(TOK):
                out = banks(f"tok{j}")
                for k in range(KL):
                    pe.transpose(out[0:n, k * P:(k + 1) * P], zT[:, KQ + k, a:a + n], ident[:, :])
                pe_b.up(pe.transpose(out[0:n, KVL:KVL + RP], zT[0:RP, KQ + KL, a:a + n], ident[0:RP, 0:RP]), f"tok{j}")
            dve_b.wait(pe, "cq")
            pe.wait_ge(s_wqb, 16)
            for j, (a, n) in enumerate(TOK):
                for c in range(3):
                    out = banks(f"q{j}{c}")
                    for k in range(KQ):
                        ins = pe.matmul(out[0:n, :], zT[:, k, a:a + n], wqb[:, k, 512 * c:512 * (c + 1)], start=(k == 0), stop=(k == KQ - 1))
                    pe_b.up(ins, f"q{j}{c}")
            dve_b.wait(pe, "lat")
            for x, c0, w in (("latT0", 0, P), ("latT1", P, P), ("krT", KVL, RP)):
                out = banks(x)
                for j, (a, n) in enumerate(TOK):
                    ins = pe.transpose(out[0:w, a:a + n], lattok[0:n, j, c0:c0 + w], ident[0:n, 0:n])
                pe_b.up(ins, x)
            act_b.wait(pe, "latT1")
            for j, (a, n) in enumerate(TOK):
                banks(f"kn{j}")
                for e in range(2):
                    for k in range(KL):
                        ins = pe.matmul(PK[j % 2][0:n, e, :], latTn[:, k, a:a + n], wkv[:, k, 4 * e:4 * e + 4, 0, :], start=(k == 0), stop=(k == KL - 1))
                pe_b.up(ins, f"kn{j}")
            for j, (a, n) in enumerate(TOK):
                dve_b.wait(pe, f"qnorm{j}")
                for x, c0, w in (("qn", 0, NOPE), ("qr", NOPE, RP)):
                    for e in range(2):
                        out = banks(f"{x}{j}{e}")
                        for q in range(4):
                            ins = pe.transpose(out[0:w, q * n:(q + 1) * n], qtok[0:n, j, 4 * e + q, c0:c0 + w], ident[0:n, 0:n])
                        pe_b.up(ins, f"{x}{j}{e}")
            pe.wait_ge(s_wpool, 16)
            for m in range(KU):
                g, e = m // 2, m % 2
                pool_b.wait(pe, f"d{g}")
                out = banks(f"po{m}")
                for k in range(2):
                    ins = pe.matmul(out[:, 0:T], wpool[:, g, k, e * P:(e + 1) * P], dT[:, k, :], start=(k == 0), stop=(k == 1))
                pe_b.up(ins, f"po{m}")
            act_b.wait(pe, "qn21")
            for h in heads:
                for k in range(KL):
                    out = banks(f"qabs{h}{k}")
                    pe_b.up(pe.matmul(out[:, 0:T], wkT[:, h, k * P:(k + 1) * P], qnT[:, h, :], start=True, stop=True), f"qabs{h}{k}")
            for x in ("up", "us"):
                if x == "us":
                    pool_b.wait(pe, "unew")
                for j in range(2):
                    out = banks(f"{x}{j}")
                    for q in range(4):
                        m = 4 * j + q
                        if x == "up":
                            src, n = uext[:, m, S:S + HIST], HIST
                        else:
                            src, n = unew[:, m, :], NS
                        ins = pe.transpose(out[0:n, q * P:(q + 1) * P], src, ident[:, :])
                    pe_b.up(ins, f"{x}{j}")
            act_b.wait(pe, "qabs71")
            dve_b.wait(pe, "us1")
            for x, h in PE_H:
                s = stp[h % 2]
                if x == "S":
                    if h >= 2:
                        dve_h.wait(pe, f"s{h - 2}")
                    for a, c0 in ((0, 0), (1, S)):
                        out = BANKS[h % 2][:, c0:c0 + S - a * P]
                        keys_ = slice(a * P, (a + 1) * P)
                        for k in range(KL):
                            pe.matmul(out, latTn[:, k, keys_], qabs[:, k, h, a * P:S], start=(k == 0), stop=False)
                        ins = pe.matmul(out, krTn[:, keys_], qrT[:, h, a * P:S], start=False, stop=True)
                elif x == "T":
                    dve_h.wait(pe, f"s{h}")
                    if h:
                        dve_h.wait(pe, f"dg{h - 1}")
                    pe.transpose(BANKS[2][:, 0:P], s[:, 0:P], ident[:, :])
                    ins = pe.transpose(BANKS[2][:, P:S], mxp[:, 0:P], ident[:, :])
                elif x == "B":
                    dve_h.wait(pe, f"dg{h}")
                    if h:
                        dve_h.wait(pe, f"sub{h - 1}")
                    ins = pe.matmul(BANKS[3][:, 0:S], ones[:, :], dgp[:, :, :].rearrange("p j n -> p (j n)"), start=True, stop=True)
                elif x == "D":
                    act_h.wait(pe, f"exp{h}")
                    if h:
                        dve_h.wait(pe, f"rd{h - 1}")
                    pe.matmul(BANKS[4][:, 0:P], ones[:, :], s[:, 0:P], start=True, stop=True)
                    pe.matmul(BANKS[4][:, P:S], ones[:, :], s[:, P:S], start=True, stop=False)
                    ins = pe.matmul(BANKS[4][:, P:S], ones[:, :], s[:, S:S + P], start=False, stop=True)
                elif x == "O":
                    if h:
                        act_h.wait(pe, f"O{h - 1}")
                    for k in range(KL):
                        latk, c0 = slice(k * P, (k + 1) * P), k * S
                        pe.matmul(BANKS[5][:, c0:c0 + P], lattok[:, 0, latk], s[:, 0:P], start=True, stop=True)
                        pe.matmul(BANKS[5][:, c0 + P:c0 + S], lattok[:, 0, latk], s[:, P:S], start=True, stop=False)
                        ins = pe.matmul(BANKS[5][:, c0 + P:c0 + S], lattok[:, 1, latk], s[:, S:S + P], start=False, stop=True)
                else:
                    act_h.wait(pe, f"O{h}")
                    if h >= 2:
                        dve_h.wait(pe, f"tmp{h - 2}")
                    for k in range(KL):
                        ins = pe.matmul(BANKS[6 + h % 2][:, 0:S], wkv[:, k, h, 1, :], olp[h % 2][:, k, :], start=(k == 0), stop=(k == KL - 1))
                pe_h.up(ins, f"{x}{h}")
            sc_tile.open(pe)
            dve_h.wait(pe, f"lo{H - 1}")
            for k in range(KL):
                pe.matmul(BANKS[7][0:NS, 0:H * NS], latTn[:, k, S:T], qabs[:, k, :, S:T], start=(k == 0), stop=False)
            pe.matmul(BANKS[7][0:NS, 0:H * NS], krTn[:, S:T], qrT[:, :, S:T], start=False, stop=True).then_inc(s_nk, 1)

            def turn_page(base, a, j):
                i = (base + a) * NPG + j
                if j % 4 == 0:
                    pe.wait_ge(seq_full[a][j // 4], base * 64 + 128)
                pt_lat.wait(pe, i - 1)
                pt_kr.wait(pe, i - 1)
                for k in range(KL):
                    pe.transpose(BANKS[j % 2][:, k * P:(k + 1) * P], lat_pg[a][j][:, k * P:(k + 1) * P], ident[:, :])
                pt_turned.up(pe.transpose(BANKS[5 + j % 2][0:RP, 0:P], kr_pg[j][:, :], ident[:, :]))

            def page_scores(base, a, j):
                i = (base + a) * NPG + j
                pt_lat.wait(pe, i + 1)
                pt_kr.wait(pe, i + 1)
                if j == 0:
                    sq_scaled.wait(pe, base + a - 1)
                out = BANKS[2 + a][:, j * 32:(j + 1) * 32]
                col = (base + a) * NT + S
                for k in range(KL):
                    pe.matmul(out, pT[j % 2][:, k, :], qabs[:, k, :, ds(col, NT)], start=(k == 0), stop=False)
                sc_tile.up(pe.matmul(out, pT[j % 2][0:RP, 2, :], qrT[:, :, ds(col, NT)], start=False, stop=True))

            def tail_pe(b, a, step):
                if step == "T":
                    sq_scaled.wait(pe, b + 1)
                    ol_done.wait(pe, b)
                    mx_turned.up(pe.transpose(BANKS[4][0:32, 0:P], smx[a][:, :], ident[:, :]))
                elif step == "B":
                    mx_diag.wait(pe, b + 1)
                    mx_spread.up(pe.matmul(BANKS[4][:, P:P + 32], ones[0:32, :], sdg[a][:, :], start=True, stop=True))
                else:
                    sum_done.wait(pe, b + 1)
                    pe.matmul(BANKS[4][:, P + 32:P + 64], ones[:, :], sdn[a][:, :], start=True, stop=True)
                    for k in range(KL):
                        out = BANKS[4][:, P + 64 + 32 * k:P + 96 + 32 * k]
                        for j in range(NPG):
                            pe.matmul(out, lat_pg[a][j][:, k * P:(k + 1) * P], st[a][:, j, :], start=(j == 0), stop=False)
                        ins = pe.matmul(out, lattok[0:NS, 2, k * P:(k + 1) * P], pN[a][:, :], start=False, stop=True)
                    pv_done.up(ins)

            def seq_pe(base, a, tail):
                turn_page(base, a, 0)
                for j in range(NPG):
                    if j + 1 < NPG:
                        turn_page(base, a, j + 1)
                    page_scores(base, a, j)
                    if tail and j in (2, 5, 12):
                        tail_pe(base + a - 1, 1 - a, {2: "T", 5: "B", 12: "PV"}[j])

            pe.wait_ge(s_sN, 1)
            seq_pe(0, 0, False)
            with pe.Fori(0, NB // 2 - 1) as i:
                for a in (1, 0):
                    seq_pe(i * 2 + (1 - a) * 2, a, True)
            seq_pe(NB - 2, 1, True)
            for step in ("T", "B", "PV"):
                tail_pe(NB - 1, 1, step)
            ol_done.wait(pe, NB)
            for h in heads:
                for k in range(KL):
                    ins = pe.matmul(BANKS[7][:, NS * h:NS * (h + 1)], wkv[:, k, h, 1, :], olS[:, k, h, :], start=(k == 0), stop=(k == KL - 1))
            ins.then_inc(s_vs, 1)

            pe.wait_ge(s_mixs, 1)

            def ss_x1(j, i, first=False, last=False):
                x1_sq.wait(pe, i * 4 + (j + 1))
                x1_ss.up(pe.matmul(PM[0][:, 0:T], ones[:, :], tmpC[j % 2][:, :], start=first, stop=last, skip_group_check=True))

            def out_piece(j, i):
                w_lo.wait(pe, i * 4 + (NZ + j + 1))
                piece_out.wait(pe, i * 4 + (NZ + j - 1))
                passes(PB[(NZ + j) % 2][:, 0:T], N_WOUT + j, mix_hi, mix_lo, KD, P)

            for j in range(4):
                out_piece(j, 0)
                if j:
                    ss_x1(j - 1, 0, first=(j == 1))
            with pe.Fori(0, KD // 4 - 1) as i:
                for j in range(4):
                    out_piece(j + 4, i)
                    ss_x1(j + 3, i)
            ss_x1(3, KD // 4 - 1, last=True)

            y_turned.open(pe)

            def ff_piece(f, j, i, first=False):
                n = N_FFN + f * NP_FF + j
                w_lo.wait(pe, i * 4 + (n - N_WIN + 1))
                ff_act.wait(pe, i * 2 + (f * HF + j // 2 - 1))
                ready = (lambda q: h2_lo.wait(pe, q + 1)) if first else None
                passes(PK[j % 2][:, j // 2, 0:T], n, hT_hi, hT_lo, KD, P, ready=ready)

            def down_piece(f, j, i):
                n = N_FFN + f * NP_FF + 2 * HF + j
                w_lo.wait(pe, i * 4 + (n - N_WIN + 1))
                if j % 2 == 0:
                    down_out.wait(pe, i * 2 + (f * KD + j // 2 - 1))
                h = j % 2
                passes(PB[j // 2][:, 0:T], n, aT_hi[:, h * HD:(h + 1) * HD, :], aT_lo[:, h * HD:(h + 1) * HD, :], HD, P, first=(h == 0), last=(h == 1))

            def turn_y(a, i):
                down_out.wait(pe, i * 2 + (KD + a + 1))
                y_out.wait(pe, i * 2 + (a - 1))
                for j, (c, n) in enumerate(TOK):
                    ins = pe.transpose(PM[a][0:n, j * P:(j + 1) * P], yT[a][:, c:c + n], ident[:, :])
                y_turned.up(ins)

            for f in range(2):
                if f == 0:
                    for j in range(4):
                        ff_piece(0, j, 0, first=(j == 0))
                    with pe.Fori(0, HF // 2 - 1) as i:
                        for j in range(4):
                            ff_piece(0, j, i + 1)
                else:
                    with pe.Fori(0, HF // 2) as i:
                        for j in range(4):
                            ff_piece(1, j, i)
                ff_split.wait(pe, (f + 1) * HF)
                if f == 0:
                    with pe.Fori(0, KD // 2) as i:
                        for j in range(4):
                            down_piece(0, j, i)
                else:
                    for j in range(4):
                        down_piece(1, j, 0)
                        if j >= 2 and j % 2:
                            turn_y(0, 0)
                    with pe.Fori(0, KD // 2 - 1) as i:
                        for j in range(4):
                            down_piece(1, j, i + 1)
                            if j == 1:
                                turn_y(1, i)
                            if j == 3:
                                turn_y(0, i + 1)
                    turn_y(1, KD // 2 - 1)


_INS = ["x_prompt", "x_sample", "cache_kv_latent", "cache_k_rope", "state_pool", "page_table", "w_mod", "b_mod", "norm1", "w_in",
        "q_a_norm", "w_q_b", "kv_a_norm", "w_kv_b", "q_norm_nope", "q_norm_rope", "k_norm_nope", "k_norm_rope", "w_pool", "b_pool",
        "pool_scale", "w_out", "norm2", "w_gate", "w_up", "w_down"]


def _constants(S, past, NT, NB, RP):
    inv = np.float32(1.0) / (ROPE_THETA ** (np.arange(0, RP, 2) / RP)).astype(np.float32)
    pos = np.zeros((3, P), np.float32)
    pos[0], pos[1] = np.arange(P), np.arange(P, 2 * P)
    pos[2, 0:NB * NT] = past + np.tile(np.arange(NT), NB)
    ang = (pos[:, :, None] * inv).astype(np.float32).transpose(1, 0, 2).astype(np.float64)
    key, query = np.arange(P)[:, None], np.arange(2 * P)[None, :]
    new = np.arange(NB * NT)
    same = (new[:, None] // NT == new[None, :] // NT) & (new[:, None] <= new[None, :])
    ratio = np.ones((4, 16), np.float32)
    for g, w in enumerate(POOL_WINDOWS):
        ratio[g, 0:w - 1] = w / np.arange(1, w)
    return {
        "c_ident": np.eye(P, dtype=np.float32),
        "c_cos": np.ascontiguousarray(np.cos(ang), np.float32),
        "c_sin": np.ascontiguousarray(np.sin(ang), np.float32),
        "c_causal": np.where(key <= query, 0.0, NEG).astype(np.float32),
        "c_newmask": np.where(same, 0.0, NEG).astype(np.float32),
        "c_ratio": np.ascontiguousarray(np.broadcast_to(ratio, (P, 4, 16))),
    }


def kernel(**inputs):
    import concourse.bacc as _bacc
    from concourse.bass_utils import run_bass_kernel_spmd as _run

    a = {n: np.ascontiguousarray(inputs[n]) for n in _INS}
    a["c_all"] = np.concatenate([np.asarray(inputs["c_prompt"]), np.asarray(inputs["c_sample"])], axis=0)
    B, S, D = a["x_prompt"].shape
    NB, NT = a["x_sample"].shape[:2]
    KVL, RP = a["cache_kv_latent"].shape[3], a["cache_k_rope"].shape[3]
    HIST, PW = a["state_pool"].shape[2:]
    past = a["page_table"].shape[1] * a["cache_kv_latent"].shape[2]
    a.update(_constants(S, past, NT, NB, RP))
    outs = {"y_p": (B, S, D), "y_s": (NB, NT, D), "lat_p": (1, B, S, KVL), "kr_p": (1, B, S, RP), "pool_p": (1, B, HIST, PW),
            "lat_s": (1, NB, NT, KVL), "kr_s": (1, NB, NT, RP), "pool_s": (1, NB, HIST, PW)}
    nc = _bacc.Bacc("TRN2", target_bir_lowering=False, num_devices=1)
    t = {n: nc.dram_tensor(f"in_{n}", v.shape, mybir.dt.from_np(v.dtype), kind="ExternalInput").ap() for n, v in a.items()}
    o = {n: nc.dram_tensor(f"out_{n}", s, F32, kind="ExternalOutput").ap() for n, s in outs.items()}
    hybrid_step(nc, t, o)
    r = _run(nc, [{f"in_{n}": v for n, v in a.items()}], core_ids=[0])
    return tuple(r.results[0][f"out_{n}"] for n in outs)
```

```python
from contextlib import ExitStack, contextmanager

import numpy as np

import concourse.bass as bass
from concourse import mybir

P = 128
F32 = mybir.dt.float32
F32R = mybir.dt.float32r
I32 = mybir.dt.int32
ALU = mybir.AluOpType
ACT = mybir.ActivationFunctionType
AX = mybir.AxisListType.X
ds = bass.ds

EPS = 1e-6
ROPE_THETA = 10000.0
POOL_WINDOWS = (2, 4, 8, 16)
NEG = -1e30


class Signal:

    def __init__(self, sem, credit=0):
        self.sem, self.credit = sem, credit

    def open(self, eng):
        if self.credit:
            eng.sem_inc(self.sem, self.credit)

    def up(self, ins):
        return ins.then_inc(self.sem, 1)

    def wait(self, eng, n):
        value = n + self.credit
        if isinstance(value, int) and value <= 0:
            return
        eng.wait_ge(self.sem, value)


class Stages:

    def __init__(self, sem, names):
        self.sem, self.at, self.n = sem, {x: i + 1 for i, x in enumerate(names)}, 0
        assert len(self.at) == len(names)

    def up(self, ins, name):
        self.n += 1
        assert self.at[name] == self.n, (name, self.n, self.at[name])
        return ins.then_inc(self.sem, 1)

    def wait(self, eng, name):
        eng.wait_ge(self.sem, self.at[name])


class Chain:

    def __init__(self, eng, sem):
        self.eng, self.sem, self.n, self.loops = eng, sem, 0, []

    def value(self):
        v = self.n
        for i, per in self.loops:
            v = i * per + v
        return v

    def link(self, ins):
        ins.then_inc(self.sem, 1)
        self.n += 1
        self.eng.wait_ge(self.sem, self.value())

    @contextmanager
    def loop(self, count, per):
        start = self.n
        with self.eng.Fori(0, count) as i:
            self.loops.append((i, per))
            yield i
            self.loops.pop()
        assert self.n - start == per, (self.n - start, per)
        self.n = start + count * per


def hybrid_step(nc, t, o):
    S = t["x_prompt"].shape[1]
    NB, NT = t["x_sample"].shape[:2]
    D = t["x_prompt"].shape[2]
    _, NPHYS, PAGE, KVL = t["cache_kv_latent"].shape
    RP = t["cache_k_rope"].shape[3]
    HALF = RP // 2
    NPG = t["page_table"].shape[1]
    QL = t["q_a_norm"].shape[1]
    NOPE = t["q_norm_nope"].shape[1]
    QKH = NOPE + RP
    H = t["w_q_b"].shape[2] // QKH
    HIST = t["state_pool"].shape[2]
    PW = t["pool_scale"].shape[1]
    FF = t["w_gate"].shape[2]
    SCALE = float(QKH) ** -0.5
    NS = NB * NT
    T = S + NS
    NV = 1 + NB
    KD = D // P
    KQ = QL // P
    KL = KVL // P
    KU = PW // P
    NG = 6
    TILES = NB * NPG
    TOK = [(0, P), (P, P), (S, NS)]
    HF = FF // P // 2
    HD = HF // 2
    EXT = HIST + S + NB * (HIST + NT)
    SEG = HIST + NT
    assert S == 2 * P and PAGE == P and NOPE == P and KL == 2 and KD == 16 and NS == 32 and NPG == 16

    with ExitStack() as ctx:
        sem = lambda name: ctx.enter_context(nc.semaphore(name))

        BASE = (nc.sbuf_base + 63) // 64 * 64
        top = [BASE]

        def region(nbytes):
            at = top[0]
            top[0] += (nbytes + 31) // 32 * 32
            assert top[0] <= nc.sbuf_usable_end, (top[0], nc.sbuf_usable_end)
            return at

        def sb(name, shape, dt, at=None):
            n = int(np.prod(shape[1:])) * 4
            if at is None:
                at = region(n)
            return nc.alloc_sbuf_tensor_at(name, shape, dt, offset=at)

        RX = region(KD * T * 4)
        RH = region(2 * KD * T * 4)
        RM = region(2 * HF * T * 4)
        RRAW = region(4 * KD * P * 4)
        RCONV = region(4 * KD * P * 4)
        RW = region(2 * KL * H * 2 * P * 4 // 2 + H * KVL * 4)
        HT_BYTES = KD * T * 4
        MIX = KU * T * 4

        xT = sb("xT", [P, KD, T], F32, RX)
        hT_hi = sb("hT_hi", [P, KD, T], F32R, RH)
        hT_lo = sb("hT_lo", [P, KD, T], F32R, RH + HT_BYTES)
        raw = [sb(f"raw{s}", [P, KD * P], F32, RRAW + s * KD * P * 4) for s in range(4)]
        conv_hi = [sb(f"conv_hi{s}", [P, KD * P], F32R, RCONV + 2 * s * KD * P * 4) for s in range(2)]
        conv_lo = [sb(f"conv_lo{s}", [P, KD * P], F32R, RCONV + (2 * s + 1) * KD * P * 4) for s in range(2)]
        wkv = sb("wkv", [P, KL, H, 2, P], F32, RW)
        wkT = sb("wkT", [P, H, KVL], F32, RW + KL * H * 2 * P * 4)
        modT = sb("modT", [P, NG, KD, NV], F32)
        rinv = sb("rinv", [P, TILES + 3, H], F32)
        krs = sb("krs", [P, TILES + 3], F32)
        ident = sb("ident", [P, P], F32)
        ones = sb("ones", [P, P], F32)
        cos = sb("cos", [P, 3, HALF], F32)
        sin = sb("sin", [P, 3, HALF], F32)
        ratio = sb("ratio", [P, 4, 16], F32)
        vecT = sb("vecT", [P, 2 * KD + KQ + 2 * KU], F32)
        gqk = sb("gqk", [P, QKH], F32)
        lattok = sb("lattok", [P, 3, KVL + RP], F32)
        stat = sb("stat", [P, 64], F32)
        pages_sb = sb("pages_sb", [1, TILES], I32)
        NVEC = 2 * KD + KQ + 2 * KU
        norm1T, norm2T = vecT[:, 0:KD], vecT[:, KD:2 * KD]
        qaT = vecT[:, 2 * KD:2 * KD + KQ]
        bpoolT = vecT[:, 2 * KD + KQ:2 * KD + KQ + KU]
        pscaleT = vecT[:, 2 * KD + KQ + KU:NVEC]
        wk_hi = sb("wk_hi", [P, KL, H * P], F32R, RM)
        wk_lo = sb("wk_lo", [P, KL, H * P], F32R, RM + 8192)
        sq = [sb(f"sq{s}", [P, H * P], F32, RM + 16384 + 4096 * s) for s in range(2)]
        sq_x = sb("sq_x", [P, D], F32, RM + 16384)
        latT_hi = [sb(f"latT_hi{s}", [P, KL, P], F32R, RM + 24576 + 2048 * s) for s in range(2)]
        latT_lo = [sb(f"latT_lo{s}", [P, KL, P], F32R, RM + 24576 + 2048 * s + 1024) for s in range(2)]
        pg = [sb(f"pg{s}", [P, KVL + RP], F32, RM + 28672 + 1280 * s) for s in range(4)]
        rxB = sb("rxB", [P, T], F32, RM + 33792)
        kvgain = sb("kvgain", [P, KVL], F32, RM + 34944)
        gk = sb("gk", [P, QKH], F32, RM + 35968)
        assert 35968 + QKH * 4 <= 4 * MIX
        hist_st = sb("hist_st", [NB * HIST, PW], F32, RH)
        cs = sb("cs", [P, KD, 32], F32, RH + 4096)
        modrow = sb("modrow", [P, 512], F32, RH + 6144)
        bmod_st = sb("bmod_st", [NG * KD, P], F32, RH + 8192)
        vec_st = sb("vec_st", [NVEC, P], F32, RH + 8704)
        bmodT = sb("bmodT", [P, NG * KD], F32, RH + 9216)
        diag_x = sb("diag_x", [P, 3, P], F32, RH + 9600)
        x_st = sb("x_st", [P, 3, D], F32, RCONV)
        c_st = sb("c_st", [NV, D], F32, RCONV + 3 * D * 4)
        kr_junk = [sb(f"kr_junk{s}", [P, RP], F32, RCONV + 2560 + 256 * s) for s in range(4)]
        h32 = [sb(f"h32_{s}", [P, T], F32, RCONV + 1152 * s) for s in range(2)]
        zT = sb("zT", [P, 7, T], F32, RM)
        sqz = sb("sqz", [P, KQ, T], F32, RM + MIX)
        sqq = sb("sqq", [P, H * QKH], F32, RM + MIX)
        kvtok = sb("kvtok", [P, 3, KVL + RP], F32, RM + 2 * MIX)
        rope_t = [sb(f"rope_t{j}", [P, H, HALF], F32, RM + 2 * MIX + 3840 + 1024 * j) for j in range(4)]
        sqk = sb("sqk", [P, H * P], F32, RM + MIX)
        sqk2 = sb("sqk2", [P, H * P], F32, RM + MIX + 4096)
        rqB = sb("rqB", [P, T], F32, RM + 3 * MIX)
        uext = sb("uext", [P, KU, EXT], F32, RM + 4 * MIX)
        wqb = sb("wqb", [P, KQ, H * QKH], F32, RRAW)
        wpool = sb("wpool", [P, 4, 2, 2 * P], F32, RRAW + 3 * KD * P * 4)
        qtok = sb("qtok", [P, 3, H, QKH], F32, RH)
        qnT = sb("qnT", [P, H, T], F32, RH + 18432)
        win = [sb(f"win{s}", [P, 2, EXT], F32, RH + 27648 + 3392 * s) for s in range(2)]
        dT = [sb(f"dT{g}", [P, 2, T], F32, (RM + 28800 + 2304 * g) if g < 3 else RH + 34432) for g in range(4)]
        unew = sb("unew", [P, KU, NS], F32, RH + 27648)
        ustate = sb("ustate", [NS, PW], F32, RH + 4096)
        ustate_p = sb("ustate_p", [HIST, PW], F32, RH)
        kvjunk = sb("kvjunk", [P, KVL], F32, RM + MIX + 4608)
        ptmp = [sb(f"ptmp{s}", [P, T], F32, RM + 2 * MIX + 3840 + 1152 * s) for s in range(2)]
        qabs = sb("qabs", [P, KL, H, T], F32, RCONV)
        qrT = sb("qrT", [RP, H, T], F32, RCONV + 18432)
        latTn = sb("latTn", [P, KL, T], F32, RCONV + 27648)
        krTn = sb("krTn", [RP, T], F32, RCONV + 27648 + 2304)
        mix_hi = sb("mix_hi", [P, KD, T], F32R, RM)
        mix_lo = sb("mix_lo", [P, KD, T], F32R, RM + 2 * MIX)
        LAT_AT = [RH, RH + NPG * KVL * 4, RRAW + KD * P * 4]
        lat_pg = [[sb(f"lat_pg{a}_{j}", [P, KVL], F32, LAT_AT[a] + j * KVL * 4) for j in range(NPG)] for a in range(3)]
        kr_pg = [sb(f"kr_pg{j}", [P, RP], F32, RH + 2 * NPG * KVL * 4 + j * RP * 4) for j in range(NPG)]
        A0 = RM + 4 * MIX
        causal = sb("causal", [P, 2 * P], F32, A0)
        latq = [sb("latq0", [P, 4, 3, P], F32, RW + KL * H * 2 * P * 4), sb("latq1", [P, 4, 3, P], F32, A0)]
        st = [sb(f"st{s}", [P, NPG, H * NT], F32, (A0 + 6144, A0 + 8192, RW + KL * H * 2 * P * 4 + 6144)[s]) for s in range(3)]
        olS = sb("olS", [P, KL, H, NS], F32, A0 + 10240)
        o_part = sb("o_part", [P, KVL], F32, A0 + 12288)
        mrow = sb("mrow", [1, P], F32, A0 + 13312)
        qseq = [sb(f"qseq{s}", [P, 3, H * NT], F32, RCONV + 31104 + 384 * s) for s in range(3)]
        pN = [sb(f"pN{s}", [H * NT, NS], F32, RCONV + 32256 + 128 * s) for s in range(3)]
        dsel = sb("dsel", [P, 32], F32, RCONV + 32640)
        sel = sb("sel", [P, 32], F32)
        rexpN = sb("rexpN", [NS, H * NT], F32)
        rrowN = sb("rrowN", [H * NT, NS], F32)
        srd = sb("srd", [P, 32], F32)
        gcol = sb("gcol", [P, 2], F32)
        neg1 = sb("neg1", [1, 1], F32)
        newmask = sb("newmask", [H * NT, NT], F32)
        col = lambda first: [stat[:, first + a:first + a + 1] for a in range(3)]
        mNew, mAll, mNeg, dAll, dNew = (col(3 * x) for x in range(5))
        sNew = [stat[0:32, 48 + NT * a:48 + NT * a + NT] for a in range(3)]
        B0 = RW + KL * H * 2 * P * 4
        stp = [sb(f"stp{s}", [P, 3 * P], F32, (B0, B0 + 1536, A0 + 1024)[s]) for s in range(3)]
        olp = [sb(f"olp{s}", [P, KL, 2 * P], F32, B0 + 3072 + 2048 * s) for s in range(2)]
        rdps = [sb("rdp0", [P, 2 * P], F32, B0 + 7168), sb("rdp1", [P, 2 * P], F32, RCONV + 31616)]
        mxp = sb("mxp", [P, P], F32, RCONV + 31104)
        dgp = sb("dgp", [P, 2, P], F32, A0 + 12544)
        assert 12544 + 1024 <= 2 * HF * T * 4 - 4 * MIX
        tmpC = [sb(f"tmpC{s}", [P, T], F32, RW + 1152 * s) for s in range(4)]
        rn2 = sb("rn2", [P, T], F32, RW + 4608)
        h2t = [sb(f"h2t{s}", [P, T], F32, RW + 5760 + 1152 * s) for s in range(4)]
        sg = [sb(f"sg{s}", [P, T], F32, RW + 10368 + 1152 * s) for s in range(2)]
        act32 = [sb(f"act32_{s}", [P, T], F32, RW + 12672 + 1152 * s) for s in range(2)]
        yT = [sb(f"yT{s}", [P, T], F32, RW + 18176 + 1152 * s) for s in range(2)]
        ystage = [sb(f"ystage{s}", [P, 3, P], F32, RW + 14976 + 1536 * s) for s in range(2)]
        dtmp = sb("dtmp", [P, NS], F32, RW + 18048)
        aT_hi = sb("aT_hi", [P, HF, T], F32R, RM)
        aT_lo = sb("aT_lo", [P, HF, T], F32R, RM + HF * T * 4)

        PB = [ctx.enter_context(nc.psum_tensor(f"PB{i}", [P, 512], F32)) for i in range(2)]
        PK = [ctx.enter_context(nc.psum_tensor(f"PK{i}", [P, 2, 512], F32)) for i in range(2)]
        PM = [ctx.enter_context(nc.psum_tensor(f"PM{i}", [P, 512], F32)) for i in range(2)]
        BANKS = [PB[0][:, :], PB[1][:, :], PK[0][:, 0, :], PK[0][:, 1, :], PK[1][:, 0, :], PK[1][:, 1, :], PM[0][:, :], PM[1][:, :]]

        page_lat = t["cache_kv_latent"][0]
        page_kr = t["cache_k_rope"][0]
        wmod_v = t["w_mod"][0]
        win_v = t["w_in"][0].rearrange("(k p) n -> p k n", p=P)
        wout_v = t["w_out"][0].rearrange("(k p) n -> p k n", p=P)
        gate_v = t["w_gate"][0].rearrange("(k p) n -> p k n", p=P)
        up_v = t["w_up"][0].rearrange("(k p) n -> p k n", p=P)
        down_v = t["w_down"][0].rearrange("(k p) n -> p k n", p=P)

        ZCOL = [m * P for m in range(6)] + [QL + KVL] + [QL + KVL + RP + m * P for m in range(KU)]
        ZW = [P] * 6 + [RP] + [P] * KU
        NZ = len(ZCOL)

        s_c = sem("s_c")
        s_const, s_x, s_wkv, s_pt, s_small = (sem(n) for n in ("s_const", "s_x", "s_wkv", "s_pt", "s_small"))
        s_zero = sem("s_zero")
        s_setT = sem("s_setT")
        s_setE = Signal(sem("s_setE"))
        s_cs = sem("s_cs")
        s_wkhi, s_wklo = sem("s_wkhi"), sem("s_wklo")
        s_actc, s_dvec, s_poolc = sem("s_actc"), sem("s_dvec"), sem("s_poolc")
        s_ssx, s_msx, s_sdx, s_diagx, s_bx, s_rxB = (sem(n) for n in ("s_ssx", "s_msx", "s_sdx", "s_diagx", "s_bx", "s_rxB"))
        page_full = [sem(f"page_full{s}") for s in range(4)]
        raw_full = [sem(f"raw_full{s}") for s in range(4)]
        tile_turned = Signal(sem("tile_turned"), 4)
        tile_hi = Signal(sem("tile_hi"))
        tile_lo = Signal(sem("tile_lo"), 2)
        keys_done = Signal(sem("keys_done"), 2)
        sq_done = Signal(sem("sq_done"), 2)
        red_done = Signal(sem("red_done"), 2)
        krs_done = Signal(sem("krs_done"), 4)
        mod_step = Signal(sem("mod_step"), 4)
        modrow_done = Signal(sem("modrow_done"), 1)
        modrow_turned = Signal(sem("modrow_turned"), 1)
        modT_done = Signal(sem("modT_done"), 1)
        s_hT = sem("s_hT")
        w_hi = Signal(sem("w_hi"))
        w_lo = Signal(sem("w_lo"))
        piece_done = Signal(sem("piece_done"))
        piece_out = Signal(sem("piece_out"))
        s_wqb, s_wpool, s_mask = sem("s_wqb"), sem("s_wpool"), sem("s_mask")
        s_rinv0, s_rinv1 = sem("s_rinv0"), sem("s_rinv1")
        s_out = sem("s_out")

        block = ctx.enter_context(nc.Block())

        def settle(eng):
            eng.wait_ge(s_const, 16)

        def bcast(ap, n):
            return ap.unsqueeze(len(ap.shape)).to_broadcast(list(ap.shape) + [n])

        def setup_groups():
            g = [("c", [(k * NV, NV, c_st[:, k * P:(k + 1) * P], P) for k in range(KD)])]
            for k in range(KD):
                g.append((("x", k), [(a, n, x_st[0:n, j, k * P:(k + 1) * P], P) for j, (a, n) in enumerate(TOK)]))
            g.append(("vec", [(0, NG * KD, bmod_st[:, :], P), (NG * KD, NVEC, vec_st[:, :], P)]))
            for m in range(KU // 2):
                g.append((("hist", m), [(j * NB * HIST, NB * HIST, hist_st[:, (2 * m + j) * P:(2 * m + j + 1) * P], P) for j in range(2)]))
            for h in range(H):
                g.append((("wk", h), [(k * P, P, wkv[:, k, h, 0, :], P) for k in range(KL)]))
            return g

        SETUP = setup_groups()
        NSET = len(SETUP)

        N_SMALL = 1 + 5 + 5 + 6
        N_WIN = NG * KD
        N_WOUT = N_WIN + NZ
        N_FFN = N_WOUT + KD

        NP_FF = 2 * HF + 2 * KD

        heads = range(H)
        PE_B = (["cqss"] + [f"tok{j}" for j in range(3)]
                + ["latT0", "latT1", "krT"] + [f"kn{j}" for j in range(3)] + [f"q{j}{c}" for j in range(3) for c in range(3)]
                + [f"po{m}" for m in range(KU)] + [f"{x}{j}{a}" for j in range(3) for x in ("qn", "qr") for a in range(2)] + [f"qabs{h}{k}" for h in heads for k in range(KL)]
                + ["up0", "up1", "us0", "us1"])
        ACT_Q = ["q00", "q01", "q02", "q10", "q11", "sqq0", "qsd0", "q12", "q20", "q21", "sqq1", "qsd1", "q22",
                 "sqq2", "qsd2"] + [f"{x}{m}" for m in range(KU) for x in ("po", "poh")]
        ACT_B = (["rc_sd", "sqz", "kvss", "kvsd", "rqsd", "krs", "latT0", "latT1", "krT", "kn0", "kn1", "kn2", "rk_sd"] + ACT_Q
                 + [f"qn{j}{a}" for j in range(3) for a in range(2)] + [f"qabs{h}0" for h in heads])
        DVE_B = (["rc_ms", "rc0", "rc1", "tok0", "tok1", "tok2", "kvms", "cqss", "cq", "lat", "kn0", "kn1", "kn2", "rk_ms", "rinv"]
                 + [f"{x}{j}" for j in range(3) for x in ("rope", "qms", "qnorm")]
                 + [f"qr{j}{a}" for j in range(3) for a in range(2)]
                 + [f"qabs{h}1" for h in heads] + ["up0", "up1", "us0", "us1"])
        Z_PE = 9
        BY_DVE = {x for x in PE_B if x[:2] in ("cq", "to", "qr", "up", "us") or x in {f"qabs{h}1" for h in heads}}
        RING_B = {}
        for x in PE_B:
            RING_B[x] = {"cqss": [6], "tok0": [2], "tok1": [3], "tok2": [7], "latT0": [0], "latT1": [1], "krT": [6],
                         "kn0": [2, 3], "kn1": [4, 5], "kn2": [2, 3]}.get(x)
        for n, x in enumerate([x for x in PE_B if RING_B[x] is None]):
            RING_B[x] = [n % 8]
        pe_b, act_b, dve_b = Stages(sem("pe_b"), PE_B), Stages(sem("act_b"), ACT_B), Stages(sem("dve_b"), DVE_B)
        pool_b = Stages(sem("pool_b"), [f"d{g}" for g in range(4)] + ["unew"] + [f"pol{m}" for m in range(KU)])
        def piped(steps, last):
            return [(x, s - lag) for s in range(H + last) for x, lag in steps if 0 <= s - lag < H]

        PE_H = piped([("T", 1), ("S", 0), ("B", 1), ("V", 3), ("D", 2), ("O", 2)], 3)
        ACT_H = piped([("exp", 1), ("O", 2), ("hi", 3)], 3)
        DVE_H = piped([("dg", 1), ("s", 0), ("sub", 1), ("rd", 2), ("tmp", 3), ("lo", 3)], 3)
        named = lambda steps: [f"{x}{h}" for x, h in steps]
        pe_h, act_h, dve_h = (Stages(sem(n), named(x)) for n, x in (("pe_h", PE_H), ("act_h", ACT_H), ("dve_h", DVE_H)))
        lat_full = [[sem(f"lat_full{a}{q}") for q in range(4)] for a in range(3)]
        kr_full = [sem(f"kr_full{q}") for q in range(4)]
        kr_last = sem("kr_last")
        NPR = NPG // 2
        pt_turned = Signal(sem("pt_turned"), NPR)
        pt_lat = Signal(sem("pt_lat"), 2)
        pt_kr = Signal(sem("pt_kr"), 2)
        seq_set = Signal(sem("seq_set"))
        sc_quad = Signal(sem("sc_quad"), 2)
        new_done = Signal(sem("new_done"))
        sq_scaled = Signal(sem("sq_scaled"), 1)
        mx_turned = Signal(sem("mx_turned"))
        mx_row = Signal(sem("mx_row"))
        mx_spread = Signal(sem("mx_spread"))
        exp_done = Signal(sem("exp_done"))
        p_turned = Signal(sem("p_turned"))
        p_out = Signal(sem("p_out"))
        pv_done = Signal(sem("pv_done"), 3)
        o_out = Signal(sem("o_out"))
        o_summed = Signal(sem("o_summed"), 1)
        ol_done = Signal(sem("ol_done"), 1)
        assert NB == 8 and (N_WIN + NZ) % 4 == 3

        def sequences(loop, body):
            body(0, 0, 0, False, True)
            with loop((NB - 2) // 3) as i:
                for n in range(1, 4):
                    body(i * 3 + n, n % 3, i + n // 3, True, True)
            body(NB - 1, (NB - 1) % 3, (NB - 1) // 3, True, False)

        s_rrow, s_rexp, s_vs, s_vhi, s_mixs = (sem(n) for n in ("s_rrow", "s_rexp", "s_vs", "s_vhi", "s_mixs"))
        x1_sq = Signal(sem("x1_sq"))
        x1_ss = Signal(sem("x1_ss"), 2)
        s_ms2, s_sd2, s_rn2, s_a2 = (sem(n) for n in ("s_ms2", "s_sd2", "s_rn2", "s_a2"))
        h2_t, h2_s, h2_hi, h2_lo = (Signal(sem(n)) for n in ("h2_t", "h2_s", "h2_hi", "h2_lo"))
        ff_silu = Signal(sem("ff_silu"), 2)
        ff_act = Signal(sem("ff_act"), 2)
        ff_split = Signal(sem("ff_split"), 2)
        down_out = Signal(sem("down_out"), 2)
        y_turned = Signal(sem("y_turned"), 2)
        y_out = Signal(sem("y_out"), 2)
        y_stored = [sem(f"y_stored{a}") for a in range(2)]

        def wparts(n, k, w):
            c = n - N_WIN
            view = lambda x: x[:, 0:k * w].rearrange("p (k c) -> p k c", k=k)
            return view(raw[n % 4]), view(conv_hi[c % 2]), view(conv_lo[c % 2])

        @block.sync
        def _(sp):
            sp.dma_start(ident[:, :], t["c_ident"]).then_inc(s_const, 16)
            sp.dma_start(c_st[:, :], t["c_all"]).then_inc(s_c, 16)
            for j, (a, n) in enumerate(TOK):
                src = t["x_prompt"][0, a:a + n, :] if j < 2 else t["x_sample"].rearrange("b n d -> (b n) d")
                sp.dma_start(x_st[0:n, j, :], src).then_inc(s_x, 16)
            sp.dma_start(wkv[:, :, :, :, :].rearrange("p k h a d -> p k (h a d)"), t["w_kv_b"][0].rearrange("(k p) n -> p k n", p=P)).then_inc(s_wkv, 16)
            sp.dma_start(bmod_st[:, :], t["b_mod"][0].rearrange("(a p) -> a p", p=P)).then_inc(s_small, 16)
            row = 0
            for name in ("norm1", "norm2", "q_a_norm", "b_pool", "pool_scale"):
                v = t[name][0]
                v = v.rearrange("g c -> (g c)") if len(v.shape) == 2 else v
                v = v.rearrange("(a p) -> a p", p=P)
                sp.dma_start(vec_st[row:row + v.shape[0], :], v).then_inc(s_small, 16)
                row += v.shape[0]
            sp.dma_start(pages_sb[:, :], t["page_table"].rearrange("b n -> (b n)").rearrange("(a n) -> a n", a=1)).then_inc(s_pt, 16)
            sp.dma_start(hist_st[:, :], t["state_pool"][0].rearrange("b n c -> (b n) c")).then_inc(s_small, 16)
            sp.dma_start(cos[:, :, :], t["c_cos"]).then_inc(s_small, 16)
            sp.dma_start(sin[:, :, :], t["c_sin"]).then_inc(s_small, 16)
            sp.dma_start(ratio[:, :, :], t["c_ratio"]).then_inc(s_small, 16)
            sp.dma_start(kvgain[:, :], t["kv_a_norm"][0].partition_broadcast(P)).then_inc(s_small, 16)
            for dst, a, b in ((gqk, "q_norm_nope", "q_norm_rope"), (gk, "k_norm_nope", "k_norm_rope")):
                sp.dma_start(dst[:, 0:NOPE], t[a][0].partition_broadcast(P)).then_inc(s_small, 16)
                for j in range(2):
                    sp.dma_start(dst[:, NOPE + j * HALF:NOPE + (j + 1) * HALF], t[b][0].partition_broadcast(P)).then_inc(s_small, 16)
            sp.dma_start(o["pool_s"][0, :, 0:HIST - NT, :], t["state_pool"][0, :, NT:HIST, :]).then_inc(s_out, 16)

            def load_page(i, j, base, lat, kr, full):
                settle(sp)
                page = sp.value_load(pages_sb[0:1, ds(base + j, 1)], min_val=0, max_val=NPHYS - 1)
                sp.dma_start(lat, page_lat[ds(page, 1), :, :].rearrange("a p n -> p (a n)")).then_inc(full, 16)
                sp.dma_start(kr, page_kr[ds(page, 1), :, :].rearrange("a p n -> p (a n)")).then_inc(full, 16)

            def ring_page(i, j, base):
                tile_turned.wait(sp, base + j - 3)
                settle(sp)
                krs_done.wait(sp, base + j - 3)
                load_page(i, j, base, pg[j % 4][:, 0:KVL], pg[j % 4][:, KVL:KVL + RP], page_full[j % 4])

            sp.wait_ge(s_pt, 16)
            with sp.Fori(0, NG) as g:
                for k in range(KD):
                    ring_page(g, k, g * KD)
                    mod_step.wait(sp, g * KD + k - 3)
                    settle(sp)
                    sp.dma_start(raw[k % 4][:, :], wmod_v[k * P:(k + 1) * P, ds(g * D, D)]).then_inc(raw_full[k % 4], 16)

            def load_win(m):
                n = N_WIN + m
                if m < 4:
                    mod_step.wait(sp, n - 3)
                else:
                    w_lo.wait(sp, m - 3)
                dst = raw[n % 4][:, 0:KD * ZW[m]].rearrange("p (k c) -> p k c", k=KD)
                sp.dma_start(dst, win_v[:, :, ZCOL[m]:ZCOL[m] + ZW[m]]).then_inc(raw_full[n % 4], 16)

            for m in range(3):
                load_win(m)
            left = (TILES - NG * KD) // 4
            with sp.Fori(0, left) as i:
                for j in range(4):
                    ring_page(i, j, i * 4 + NG * KD)
            for m in range(3, NZ):
                load_win(m)
            w_lo.wait(sp, NZ - 3)
            sp.dma_start(wpool[:, :, :, :].rearrange("p g k n -> p (g k) n"), t["w_pool"][0].rearrange("g (k p) n -> p (g k) n", p=P)).then_inc(s_wpool, 16)
            wqb_v = t["w_q_b"][0].rearrange("(k p) n -> p k n", p=P)
            for half in range(2):
                w_lo.wait(sp, NZ - 1 + half)
                ks = slice(half * KQ // 2, (half + 1) * KQ // 2)
                sp.dma_start(wqb[:, ks, :], wqb_v[:, ks, :]).then_inc(s_wqb, 16)
            sp.dma_start(newmask[:, :], t["c_newmask"]).then_inc(s_mask, 16)
            dve_b.wait(sp, "lat")
            sp.dma_start(o["lat_p"][0, 0].rearrange("(a p) n -> p a n", p=P), lattok[:, 0:2, 0:KVL]).then_inc(s_out, 16)
            sp.dma_start(o["kr_p"][0, 0].rearrange("(a p) n -> p a n", p=P), lattok[:, 0:2, KVL:KVL + RP]).then_inc(s_out, 16)
            sp.dma_start(o["lat_s"][0].rearrange("b n c -> (b n) c"), lattok[0:NS, 2, 0:KVL]).then_inc(s_out, 16)
            sp.dma_start(o["kr_s"][0].rearrange("b n c -> (b n) c"), lattok[0:NS, 2, KVL:KVL + RP]).then_inc(s_out, 16)

            def load_wout(m, i=0):
                n = N_WOUT + m
                col = i * 4 * P + m * P
                sp.dma_start(wparts(n, KD, P)[0], wout_v[:, :, ds(col, P)]).then_inc(raw_full[n % 4], 16)

            pe_b.wait(sp, "q22")
            pe_b.wait(sp, "po7")
            for m in range(2):
                load_wout(m)
            dve_b.wait(sp, "us1")
            pool_b.wait(sp, "unew")
            sp.dma_start(causal[:, :], t["c_causal"]).then_inc(s_mask, 16)
            sp.dma_start(o["pool_p"][0, 0], ustate_p[:, :]).then_inc(s_out, 16)
            sp.dma_start(o["pool_s"][0, :, HIST - NT:HIST, :], ustate[:, :]).then_inc(s_out, 16)
            sp.wait_ge(s_out, 16 * 7)

            def load_latents(b, a):
                pv_done.wait(sp, b - 2)
                settle(sp)
                for j in range(NPG):
                    page = sp.value_load(pages_sb[0:1, ds(b * NPG + j, 1)], min_val=0, max_val=NPHYS - 1)
                    sp.dma_start(lat_pg[a][j][:, :], page_lat[ds(page, 1), :, :].rearrange("a p n -> p (a n)")).then_inc(lat_full[a][j // 4], 16)

            with sp.Fori(0, NB // 3) as i:
                for a in range(3):
                    load_latents(i * 3 + a, a)
            for b in range(NB // 3 * 3, NB):
                load_latents(b, b % 3)
            pv_done.wait(sp, NB - 2)
            for m in range(2, 4):
                load_wout(m)
            w_lo.wait(sp, NZ + 1)
            with sp.Fori(0, (KD - 4) // 4) as i:
                for j in range(4):
                    w_lo.wait(sp, NZ + i * 4 + j + 1)
                    settle(sp)
                    load_wout(4 + j, i)
            for f in range(2):
                n0 = N_FFN + f * NP_FF
                with sp.Fori(0, HF // 2) as i:
                    for j in range(4):
                        w_lo.wait(sp, i * 4 + (n0 + j - 4 - N_WIN + 1))
                        settle(sp)
                        src = (gate_v, up_v)[j % 2][:, :, ds(i * 2 * P + (f * HF + j // 2) * P, P)]
                        sp.dma_start(wparts(n0 + j, KD, P)[0], src).then_inc(raw_full[(n0 + j) % 4], 16)
                n1 = n0 + 2 * HF

                def load_down(i, j):
                    w_lo.wait(sp, i * 4 + (n1 + j - 4 - N_WIN + 1))
                    settle(sp)
                    r = f * HF + (j % 2) * HD
                    src = down_v[:, r:r + HD, ds(i * 2 * P + (j // 2) * P, P)]
                    sp.dma_start(wparts(n1 + j, HD, P)[0], src).then_inc(raw_full[(n1 + j) % 4], 16)

                def store_y(i, a):
                    y_out.wait(sp, i * 2 + a + 1)
                    settle(sp)
                    col = i * 2 * P + a * P
                    sp.dma_start(o["y_p"][0, :, ds(col, P)].rearrange("(a p) n -> p a n", p=P), ystage[a][:, 0:2, :]).then_inc(y_stored[a], 16)
                    sp.dma_start(o["y_s"].rearrange("b n d -> (b n) d")[:, ds(col, P)], ystage[a][0:NS, 2, :]).then_inc(y_stored[a], 16)

                if f == 0:
                    with sp.Fori(0, KD // 2) as i:
                        for j in range(4):
                            load_down(i, j)
                else:
                    for r in range(2):
                        for j in range(4):
                            load_down(r, j)
                    with sp.Fori(0, KD // 2 - 2) as i:
                        for j in range(4):
                            load_down(i + 2, j)
                            if j % 2:
                                store_y(i, j // 2)
                    for r in range(KD // 2 - 2, KD // 2):
                        for a in range(2):
                            store_y(r, a)
            for a in range(2):
                sp.wait_ge(y_stored[a], KD * 16)
            sp.wait_ge(s_out, 16 * 7)

        @block.gpsimd
        def _(pool):
            ch = Chain(pool, s_poolc)
            ff_split.open(pool)
            pool.memset(ones[:, :], 1.0).then_inc(s_zero, 1)
            pool.memset(neg1[:, :], -1.0)
            pool.memset(cs[:, :, :], 0.0).then_inc(s_zero, 1)
            pool.memset(stat[:, :], 1.0).then_inc(s_zero, 1)
            pool.memset(uext[:, :, 0:HIST], 0.0).then_inc(s_zero, 1)
            pool.memset(rinv[:, TILES:TILES + 3, :], 1.0).then_inc(s_zero, 1)
            pool.memset(krs[:, TILES:TILES + 3], 1.0).then_inc(s_zero, 1)
            modT_done.wait(pool, NG)
            pool.wait_ge(s_rxB, 1)
            s_setE.wait(pool, NSET - 1)
            sc1 = modT[:, 1, :, :]
            ch.link(pool.tensor_scalar(sc1, sc1, 1.0, None, ALU.add))
            ch.link(pool.tensor_tensor(sc1, sc1, bcast(norm1T, NV), ALU.mult))
            for k in range(KD):
                h = h32[k % 2]
                a, b = modT[:, 1, k, :], modT[:, 0, k, :]
                ch.link(pool.tensor_tensor(h[:, :], xT[:, k, :], rxB[:, :], ALU.mult))
                ch.link(pool.tensor_scalar(h[:, 0:S], h[:, 0:S], a[:, 0:1], b[:, 0:1], ALU.mult, ALU.add))
                hs = h[:, S:T].rearrange("p (b n) -> p b n", b=NB)
                ch.link(pool.tensor_tensor(hs, hs, bcast(a[:, 1:NV], NT), ALU.mult))
                ch.link(pool.tensor_tensor(hs, hs, bcast(b[:, 1:NV], NT), ALU.add))
                ch.link(pool.tensor_copy(hT_hi[:, k, :], h[:, :]))
                ins = pool.tensor_tensor(hT_lo[:, k, :], h[:, :], hT_hi[:, k, :].bitcast(F32), ALU.subtract)
                ins.then_inc(s_hT, 1)
            piece_out.wait(pool, NZ)
            for g, w in enumerate(POOL_WINDOWS):
                f = uext[:, 2 * g:2 * g + 2, :]
                s, step, n = f, 1, 0
                while step < w:
                    d = win[n % 2]
                    ch.link(pool.tensor_tensor(d[:, :, 2 * step - 1:EXT], s[:, :, 2 * step - 1:EXT], s[:, :, step - 1:EXT - step], ALU.add))
                    s, step, n = d, 2 * step, n + 1
                head = s[:, :, HIST:HIST + w - 1]
                ch.link(pool.tensor_tensor(head, head, ratio[:, g:g + 1, 0:w - 1].to_broadcast([P, 2, w - 1]), ALU.mult))
                ch.link(pool.tensor_scalar(s[:, :, HIST:EXT], s[:, :, HIST:EXT], 1.0 / w, None, ALU.mult))
                if g == 2:
                    dve_b.wait(pool, "lat")
                ch.link(pool.tensor_tensor(dT[g][:, :, 0:S], s[:, :, HIST:HIST + S], f[:, :, HIST:HIST + S], ALU.subtract))
                for a in range(2):
                    tail = lambda x: x[:, a, HIST + S:EXT].rearrange("p (b n) -> p b n", b=NB)[:, :, HIST:SEG]
                    ins = pool.tensor_tensor(dT[g][:, a, S:T].rearrange("p (b n) -> p b n", b=NB), tail(s), tail(f), ALU.subtract)
                    if a == 0:
                        ch.link(ins)
                pool_b.up(ins, f"d{g}")
                pool_b.wait(pool, f"d{g}")
            pool_b.up(pool.tensor_copy(unew[:, :, :].rearrange("p m (b n) -> p m b n", b=NB),
                                       uext[:, :, HIST + S:EXT].rearrange("p m (b n) -> p m b n", b=NB)[:, :, :, HIST:SEG]), "unew")
            for m in range(KU):
                act_b.wait(pool, f"poh{m}")
                pool_b.up(pool.tensor_tensor(mix_lo[:, KU + m, :], ptmp[m % 2][:, :], mix_hi[:, KU + m, :].bitcast(F32), ALU.subtract), f"pol{m}")
            pool.wait_ge(s_pt, 16)
            pe_b.wait(pool, "po7")
            pool_b.wait(pool, "unew")
            with pool.Fori(0, NB) as b:
                for j in (*range(8), 12, 13):
                    if j % 2 == 0:
                        pt_turned.wait(pool, b * NPR + (j // 2 + 1 - NPR))
                    page = pool.value_load(pages_sb[0:1, ds(b * NPG + j, 1)], min_val=0, max_val=NPHYS - 1)
                    pool.dma_start(kr_pg[j][:, :], page_kr[ds(page, 1), :, :].rearrange("a p n -> p (a n)")).then_inc(kr_full[j // 4], 16)
            sc2 = modT[:, 4, :, :]
            ch.link(pool.tensor_scalar(sc2, sc2, 1.0, None, ALU.add))
            pool.tensor_tensor(sc2, sc2, bcast(norm2T, NV), ALU.mult).then_inc(s_a2, 1)
            pool.wait_ge(s_a2, 1)
            for k in range(KD):
                h2_t.wait(pool, k + 1)
                hs = h2t[k % 4][:, S:T].rearrange("p (b n) -> p b n", b=NB)
                ch.link(pool.tensor_tensor(hs, hs, bcast(modT[:, 4, k, 1:NV], NT), ALU.mult))
                h2_s.up(pool.tensor_tensor(hs, hs, bcast(modT[:, 3, k, 1:NV], NT), ALU.add))
            for f in range(2):
                if f:
                    piece_done.wait(pool, N_FFN + NP_FF - N_WIN)
                with ch.loop(HF // 2, 2) as i:
                    for a in range(2):
                        ff_act.wait(pool, i * 2 + (f * HF + a + 1))
                        settle(pool)
                        ch.link(pool.tensor_copy(aT_hi[:, ds(i * 2 + a, 1), :].rearrange("p a n -> p (a n)"), act32[a][:, :]))
                        ff_split.up(pool.tensor_tensor(aT_lo[:, ds(i * 2 + a, 1), :].rearrange("p a n -> p (a n)"), act32[a][:, :],
                                                       aT_hi[:, ds(i * 2 + a, 1), :].rearrange("p a n -> p (a n)").bitcast(F32), ALU.subtract))

        @block.scalar
        def _(act):
            ch = Chain(act, s_actc)
            krs_done.open(act)
            sq_done.open(act)
            for signal in (modrow_done, pt_lat, ff_silu, y_out):
                signal.open(act)
            act.wait_ge(s_zero, 2)
            act.wait_ge(s_setT, 1)
            act.activation(cs[:, :, 0:NV], PB[0][:, 0:KD * NV].rearrange("p (k v) -> p k v", k=KD), ACT.Silu).then_inc(s_cs, 1)
            act.wait_ge(s_zero, 3)
            act.wait_ge(s_x, 48)
            for j, (a, n) in enumerate(TOK):
                ins = act.activation(sq_x[0:n, :], x_st[0:n, j, :], ACT.Square, accum_out=stat[0:n, j:j + 1])
                if j < 2:
                    ch.link(ins)
                else:
                    ins.then_inc(s_ssx, 1)
            act.wait_ge(s_msx, 1)
            act.activation(stat[:, 3:6], stat[:, 3:6], ACT.Sqrt).then_inc(s_sdx, 1)
            act.wait_ge(s_wkv, 16)
            act.activation(wk_hi[:, :, :].rearrange("p k (h d) -> p k h d", h=H), wkv[:, :, :, 0, :], ACT.Copy).then_inc(s_wkhi, 1)

            def tile_parts(base, j):
                i = base + j
                tile_turned.wait(act, i + 1)
                keys_done.wait(act, i - 1)
                tile_hi.up(act.activation(latT_hi[j % 2][:, :, :], PB[j % 2][:, 0:KVL].rearrange("p (k n) -> p k n", k=KL), ACT.Copy))
                settle(act)
                krs_done.up(act.activation(kr_junk[j % 4][:, :], pg[j % 4][:, KVL:KVL + RP], ACT.Square, accum_out=krs[:, ds(i, 1)]))

            def tile_squares(base, j):
                i = base + j
                keys_done.wait(act, i + 1)
                red_done.wait(act, i - 1)
                sq_done.up(act.activation(sq[j % 2][:, :].rearrange("p (a n) -> p a n", a=2), PK[j % 2][:, :, :], ACT.Square))

            act.wait_ge(s_diagx, 1)
            tile_parts(0, 0)
            with act.Fori(0, NG) as g:
                for k in range(KD):
                    tile_parts(g * KD, k + 1)
                    if k == KD - 1:
                        mod_step.wait(act, g * KD + KD)
                        modrow_turned.wait(act, g)
                        modrow_done.up(act.activation(modrow[:, :], PM[0][:, :], ACT.Copy))
                    tile_squares(g * KD, k)
            left = (TILES - NG * KD) // 4
            with act.Fori(0, left - 1) as i:
                for j in range(4):
                    tile_parts(i * 4 + NG * KD, j + 1)
                    tile_squares(i * 4 + NG * KD, j)
            for j in range(4):
                if j < 3:
                    tile_parts(TILES - 4, j + 1)
                tile_squares(TILES - 4, j)
            def weight_hi(n, k, w, i=0):
                src, hi, _ = wparts(n, k, w)
                act.wait_ge(raw_full[n % 4], i * 16 + (n // 4 + 1) * 16)
                piece_done.wait(act, i * 4 + (n - N_WIN - 1))
                w_hi.up(act.activation(hi, src, ACT.Copy))

            act.wait_ge(s_hT, KD)
            krs_done.wait(act, TILES)
            weight_hi(N_WIN, KD, ZW[0])
            for m in range(NZ):
                if m == 3:
                    dve_b.wait(act, "rc_ms")
                    act_b.up(act.activation(rinv[:, 0:TILES, :], rinv[:, 0:TILES, :], ACT.Sqrt), "rc_sd")
                if m == Z_PE - 1:
                    piece_out.wait(act, 7)
                    act_b.up(act.activation(sqz[:, :, :], zT[:, 0:KQ, :], ACT.Square), "sqz")
                if m + 1 < NZ:
                    weight_hi(N_WIN + m + 1, KD, ZW[m + 1])
                piece_done.wait(act, m + 1)
                src = PB[m % 2][0:ZW[m], 0:T]
                if m < 7:
                    ins = act.activation(zT[0:ZW[m], m, :], src, ACT.Copy)
                else:
                    ch.link(act.activation(uext[:, m - 7, HIST:HIST + S], src[:, 0:S], ACT.Copy))
                    dst = uext[:, m - 7, HIST + S:EXT].rearrange("p (b n) -> p b n", b=NB)[:, :, HIST:SEG]
                    ins = act.activation(dst, src[:, S:T].rearrange("p (b n) -> p b n", b=NB), ACT.Copy)
                piece_out.up(ins)
                if m == Z_PE + 1:
                    dve_b.wait(act, "tok2")
                    for j, (a, n) in enumerate(TOK):
                        ins = act.activation(kvjunk[0:n, :], kvtok[0:n, j, 0:KVL], ACT.Square, accum_out=stat[0:n, 9 + j:10 + j])
                        if j < 2:
                            ch.link(ins)
                    act_b.up(ins, "kvss")
                if m == Z_PE + 2:
                    dve_b.wait(act, "kvms")
                    act_b.up(act.activation(stat[:, 12:15], stat[:, 12:15], ACT.Sqrt), "kvsd")
                    dve_b.wait(act, "cqss")
                    act_b.up(act.activation(rqB[:, :], rqB[:, :], ACT.Sqrt), "rqsd")
            dve_b.wait(act, "lat")
            for j, (a, n) in enumerate(TOK):
                ins = act.activation(kvjunk[0:n, 0:RP], lattok[0:n, j, KVL:KVL + RP], ACT.Square, accum_out=krs[0:n, TILES + j:TILES + j + 1])
                if j < 2:
                    ch.link(ins)
            act_b.up(ins, "krs")
            for k in range(KL):
                pe_b.wait(act, f"latT{k}")
                act_b.up(act.activation(latTn[:, k, :], BANKS[RING_B[f"latT{k}"][0]][:, 0:T], ACT.Copy), f"latT{k}")
            pe_b.wait(act, "krT")
            act_b.up(act.activation(krTn[:, :], BANKS[RING_B["krT"][0]][0:RP, 0:T], ACT.Copy), "krT")
            act_b.wait(act, "krs")
            pe_b.wait(act, "cqss")
            for j, (a, n) in enumerate(TOK):
                pe_b.wait(act, f"kn{j}")
                if j == 2:
                    dve_b.wait(act, "kn0")
                dst = (sqk, sqk2, sqk)[j]
                act_b.up(act.activation(dst[0:n, :].rearrange("p (a n) -> p a n", a=2), PK[j % 2][0:n, :, :], ACT.Square), f"kn{j}")
            dve_b.wait(act, "rk_ms")
            act_b.up(act.activation(rinv[:, TILES:TILES + 3, :], rinv[:, TILES:TILES + 3, :], ACT.Sqrt), "rk_sd")
            qflat = qtok[:, :, :, :].rearrange("p j h d -> p j (h d)")
            for x in ACT_Q:
                if x[:2] == "po":
                    m = int(x[-1])
                    if x[:3] == "poh":
                        act_b.wait(act, f"po{m}")
                        ins = act.activation(mix_hi[:, KU + m, :], ptmp[m % 2][:, :], ACT.Copy)
                    else:
                        pe_b.wait(act, x)
                        if m >= 2:
                            pool_b.wait(act, f"pol{m - 2}")
                        ins = act.activation(ptmp[m % 2][:, :], BANKS[RING_B[x][0]][:, 0:T], ACT.Identity, scale=pscaleT[:, m:m + 1], bias=bpoolT[:, m:m + 1])
                    act_b.up(ins, x)
                    continue
                j = int(x[1] if x[1].isdigit() else x[3])
                n = TOK[j][1]
                ms = stat[0:n, 16 + 8 * j:24 + 8 * j]
                if x[1].isdigit():
                    c = int(x[2])
                    pe_b.wait(act, x)
                    ins = act.activation(qflat[0:n, j, 512 * c:512 * (c + 1)], BANKS[RING_B[x][0]][0:n, :], ACT.Copy)
                elif x[0] == "s":
                    dve_b.wait(act, f"rope{j}")
                    ins = act.activation(sqq[0:n, :], qflat[0:n, j, :], ACT.Square)
                else:
                    dve_b.wait(act, f"qms{j}")
                    ins = act.activation(ms, ms, ACT.Sqrt)
                act_b.up(ins, x)
            for j, (a, n) in enumerate(TOK):
                for e in range(2):
                    pe_b.wait(act, f"qn{j}{e}")
                    src = BANKS[RING_B[f"qn{j}{e}"][0]][:, 0:4 * n].rearrange("p (h n) -> p h n", h=4)
                    act_b.up(act.activation(qnT[:, 4 * e:4 * e + 4, a:a + n], src, ACT.Identity, scale=gcol[:, 0:1]), f"qn{j}{e}")
            for h in heads:
                pe_b.wait(act, f"qabs{h}0")
                act_b.up(act.activation(qabs[:, 0, h, :], BANKS[RING_B[f"qabs{h}0"][0]][:, 0:T], ACT.Copy), f"qabs{h}0")
            def load_rotary(b, j, full):
                page = act.value_load(pages_sb[0:1, ds(b * NPG + j, 1)], min_val=0, max_val=NPHYS - 1)
                act.dma_start(kr_pg[j][:, :], page_kr[ds(page, 1), :, :].rearrange("a p n -> p (a n)")).then_inc(full, 16)

            act.wait_ge(s_pt, 16)
            pe_b.wait(act, "po7")
            for x, h in ACT_H:
                if x == "exp":
                    dve_h.wait(act, f"sub{h}")
                    act_h.up(act.activation(stp[h % 3][:, :], stp[h % 3][:, :], ACT.Exp), f"exp{h}")
                elif x == "O":
                    pe_h.wait(act, f"O{h}")
                    if h >= 2:
                        dve_h.wait(act, f"lo{h - 2}")
                    act_h.up(act.activation(olp[h % 2][:, :, :], BANKS[5].rearrange("p (k n) -> p k n", k=KL), ACT.Copy), f"O{h}")
                else:
                    dve_h.wait(act, f"tmp{h}")
                    act_h.up(act.activation(mix_hi[:, h, 0:S], olp[h % 2][:, 0, :], ACT.Copy), f"hi{h}")
                if x == "exp" and h in (1, 2, 3, 4, 5, 6):
                    j = (8, 9, 10, 11, 14, 15)[h - 1]
                    load_rotary(0, j, kr_full[2] if j < 12 else kr_last)


            def seq_act(b, a, r, tail, more):
                for p in range(NPR):
                    pt_turned.wait(act, b * NPR + (p + 1))
                    sc_quad.wait(act, b * 4 + (p // 2 - 1))
                    dst = latq[p // 2 % 2][:, 2 * (p % 2):2 * (p % 2) + 2, 0:2, :]
                    pt_lat.up(act.activation(dst, BANKS[p % 2].rearrange("p (e k n) -> p e k n", e=2, k=2), ACT.Copy))
                    if tail and p == 3:
                        exp_act(b - 1, (a - 1) % 3)
                    if more and p in (5, 6):
                        for j in (2 * p - 2, 2 * p - 1):
                            load_rotary(b + 1, j, kr_full[2])
                    if tail and p == 7:
                        weighted_act(b - 1)
                    if more and p == 7:
                        for j in (14, 15):
                            load_rotary(b + 1, j, kr_last)

            def exp_act(b, a):
                mx_spread.wait(act, b + 1)
                ch.link(act.activation(mNeg[a], BANKS[4][:, P:P + 1], ACT.Copy))
                act.activation(st[a][:, :, :], st[a][:, :, :], ACT.Exp, bias=mNeg[a], accum_out=dAll[a])
                settle(act)
                exp_done.up(act.activation(pN[a][:, ds(b * NT, NT)], sNew[a], ACT.Exp, bias=mNeg[a][0:32, :], accum_out=dNew[a][0:32, :]))

            def weighted_act(b):
                pv_done.wait(act, b + 1)
                o_summed.wait(act, b)
                o_out.up(act.activation(o_part[:, :], BANKS[4][:, KVL:2 * KVL], ACT.Copy))

            sequences(lambda n: ch.loop(n, 3), seq_act)
            exp_act(NB - 1, (NB - 1) % 3)
            weighted_act(NB - 1)
            act.wait_ge(s_vs, 1)
            act.activation(mix_hi[:, 0:H, S:T], BANKS[7][:, 0:H * NS].rearrange("p (h n) -> p h n", h=H), ACT.Copy).then_inc(s_vhi, 1)

            weight_hi(N_WOUT, KD, P)

            with act.Fori(0, KD // 4 - 1) as i:
                for j in range(4):
                    weight_hi(N_WOUT + j + 1, KD, P, i)
                    piece_out.wait(act, i * 4 + (NZ + j + 1))
                    x1_ss.wait(act, i * 4 + (j - 1))
                    settle(act)
                    x1_sq.up(act.activation(tmpC[j % 2][:, :], xT[:, ds(i * 4 + j, 1), :].rearrange("p a n -> p (a n)"), ACT.Square))
            for j in range(4):
                m = KD - 4 + j
                weight_hi(N_WOUT + m + 1, KD, P)
                piece_out.wait(act, NZ + m + 1)
                x1_ss.wait(act, m - 1)
                x1_sq.up(act.activation(tmpC[j % 2][:, :], xT[:, m, :], ACT.Square))
            act.wait_ge(s_ms2, 1)
            act.activation(rn2[:, :], rn2[:, :], ACT.Sqrt).then_inc(s_sd2, 1)
            weight_hi(N_FFN + 1, KD, P)
            act.wait_ge(s_a2, 1)
            for k in range(KD):
                h2_t.wait(act, k + 1)
                h = h2t[k % 4]
                ch.link(act.activation(h[:, 0:S], h[:, 0:S], ACT.Identity, scale=modT[:, 4, k, 0:1], bias=modT[:, 3, k, 0:1]))
                h2_s.wait(act, k + 1)
                h2_hi.up(act.activation(hT_hi[:, k, :], h[:, :], ACT.Copy))


            def silu(f, a, i=0):
                n = N_FFN + f * NP_FF + 2 * a - N_WIN
                piece_done.wait(act, i * 4 + (n + 1))
                ff_act.wait(act, i * 2 + (f * HF + a - 1))
                ff_silu.up(act.activation(sg[a][:, :], PK[0][:, a, 0:T], ACT.Silu))

            def y_rows(a, i=0, r=0):
                y_turned.wait(act, i * 2 + (2 * r + a + 1))
                if r:
                    act.wait_ge(y_stored[a], i * 32 + r * 32)
                ch.link(act.activation(ystage[a][:, 0:2, :], PM[a][:, 0:2 * P].rearrange("p (j n) -> p j n", j=2), ACT.Copy))
                y_out.up(act.activation(ystage[a][0:NS, 2, :], PM[a][0:NS, 2 * P:3 * P], ACT.Copy))

            for f in range(2):
                n0 = N_FFN + f * NP_FF
                n1 = n0 + 2 * HF
                for j in range(4):
                    if f or j:
                        weight_hi(n0 + j + 1, KD, P)
                    if j % 2 == 0:
                        silu(f, j // 2)
                with act.Fori(0, HF // 2 - 2) as i:
                    for j in range(4):
                        weight_hi(n0 + 4 + j + 1, KD, P, i)
                        if j % 2 == 0:
                            silu(f, j // 2, i + 1)
                last = HF // 2 - 1
                for j in range(4):
                    n = n0 + 4 * last + j + 1
                    weight_hi(n, HD if n == n1 else KD, P)
                    if j % 2 == 0:
                        silu(f, j // 2, last)
                last = KD // 2 - 1
                if f == 0:
                    with act.Fori(0, last) as i:
                        for j in range(4):
                            weight_hi(n1 + j + 1, HD, P, i)
                    for j in range(4):
                        n = n1 + 4 * last + j + 1
                        weight_hi(n, KD if j == 3 else HD, P)
                else:
                    for j in range(4):
                        weight_hi(n1 + j + 1, HD, P)
                    for j in range(4):
                        weight_hi(n1 + 4 + j + 1, HD, P)
                        if j % 2:
                            y_rows(j // 2)
                    with ch.loop(last - 2, 2) as i:
                        for j in range(4):
                            weight_hi(n1 + 8 + j + 1, HD, P, i)
                            if j % 2:
                                y_rows(j // 2, i, 1)
                    for j in range(4):
                        if j < 3:
                            weight_hi(n1 + 4 * last + j + 1, HD, P)
                        if j % 2:
                            y_rows(j // 2, 0, last - 1)
                    for a in range(2):
                        y_rows(a, 0, last)

        @block.vector
        def _(dve):
            ch = Chain(dve, s_dvec)
            tile_lo.open(dve)
            red_done.open(dve)
            modT_done.open(dve)
            for signal in (ol_done, pt_kr, sq_scaled, ff_act, down_out):
                signal.open(dve)
            for n, (what, parts) in enumerate(SETUP):
                if n == 0:
                    continue
                dve.wait_ge(s_setT, n + 1)
                src = PB[n % 2]
                if what == "vec":
                    ch.link(dve.tensor_copy(bmodT[:, :], src[:, 0:NG * KD]))
                    ch.link(dve.tensor_copy(vecT[:, :], src[:, NG * KD:NG * KD + NVEC]))
                    ins = dve.tensor_tensor(bpoolT, bpoolT, pscaleT, ALU.mult)
                elif what[0] == "x":
                    ins = dve.tensor_copy(xT[:, what[1], :], src[:, 0:T])
                elif what[0] == "hist":
                    m = 2 * what[1]
                    for j in range(2):
                        dst = uext[:, m + j, HIST + S:EXT].rearrange("p (b n) -> p b n", b=NB)[:, :, 0:HIST]
                        ins = dve.tensor_copy(dst, src[:, j * NB * HIST:(j + 1) * NB * HIST].rearrange("p (b n) -> p b n", b=NB))
                        if j == 0:
                            ch.link(ins)
                else:
                    ins = dve.tensor_copy(wkT[:, what[1], :], src[:, 0:KVL])
                s_setE.up(ins)
                if n == KD:
                    dve.wait_ge(s_ssx, 1)
                    dve.tensor_scalar(stat[:, 3:6], stat[:, 0:3], 1.0 / D, EPS, ALU.mult, ALU.add).then_inc(s_msx, 1)
            dve.wait_ge(s_sdx, 1)
            ch.link(dve.reciprocal(stat[:, 6:9], stat[:, 3:6]))
            for j in range(3):
                ins = dve.tensor_scalar(diag_x[:, j, :], ident[:, :], stat[:, 6 + j:7 + j], None, ALU.mult)
                if j < 2:
                    ch.link(ins)
                else:
                    ins.then_inc(s_diagx, 1)
            dve.wait_ge(s_wkhi, 1)
            dve.tensor_tensor(wk_lo[:, :, :].rearrange("p k (h d) -> p k h d", h=H), wkv[:, :, :, 0, :],
                              wk_hi[:, :, :].bitcast(F32).rearrange("p k (h d) -> p k h d", h=H), ALU.subtract).then_inc(s_wklo, 1)
            dve.wait_ge(s_bx, 1)
            dve.tensor_copy(rxB[:, :], PM[1][:, 0:T]).then_inc(s_rxB, 1)
            ch.link(dve.tensor_tensor(sel[:, :], ident[:, 0:32], ident[:, 32:64], ALU.add))
            ch.link(dve.tensor_tensor(sel[:, :], sel[:, :], ident[:, 64:96], ALU.add))
            ch.link(dve.tensor_tensor(sel[:, :], sel[:, :], ident[:, 96:128], ALU.add))
            dve.wait_ge(s_small, 16 * N_SMALL)
            ch.link(dve.scalar_tensor_tensor(out=gqk[:, :], in0=gqk[:, :], scalar=SCALE, in1=gk[:, :], op0=ALU.mult, op1=ALU.mult))

            def tile_rest(base, j):
                i = base + j
                tile_hi.wait(dve, i + 1)
                tile_lo.up(dve.tensor_tensor(latT_lo[j % 2][:, :, :], PB[j % 2][:, 0:KVL].rearrange("p (k n) -> p k n", k=KL),
                                             latT_hi[j % 2][:, :, :].bitcast(F32), ALU.subtract))

            def tile_norms(base, j):
                i = base + j
                sq_done.wait(dve, i + 1)
                settle(dve)
                red_done.up(dve.tensor_reduce(rinv[:, ds(i, 1), :].rearrange("p a h -> p (a h)"), sq[j % 2][:, :].rearrange("p (h d) -> p h d", h=H), AX, ALU.add))

            tile_rest(0, 0)
            with dve.Fori(0, NG) as g:
                for k in range(KD):
                    tile_rest(g * KD, k + 1)
                    tile_norms(g * KD, k)
                    if k == KD - 1:
                        modrow_turned.wait(dve, g + 1)
                        for j in range(4):
                            src = PM[1][:, :].rearrange("p (b q) -> p b q", b=4)[:, :, 32 * j:32 * j + NV]
                            bias = bcast(bmodT[:, ds(g * KD + 4 * j, 4)], NV)
                            dst = modT[:, ds(g, 1), 4 * j:4 * j + 4, :].rearrange("p a b v -> p (a b) v")
                            ins = dve.tensor_tensor(dst, src, bias, ALU.add)
                        modT_done.up(ins)
            left = (TILES - NG * KD) // 4
            with dve.Fori(0, left - 1) as i:
                for j in range(4):
                    tile_rest(i * 4 + NG * KD, j + 1)
                    tile_norms(i * 4 + NG * KD, j)
            for j in range(4):
                if j < 3:
                    tile_rest(TILES - 4, j + 1)
                tile_norms(TILES - 4, j)
            def weight_lo(n, k, w, i=0):
                src, hi, lo = wparts(n, k, w)
                w_hi.wait(dve, i * 4 + (n - N_WIN + 1))
                w_lo.up(dve.tensor_tensor(lo, src, hi.bitcast(F32), ALU.subtract))

            def rope(x, j, n, nh, out):
                c = cos[0:n, j:j + 1, :].to_broadcast([n, nh, HALF])
                s = sin[0:n, j:j + 1, :].to_broadcast([n, nh, HALF])
                x1, x2 = x[:, :, 0:HALF], x[:, :, HALF:RP]
                r = [rope_t[q][0:n, 0:nh, :] for q in range(4)]
                for q, (u, v) in enumerate(((x1, c), (x2, s), (x1, s), (x2, c))):
                    ch.link(dve.tensor_tensor(r[q], u, v, ALU.mult))
                ch.link(dve.tensor_tensor(out[:, :, 0:HALF], r[0], r[1], ALU.subtract))
                return dve.tensor_tensor(out[:, :, HALF:RP], r[2], r[3], ALU.add)

            rc = rinv[:, 0:TILES, :]
            for m in range(NZ):
                weight_lo(N_WIN + m, KD, ZW[m])
                if m == 2:
                    red_done.wait(dve, TILES)
                    krs_done.wait(dve, TILES)
                    ch.link(dve.tensor_tensor(rc, rc, bcast(krs[:, 0:TILES], H), ALU.add))
                    dve_b.up(dve.tensor_scalar(rc, rc, 1.0 / QKH, EPS, ALU.mult, ALU.add), "rc_ms")
                if m in (4, 5):
                    act_b.wait(dve, "rc_sd")
                    half = rinv[:, (m - 4) * TILES // 2:(m - 3) * TILES // 2, :]
                    dve_b.up(dve.reciprocal(half, half), f"rc{m - 4}")
                if m == Z_PE + 1:
                    for j, (a, n) in enumerate(TOK):
                        pe_b.wait(dve, f"tok{j}")
                        dve_b.up(dve.tensor_copy(kvtok[0:n, j, :], BANKS[RING_B[f"tok{j}"][0]][0:n, 0:KVL + RP]), f"tok{j}")
                if m == Z_PE + 2:
                    act_b.wait(dve, "kvss")
                    dve_b.up(dve.tensor_scalar(stat[:, 12:15], stat[:, 9:12], 1.0 / KVL, EPS, ALU.mult, ALU.add), "kvms")
                    pe_b.wait(dve, "cqss")
                    dve.tensor_copy(gcol[:, 0:1], BANKS[RING_B["cqss"][0]][:, T:T + 1])
                    dve.tensor_copy(gcol[0:RP, 1:2], BANKS[RING_B["cqss"][0]][0:RP, T + 1:T + 2])
                    dve_b.up(dve.tensor_scalar(rqB[:, :], BANKS[RING_B["cqss"][0]][:, 0:T], 1.0 / QL, EPS, ALU.mult, ALU.add), "cqss")
                if m == Z_PE + 3:
                    act_b.wait(dve, "rqsd")
                    ch.link(dve.reciprocal(rqB[:, :], rqB[:, :]))
                    for k in range(KQ):
                        ins = dve.scalar_tensor_tensor(out=zT[:, k, :], in0=zT[:, k, :], scalar=qaT[:, k:k + 1], in1=rqB[:, :], op0=ALU.mult, op1=ALU.mult)
                    dve_b.up(ins, "cq")
                if m == Z_PE + 4:
                    act_b.wait(dve, "kvsd")
                    ch.link(dve.reciprocal(stat[:, 12:15], stat[:, 12:15]))
                    for j, (a, n) in enumerate(TOK):
                        ch.link(dve.scalar_tensor_tensor(out=lattok[0:n, j, 0:KVL], in0=kvtok[0:n, j, 0:KVL], scalar=stat[0:n, 12 + j:13 + j],
                                                         in1=kvgain[0:n, :], op0=ALU.mult, op1=ALU.mult))
                        ins = rope(kvtok[0:n, j:j + 1, KVL:KVL + RP], j, n, 1, lattok[0:n, j:j + 1, KVL:KVL + RP])
                        if j < 2:
                            ch.link(ins)
                    dve_b.up(ins, "lat")
                    dve_b.wait(dve, "lat")

            for j, (a, n) in enumerate(TOK):
                act_b.wait(dve, f"kn{j}")
                src = (sqk, sqk2, sqk)[j]
                dve_b.up(dve.tensor_reduce(rinv[0:n, TILES + j, :], src[0:n, :].rearrange("p (h d) -> p h d", h=H), AX, ALU.add), f"kn{j}")
            dve_b.wait(dve, "kn2")
            rn = rinv[:, TILES:TILES + 3, :]
            ch.link(dve.tensor_tensor(rn, rn, bcast(krs[:, TILES:TILES + 3], H), ALU.add))
            dve_b.up(dve.tensor_scalar(rn, rn, 1.0 / QKH, EPS, ALU.mult, ALU.add), "rk_ms")
            act_b.wait(dve, "rk_sd")
            dve_b.up(dve.reciprocal(rn, rn), "rinv")
            for j, (a, n) in enumerate(TOK):
                act_b.wait(dve, f"q{j}2")
                x = qtok[0:n, j, :, NOPE:QKH]
                dve_b.up(rope(x, j, n, H, x), f"rope{j}")
                act_b.wait(dve, f"sqq{j}")
                ms = stat[0:n, 16 + 8 * j:24 + 8 * j]
                ch.link(dve.tensor_reduce(ms, sqq[0:n, :].rearrange("p (h d) -> p h d", h=H), AX, ALU.add))
                dve_b.up(dve.tensor_scalar(ms, ms, 1.0 / QKH, EPS, ALU.mult, ALU.add), f"qms{j}")
                act_b.wait(dve, f"qsd{j}")
                ch.link(dve.reciprocal(ms, ms))
                dve_b.up(dve.tensor_tensor(qtok[0:n, j, :, :], qtok[0:n, j, :, :], bcast(ms, QKH), ALU.mult), f"qnorm{j}")
            for j, (a, n) in enumerate(TOK):
                for e in range(2):
                    pe_b.wait(dve, f"qr{j}{e}")
                    src = BANKS[RING_B[f"qr{j}{e}"][0]][0:RP, 0:4 * n].rearrange("p (h n) -> p h n", h=4)
                    dve_b.up(dve.tensor_scalar(qrT[:, 4 * e:4 * e + 4, a:a + n], src, gcol[0:RP, 1:2], None, ALU.mult), f"qr{j}{e}")
            for h in heads:
                pe_b.wait(dve, f"qabs{h}1")
                dve_b.up(dve.tensor_copy(qabs[:, 1, h, :], BANKS[RING_B[f"qabs{h}1"][0]][:, 0:T]), f"qabs{h}1")
            for x, dst, n in (("up", ustate_p, HIST), ("us", ustate, NS)):
                for j in range(2):
                    pe_b.wait(dve, f"{x}{j}")
                    dve_b.up(dve.tensor_copy(dst[:, 512 * j:512 * (j + 1)], BANKS[RING_B[f"{x}{j}"][0]][0:n, :]), f"{x}{j}")
            dve_b.wait(dve, "rinv")
            dve.tensor_copy(rexpN[:, :].rearrange("p (h n) -> p h n", h=H), bcast(rinv[0:NS, TILES + 2, :], NT)).then_inc(s_rexp, 1)
            dve.wait_ge(s_rrow, 1)
            ch.link(dve.tensor_copy(rrowN[:, :], BANKS[6][0:32, 0:NS]))
            dve.sem_inc(s_rexp, 1)
            for x, h in DVE_H:
                s = stp[h % 3]
                if x == "s":
                    if h == 0:
                        dve.wait_ge(s_mask, 32)
                    pe_h.wait(dve, f"S{h}")
                    if h >= 3:
                        pe_h.wait(dve, f"O{h - 3}")
                    ps = BANKS[h % 2]
                    ch.link(dve.scalar_tensor_tensor(out=s[:, 0:S], in0=ps[:, 0:S], scalar=rinv[:, TILES, h:h + 1], in1=causal[:, :], op0=ALU.mult, op1=ALU.add))
                    ch.link(dve.scalar_tensor_tensor(out=s[:, S:S + P], in0=ps[:, S:S + P], scalar=rinv[:, TILES + 1, h:h + 1], in1=causal[:, 0:P], op0=ALU.mult, op1=ALU.add))
                    if h >= 1:
                        pe_h.wait(dve, f"T{h - 1}")
                    dve_h.up(dve.tensor_tensor(mxp[:, 0:P], s[:, P:S], s[:, S:S + P], ALU.max), f"s{h}")
                elif x == "dg":
                    pe_h.wait(dve, f"T{h}")
                    if h >= 1:
                        pe_h.wait(dve, f"B{h - 1}")
                    ch.link(dve.tensor_reduce(stat[:, 40:42], BANKS[2][:, 0:S].rearrange("p (j n) -> p j n", j=2), AX, ALU.max))
                    ch.link(dve.tensor_scalar(dgp[:, 0, :], ident[:, :], stat[:, 40:41], None, ALU.mult))
                    dve_h.up(dve.tensor_scalar(dgp[:, 1, :], ident[:, :], stat[:, 41:42], None, ALU.mult), f"dg{h}")
                elif x == "sub":
                    pe_h.wait(dve, f"B{h}")
                    ch.link(dve.tensor_tensor(s[:, 0:S], s[:, 0:S], BANKS[3][:, 0:S], ALU.subtract))
                    dve_h.up(dve.tensor_tensor(s[:, S:S + P], s[:, S:S + P], BANKS[3][:, P:S], ALU.subtract), f"sub{h}")
                elif x == "rd":
                    pe_h.wait(dve, f"D{h}")
                    dve_h.up(dve.reciprocal(rdps[h % 2][:, :], BANKS[4][:, 0:S]), f"rd{h}")
                elif x == "tmp":
                    pe_h.wait(dve, f"V{h}")
                    dve_h.wait(dve, f"rd{h}")
                    dve_h.up(dve.tensor_tensor(olp[h % 2][:, 0, :], BANKS[6 + h % 2][:, 0:S], rdps[h % 2][:, :], ALU.mult), f"tmp{h}")
                else:
                    act_h.wait(dve, f"hi{h}")
                    if h == 0:
                        pool_b.wait(dve, f"pol{KU - 1}")
                    dve_h.up(dve.tensor_tensor(mix_lo[:, h, 0:S], olp[h % 2][:, 0, :], mix_hi[:, h, 0:S].bitcast(F32), ALU.subtract), f"lo{h}")

            def set_sequence(b, a):
                pv_done.wait(dve, b - 2)
                settle(dve)
                own = ds(b * NT + S, NT)
                heads4 = lambda x: x.rearrange("p (h n) -> p h n", h=H)
                for k in range(KL):
                    dve.tensor_copy(heads4(qseq[a][:, k, :]), qabs[:, k, :, own])
                dve.tensor_copy(heads4(qseq[a][0:RP, 2, :]), qrT[:, :, own])
                dve.memset(pN[a][:, :], 0.0)
                r = rinv[:, ds(b * NPG, NPG), :].rearrange("p j h -> p (j h)")
                seq_set.up(dve.tensor_copy(st[a][:, :, :].rearrange("p j (h n) -> p (j h) n", h=H), bcast(r, NT)))

            def new_keys(b, a):
                pt_kr.up(dve.tensor_tensor(sNew[a], BANKS[6][0:32, ds(b * NT + 2 * P, NT)], rrowN[:, ds(b * NT, NT)], ALU.mult))
                pt_kr.wait(dve, b * NPR + 2)
                ch.link(dve.tensor_tensor(sNew[a], sNew[a], newmask[:, :], ALU.add))
                new_done.up(dve.tensor_reduce(mNew[a][0:32, :], sNew[a], AX, ALU.max))

            def tail_dve(b, a, step):
                s = st[a][:, :, :].rearrange("p j n -> p (j n)")
                if step == "scale":
                    sc_quad.wait(dve, b * 4 + 4)
                    ch.link(dve.tensor_copy(s, BANKS[3]))
                    ch.link(dve.tensor_tensor(s, s, BANKS[2], ALU.mult))
                    ch.link(dve.tensor_reduce(mAll[a], s, AX, ALU.max))
                    new_done.wait(dve, b + 1)
                    sq_scaled.up(dve.tensor_tensor(mAll[a][0:32, :], mAll[a][0:32, :], mNew[a][0:32, :], ALU.max))
                elif step == "max":
                    mx_turned.wait(dve, b + 1)
                    ch.link(dve.tensor_reduce(mrow[:, 0:32], BANKS[4][0:1, 0:P].rearrange("p (g n) -> p n g", g=4), AX, ALU.max))
                    mx_row.up(dve.tensor_copy(mrow[:, 32:P].rearrange("p (g n) -> p g n", g=3), mrow[:, 0:32].unsqueeze(1).to_broadcast([1, 3, 32])))
                elif step == "turned":
                    p_turned.wait(dve, b + 1)
                    dve.tensor_copy(s, BANKS[7])
                    dve.tensor_copy(pN[a][:, :], BANKS[4][0:NS, 0:32])
                    ch.link(dve.tensor_tensor(dAll[a][0:32, :], dAll[a][0:32, :], dNew[a][0:32, :], ALU.add))
                    p_out.up(dve.tensor_scalar(dsel[:, :], sel[:, :], dAll[a], None, ALU.mult))
                else:
                    o_summed.wait(dve, b + 1)
                    ch.link(dve.reciprocal(srd[:, :], BANKS[4][:, P + 32:P + 64]))
                    for k in range(KL):
                        ins = dve.tensor_tensor(olS[:, k, :, ds(b * NT, NT)], BANKS[4][:, P + 64 + 32 * k:P + 96 + 32 * k].rearrange("p (h n) -> p h n", h=H),
                                                srd[:, :].rearrange("p (h n) -> p h n", h=H), ALU.mult)
                    ol_done.up(ins)

            def seq_dve(b, a, r, tail, more):
                done = lambda step: tail and tail_dve(b - 1, (a - 1) % 3, step)
                for p in range(NPR):
                    pt_turned.wait(dve, b * NPR + (p + 1))
                    sc_quad.wait(dve, b * 4 + (p // 2 - 1))
                    dst = latq[p // 2 % 2][0:RP, 2 * (p % 2):2 * (p % 2) + 2, 2, :]
                    ins = dve.tensor_copy(dst, BANKS[5 + p % 2][0:RP, 0:2 * P].rearrange("p (e n) -> p e n", e=2))
                    if p == 1:
                        ch.link(ins)
                        new_keys(b, a)
                    else:
                        pt_kr.up(ins)
                    if p == 0:
                        done("scale")
                    elif p == 3:
                        done("max")
                    elif p == 5:
                        done("turned")
                    elif p == 6 and more:
                        set_sequence(b + 1, (a + 1) % 3)
                done("out")

            set_sequence(0, 0)
            sequences(lambda n: ch.loop(n, 3 * 8), seq_dve)
            for step in ("scale", "max", "turned", "out"):
                tail_dve(NB - 1, (NB - 1) % 3, step)
            dve.wait_ge(s_vhi, 1)
            dve.tensor_tensor(mix_lo[:, 0:H, S:T], BANKS[7][:, 0:H * NS].rearrange("p (h n) -> p h n", h=H),
                              mix_hi[:, 0:H, S:T].bitcast(F32), ALU.subtract).then_inc(s_mixs, 1)

            def gated(dst, old, ps, g, m, up, by):
                gate = modT[:, g, ds(m, 1), :].rearrange("p a v -> p (a v)")
                seqs = lambda x: x.rearrange("p (b n) -> p b n", b=NB)
                ch.link(dve.tensor_tensor(seqs(dtmp[:, :]), seqs(ps[:, S:T]), bcast(gate[:, 1:NV], NT), ALU.mult))
                ch.link(dve.tensor_tensor(tmpC[2][:, 0:S], ps[:, 0:S], gate[:, 0:1].to_broadcast([P, S]), ALU.mult))
                ch.link(dve.tensor_tensor(dst[:, S:T], old[:, S:T], dtmp[:, :], ALU.add))
                up(dve.tensor_tensor(dst[:, 0:S], old[:, 0:S], tmpC[2][:, 0:S], ALU.add))

            weight_lo(N_WOUT, KD, P)

            def out_tile(j, i):
                piece_done.wait(dve, i * 4 + (NZ + j + 1))
                x = xT[:, ds(i * 4 + j, 1), :].rearrange("p a n -> p (a n)")
                gated(x, x, PB[(NZ + j) % 2], 2, i * 4 + j, piece_out.up, None)

            with ch.loop(KD // 4 - 1, 12) as i:
                for j in range(4):
                    weight_lo(N_WOUT + j + 1, KD, P, i)
                    out_tile(j, i)
            for j in range(4):
                weight_lo(N_WOUT + KD - 4 + j + 1, KD, P)
                out_tile(j, KD // 4 - 1)
            x1_ss.wait(dve, KD)
            dve.tensor_scalar(rn2[:, :], PM[0][:, 0:T], 1.0 / D, EPS, ALU.mult, ALU.add).then_inc(s_ms2, 1)
            dve.wait_ge(s_sd2, 1)
            dve.reciprocal(rn2[:, :], rn2[:, :]).then_inc(s_rn2, 1)
            dve.wait_ge(s_rn2, 1)
            piece_out.wait(dve, NZ + KD)

            def h2_rest(k):
                h2_hi.wait(dve, k + 1)
                h2_lo.up(dve.tensor_tensor(hT_lo[:, k, :], h2t[k % 4][:, :], hT_hi[:, k, :].bitcast(F32), ALU.subtract))

            for k in range(KD):
                if k >= 4:
                    h2_lo.wait(dve, k - 3)
                h2_t.up(dve.tensor_tensor(h2t[k % 4][:, :], xT[:, k, :], rn2[:, :], ALU.mult))
                if k >= 2:
                    h2_rest(k - 2)
            h2_rest(KD - 2)
            h2_rest(KD - 1)


            def activate(f, a, i=0):
                n = N_FFN + f * NP_FF + 2 * a + 1 - N_WIN
                piece_done.wait(dve, i * 4 + (n + 1))
                ff_silu.wait(dve, i * 2 + (f * HF + a + 1))
                ff_split.wait(dve, i * 2 + (f * HF + a - 1))
                ff_act.up(dve.tensor_tensor(act32[a][:, :], sg[a][:, :], PK[1][:, a, 0:T], ALU.mult))

            def down_tile(f, a, i):
                n = N_FFN + f * NP_FF + 2 * HF + 2 * a + 1 - N_WIN
                piece_done.wait(dve, i * 4 + (n + 1))
                x = xT[:, ds(i * 2 + a, 1), :].rearrange("p a n -> p (a n)")
                if f:
                    y_turned.wait(dve, i * 2 + (a - 1))
                gated(yT[a] if f else x, x, PB[a], 5, i * 2 + a, down_out.up, None)

            for f in range(2):
                n0 = N_FFN + f * NP_FF
                n1 = n0 + 2 * HF
                with dve.Fori(0, HF // 2 - 1) as i:
                    for j in range(4):
                        weight_lo(n0 + j + 1, KD, P, i)
                        if j % 2:
                            activate(f, j // 2, i)
                last = HF // 2 - 1
                for j in range(4):
                    n = n0 + 4 * last + j + 1
                    weight_lo(n, HD if n == n1 else KD, P)
                    if j % 2:
                        activate(f, j // 2, last)
                last = KD // 2 - 1
                with ch.loop(last, 6) as i:
                    for j in range(4):
                        weight_lo(n1 + j + 1, HD, P, i)
                        if j % 2:
                            down_tile(f, j // 2, i)
                for j in range(4):
                    if f == 0 or j < 3:
                        weight_lo(n1 + 4 * last + j + 1, KD if j == 3 else HD, P)
                    if j % 2:
                        down_tile(f, j // 2, last)

        @block.tensor
        def _(pe):
            tile_turned.open(pe)
            pt_turned.open(pe)
            pv_done.open(pe)
            x1_ss.open(pe)
            keys_done.open(pe)
            mod_step.open(pe)
            for signal in (modrow_turned, o_summed, sc_quad, y_turned):
                signal.open(pe)
            pe.wait_ge(s_const, 16)
            for n, (what, parts) in enumerate(SETUP):
                if n == 0:
                    pe.wait_ge(s_c, 16)
                if what == "vec":
                    pe.wait_ge(s_small, 16 * N_SMALL)
                if what == ("x", 0):
                    pe.wait_ge(s_x, 48)
                if what == ("wk", 0):
                    pe.wait_ge(s_wkv, 16)
                if n == 2:
                    pe.wait_ge(s_cs, 1)
                elif n > 2:
                    s_setE.wait(pe, n - 1 - 1)
                for a, w, src, rows in parts:
                    ins = pe.transpose(PB[n % 2][0:rows, a:a + w], src, ident[0:w, 0:w])
                ins.then_inc(s_setT, 1)
            pe.wait_ge(s_diagx, 1)
            pe.wait_ge(s_zero, 1)
            for j, (a, n) in enumerate(TOK):
                ins = pe.matmul(PM[1][:, a:a + n], ones[0:n, :], diag_x[0:n, j, 0:n], start=True, stop=True)
            ins.then_inc(s_bx, 1)

            def turn(base, j):
                i = base + j
                pe.wait_ge(page_full[j % 4], (base + (j // 4) * 4) * 8 + 32)
                tile_lo.wait(pe, i - 1)
                for k in range(KL):
                    ins = pe.transpose(PB[j % 2][:, k * P:(k + 1) * P], pg[j % 4][:, k * P:(k + 1) * P], ident[:, :])
                tile_turned.up(ins)

            def mod(g, k):
                pe.wait_ge(raw_full[k % 4], (g * KD + (k // 4) * 4) * 4 + 16)
                if k == 0:
                    modrow_done.wait(pe, g)
                for j in range(4):
                    ins = pe.matmul(PM[0][32 * j:32 * j + 32, :], cs[:, k, :], raw[k % 4][:, 512 * j:512 * (j + 1)],
                                    start=(k == 0), stop=(k == KD - 1), tile_position=(0, 32 * j))
                mod_step.up(ins)

            def keys(base, j):
                i = base + j
                tile_lo.wait(pe, i + 1)
                sq_done.wait(pe, i - 1)
                for n, (L, W) in enumerate(((latT_hi, wk_hi), (latT_hi, wk_lo), (latT_lo, wk_hi))):
                    for k in range(KL):
                        for a in range(2):
                            ins = pe.matmul(PK[j % 2][:, a, :], L[j % 2][:, k, :], W[:, k, 512 * a:512 * (a + 1)],
                                            start=(n == 0 and k == 0), stop=(n == 2 and k == KL - 1))
                keys_done.up(ins)

            s_setE.wait(pe, NSET - 1)
            turn(0, 0)
            pe.wait_ge(s_wklo, 1)
            pe.wait_ge(s_cs, 1)
            pe.wait_ge(s_rxB, 1)
            with pe.Fori(0, NG) as g:
                for k in range(KD):
                    turn(g * KD, k + 1)
                    mod(g, k)
                    keys(g * KD, k)
                modrow_done.wait(pe, g + 1)
                modT_done.wait(pe, g)
                for b in range(4):
                    ins = pe.transpose(PM[1][:, b * P:(b + 1) * P], modrow[:, b * P:(b + 1) * P], ident[:, :])
                modrow_turned.up(ins)
            left = (TILES - NG * KD) // 4
            with pe.Fori(0, left - 1) as i:
                for j in range(4):
                    turn(i * 4 + NG * KD, j + 1)
                    keys(i * 4 + NG * KD, j)
            for j in range(4):
                if j < 3:
                    turn(TILES - 4, j + 1)
                keys(TILES - 4, j)
            def passes(out, n, rhs_hi, rhs_lo, k, w, first=True, last=True, ready=None):
                _, hi, lo = wparts(n, k, w)
                for q in range(k):
                    if ready:
                        ready(q)
                    for e, (a, b) in enumerate(((hi, rhs_hi), (hi, rhs_lo), (lo, rhs_hi))):
                        ins = pe.matmul(out, a[:, q, :], b[:, q, :], start=(first and q == 0 and e == 0), stop=(last and q == k - 1 and e == 2))
                piece_done.up(ins)

            last_use = {}

            def banks(name):
                for b in RING_B[name]:
                    if b in last_use:
                        x = last_use[b]
                        (dve_b if x in BY_DVE else act_b).wait(pe, x)
                    last_use[b] = name
                return BANKS[RING_B[name][0]]

            pe.wait_ge(s_hT, KD)
            for m in range(NZ):
                w_lo.wait(pe, m + 1)
                piece_out.wait(pe, m - 1)
                passes(PB[m % 2][0:ZW[m], 0:T], N_WIN + m, hT_hi, hT_lo, KD, ZW[m])
                if m == Z_PE:
                    sq_done.wait(pe, TILES)
                    modT_done.wait(pe, NG)
                    act_b.wait(pe, "sqz")
                    out = banks("cqss")
                    for k in range(KQ):
                        ins = pe.matmul(out[:, 0:T], ones[:, :], sqz[:, k, :], start=(k == 0), stop=(k == KQ - 1))
                    pe.matmul(out[:, T:T + 1], gqk[:, 0:NOPE], ident[:, 0:1], start=True, stop=True)
                    ins = pe.matmul(out[0:RP, T + 1:T + 2], gqk[:, NOPE:QKH], ident[:, 0:1], start=True, stop=True)
                    pe_b.up(ins, "cqss")
                    for j, (a, n) in enumerate(TOK):
                        out = banks(f"tok{j}")
                        for k in range(KL):
                            pe.transpose(out[0:n, k * P:(k + 1) * P], zT[:, KQ + k, a:a + n], ident[:, :])
                        pe_b.up(pe.transpose(out[0:n, KVL:KVL + RP], zT[0:RP, KQ + KL, a:a + n], ident[0:RP, 0:RP]), f"tok{j}")
            piece_out.wait(pe, NZ)
            dve_b.wait(pe, "lat")
            for x, c0, w in (("latT0", 0, P), ("latT1", P, P), ("krT", KVL, RP)):
                out = banks(x)
                for j, (a, n) in enumerate(TOK):
                    ins = pe.transpose(out[0:w, a:a + n], lattok[0:n, j, c0:c0 + w], ident[0:n, 0:n])
                pe_b.up(ins, x)
            act_b.wait(pe, "latT1")
            for j, (a, n) in enumerate(TOK):
                banks(f"kn{j}")
                for e in range(2):
                    for k in range(KL):
                        ins = pe.matmul(PK[j % 2][0:n, e, :], latTn[:, k, a:a + n], wkv[:, k, 4 * e:4 * e + 4, 0, :], start=(k == 0), stop=(k == KL - 1))
                pe_b.up(ins, f"kn{j}")
            pe.wait_ge(s_wqb, 32)
            for j, (a, n) in enumerate(TOK):
                for c in range(3):
                    out = banks(f"q{j}{c}")
                    for k in range(KQ):
                        ins = pe.matmul(out[0:n, :], zT[:, k, a:a + n], wqb[:, k, 512 * c:512 * (c + 1)], start=(k == 0), stop=(k == KQ - 1))
                    pe_b.up(ins, f"q{j}{c}")
            pe.wait_ge(s_wpool, 16)
            for m in range(KU):
                g, e = m // 2, m % 2
                pool_b.wait(pe, f"d{g}")
                out = banks(f"po{m}")
                for k in range(2):
                    ins = pe.matmul(out[:, 0:T], wpool[:, g, k, e * P:(e + 1) * P], dT[g][:, k, :], start=(k == 0), stop=(k == 1))
                pe_b.up(ins, f"po{m}")
            for j, (a, n) in enumerate(TOK):
                dve_b.wait(pe, f"qnorm{j}")
                for x, c0, w in (("qn", 0, NOPE), ("qr", NOPE, RP)):
                    for e in range(2):
                        out = banks(f"{x}{j}{e}")
                        for q in range(4):
                            ins = pe.transpose(out[0:w, q * n:(q + 1) * n], qtok[0:n, j, 4 * e + q, c0:c0 + w], ident[0:n, 0:n])
                        pe_b.up(ins, f"{x}{j}{e}")
            act_b.wait(pe, "qn21")
            for h in heads:
                for k in range(KL):
                    out = banks(f"qabs{h}{k}")
                    pe_b.up(pe.matmul(out[:, 0:T], wkT[:, h, k * P:(k + 1) * P], qnT[:, h, :], start=True, stop=True), f"qabs{h}{k}")
            for x in ("up", "us"):
                if x == "us":
                    pool_b.wait(pe, "unew")
                for j in range(2):
                    out = banks(f"{x}{j}")
                    for q in range(4):
                        m = 4 * j + q
                        if x == "up":
                            src, n = uext[:, m, S:S + HIST], HIST
                        else:
                            src, n = unew[:, m, :], NS
                        ins = pe.transpose(out[0:n, q * P:(q + 1) * P], src, ident[:, :])
                    pe_b.up(ins, f"{x}{j}")
            def claim(b):
                x = last_use[b]
                (dve_b if x in BY_DVE else act_b).wait(pe, x)

            FIRST = {("S", 0): 0, ("S", 1): 1, ("T", 0): 2, ("B", 0): 3, ("D", 0): 4, ("O", 0): 5, ("V", 0): 6, ("V", 1): 7}
            pe.wait_ge(s_rexp, 1)
            claim(6)
            pe.matmul(BANKS[6][0:32, 0:NS], rexpN[:, :], ident[0:NS, 0:NS], start=True, stop=True).then_inc(s_rrow, 1)
            for x, h in PE_H:
                if (x, h) in FIRST:
                    claim(FIRST[x, h])
                if x == "S":
                    act_b.wait(pe, f"qabs{h}0")
                    dve_b.wait(pe, f"qabs{h}1")
                if (x, h) == ("V", 0):
                    pe.wait_ge(s_rexp, 2)
                s = stp[h % 3]
                if x == "S":
                    if h >= 2:
                        dve_h.wait(pe, f"s{h - 2}")
                    for a, c0 in ((0, 0), (1, S)):
                        out = BANKS[h % 2][:, c0:c0 + S - a * P]
                        keys_ = slice(a * P, (a + 1) * P)
                        for k in range(KL):
                            pe.matmul(out, latTn[:, k, keys_], qabs[:, k, h, a * P:S], start=(k == 0), stop=False)
                        ins = pe.matmul(out, krTn[:, keys_], qrT[:, h, a * P:S], start=False, stop=True)
                elif x == "T":
                    dve_h.wait(pe, f"s{h}")
                    if h:
                        dve_h.wait(pe, f"dg{h - 1}")
                    pe.transpose(BANKS[2][:, 0:P], s[:, 0:P], ident[:, :])
                    ins = pe.transpose(BANKS[2][:, P:S], mxp[:, 0:P], ident[:, :])
                elif x == "B":
                    dve_h.wait(pe, f"dg{h}")
                    if h:
                        dve_h.wait(pe, f"sub{h - 1}")
                    ins = pe.matmul(BANKS[3][:, 0:S], ones[:, :], dgp[:, :, :].rearrange("p j n -> p (j n)"), start=True, stop=True)
                elif x == "D":
                    act_h.wait(pe, f"exp{h}")
                    if h:
                        dve_h.wait(pe, f"rd{h - 1}")
                    pe.matmul(BANKS[4][:, 0:P], ones[:, :], s[:, 0:P], start=True, stop=True)
                    pe.matmul(BANKS[4][:, P:S], ones[:, :], s[:, P:S], start=True, stop=False)
                    ins = pe.matmul(BANKS[4][:, P:S], ones[:, :], s[:, S:S + P], start=False, stop=True)
                elif x == "O":
                    if h:
                        act_h.wait(pe, f"O{h - 1}")
                    for k in range(KL):
                        latk, c0 = slice(k * P, (k + 1) * P), k * S
                        pe.matmul(BANKS[5][:, c0:c0 + P], lattok[:, 0, latk], s[:, 0:P], start=True, stop=True)
                        pe.matmul(BANKS[5][:, c0 + P:c0 + S], lattok[:, 0, latk], s[:, P:S], start=True, stop=False)
                        ins = pe.matmul(BANKS[5][:, c0 + P:c0 + S], lattok[:, 1, latk], s[:, S:S + P], start=False, stop=True)
                else:
                    act_h.wait(pe, f"O{h}")
                    if h >= 2:
                        dve_h.wait(pe, f"tmp{h - 2}")
                    for k in range(KL):
                        ins = pe.matmul(BANKS[6 + h % 2][:, 0:S], wkv[:, k, h, 1, :], olp[h % 2][:, k, :], start=(k == 0), stop=(k == KL - 1))
                pe_h.up(ins, f"{x}{h}")
            dve_h.wait(pe, f"tmp{H - 1}")
            K3 = [(0, P), (1, P), (2, RP)]

            def turn_pair(b, a, r, p):
                i = b * NPR + p
                if p % 2 == 0:
                    pe.wait_ge(lat_full[a][p // 2], r * 64 + 64)
                    pe.wait_ge(kr_full[p // 2], b * (32 if p == 6 else 64) + (32 if p == 6 else 64))
                if p == 7:
                    pe.wait_ge(kr_last, b * 32 + 32)
                pt_lat.wait(pe, i - 1)
                pt_kr.wait(pe, i - 1)
                for e in range(2):
                    for k in range(KL):
                        x = 2 * e + k
                        pe.transpose(BANKS[p % 2][:, x * P:(x + 1) * P], lat_pg[a][2 * p + e][:, k * P:(k + 1) * P], ident[:, :])
                for e in range(2):
                    ins = pe.transpose(BANKS[5 + p % 2][0:RP, e * P:(e + 1) * P], kr_pg[2 * p + e][:, :], ident[:, :])
                if p == 1:
                    seq_set.wait(pe, b + 1)
                    for (k, rows), x in zip(K3, (latTn[:, 0, S:T], latTn[:, 1, S:T], krTn[:, S:T])):
                        ins = pe.matmul(BANKS[6][0:32, 2 * P:2 * P + NS], qseq[a][0:rows, k, :], x, start=(k == 0), stop=(k == 2))
                pt_turned.up(ins)

            def spread_norms(b, a):
                sq_scaled.wait(pe, b)
                for c in range(4):
                    for g in range(4):
                        pe.matmul(BANKS[3][32 * g:32 * g + 32, c * P:(c + 1) * P], st[a][:, 4 * c + g, :], ident[:, :], start=True, stop=True,
                                  tile_position=(0, 32 * g))

            def quad_scores(b, a, c):
                i = b * NPR + 2 * c
                pt_lat.wait(pe, i + 2)
                pt_kr.wait(pe, i + 2)
                for k, rows in K3:
                    for g in range(4):
                        ins = pe.matmul(BANKS[2][32 * g:32 * g + 32, c * P:(c + 1) * P], qseq[a][0:rows, k, :], latq[c % 2][0:rows, g, k, :],
                                        start=(k == 0), stop=(k == 2), tile_position=(0, 32 * g))
                sc_quad.up(ins)

            def tail_pe(b, a, step):
                T4 = BANKS[4]
                if step == "T":
                    sq_scaled.wait(pe, b + 1)
                    ol_done.wait(pe, b)
                    mx_turned.up(pe.transpose(T4[0:1, 0:P], mAll[a], ident[:, :]))
                elif step == "B":
                    mx_row.wait(pe, b + 1)
                    mx_spread.up(pe.matmul(T4[:, P:P + 1], mrow[:, :], neg1[:, :], start=True, stop=True))
                elif step == "P":
                    exp_done.wait(pe, b + 1)
                    for c in range(4):
                        pe.transpose(BANKS[7][:, c * P:(c + 1) * P], st[a][:, 4 * c:4 * c + 4, :].rearrange("p j n -> p (j n)"), ident[:, :])
                    p_turned.up(pe.transpose(T4[0:NS, 0:32], pN[a][:, :], ident[0:32, 0:32]))
                elif step == "PV":
                    p_out.wait(pe, b + 1)
                    pe.matmul(T4[:, P + 32:P + 64], ones[:, :], dsel[:, :], start=True, stop=True)
                    for c in range(4):
                        for g in range(4):
                            pe.matmul(T4[32 * g:32 * g + 32, KVL:2 * KVL], st[a][:, 4 * c + g, :], lat_pg[a][4 * c + g][:, :],
                                      start=(c == 0), stop=(c == 3 and g > 0), tile_position=(0, 32 * g))
                    pv_done.up(pe.matmul(T4[0:32, KVL:2 * KVL], pN[a][:, :], lattok[0:NS, 2, 0:KVL], start=False, stop=True, tile_position=(0, 0)))
                else:
                    o_out.wait(pe, b + 1)
                    for k in range(KL):
                        ins = pe.matmul(T4[:, P + 64 + 32 * k:P + 96 + 32 * k], o_part[:, k * P:(k + 1) * P], sel[:, :], start=True, stop=True)
                    o_summed.up(ins)

            def seq_pe(b, a, r, tail, more):
                done = lambda step: tail and tail_pe(b - 1, (a - 1) % 3, step)
                turn_pair(b, a, r, 0)
                turn_pair(b, a, r, 1)
                turn_pair(b, a, r, 2)
                done("T")
                turn_pair(b, a, r, 3)
                quad_scores(b, a, 0)
                done("B")
                turn_pair(b, a, r, 4)
                spread_norms(b, a)
                quad_scores(b, a, 1)
                done("P")
                turn_pair(b, a, r, 5)
                turn_pair(b, a, r, 6)
                quad_scores(b, a, 2)
                done("PV")
                turn_pair(b, a, r, 7)
                quad_scores(b, a, 3)
                done("C")

            sequences(lambda n: pe.Fori(0, n), seq_pe)
            for step in ("T", "B", "P", "PV", "C"):
                tail_pe(NB - 1, (NB - 1) % 3, step)
            ol_done.wait(pe, NB)
            for h in heads:
                for k in range(KL):
                    ins = pe.matmul(BANKS[7][:, NS * h:NS * (h + 1)], wkv[:, k, h, 1, :], olS[:, k, h, :], start=(k == 0), stop=(k == KL - 1))
            ins.then_inc(s_vs, 1)

            pe.wait_ge(s_mixs, 1)
            pool_b.wait(pe, f"pol{KU - 1}")

            def ss_x1(j, i, first=False, last=False):
                x1_sq.wait(pe, i * 4 + (j + 1))
                x1_ss.up(pe.matmul(PM[0][:, 0:T], ones[:, :], tmpC[j % 2][:, :], start=first, stop=last, skip_group_check=True))

            def out_piece(j, i):
                w_lo.wait(pe, i * 4 + (NZ + j + 1))
                piece_out.wait(pe, i * 4 + (NZ + j - 1))
                passes(PB[(NZ + j) % 2][:, 0:T], N_WOUT + j, mix_hi, mix_lo, KD, P)

            for j in range(4):
                out_piece(j, 0)
                if j:
                    ss_x1(j - 1, 0, first=(j == 1))
            with pe.Fori(0, KD // 4 - 1) as i:
                for j in range(4):
                    out_piece(j + 4, i)
                    ss_x1(j + 3, i)
            ss_x1(3, KD // 4 - 1, last=True)


            def ff_piece(f, j, i, first=False):
                n = N_FFN + f * NP_FF + j
                w_lo.wait(pe, i * 4 + (n - N_WIN + 1))
                ff_act.wait(pe, i * 2 + (f * HF + j // 2 - 1))
                ready = (lambda q: h2_lo.wait(pe, q + 1)) if first else None
                passes(PK[j % 2][:, j // 2, 0:T], n, hT_hi, hT_lo, KD, P, ready=ready)

            def down_piece(f, j, i):
                n = N_FFN + f * NP_FF + 2 * HF + j
                w_lo.wait(pe, i * 4 + (n - N_WIN + 1))
                if j % 2 == 0:
                    down_out.wait(pe, i * 2 + (f * KD + j // 2 - 1))
                h = j % 2
                passes(PB[j // 2][:, 0:T], n, aT_hi[:, h * HD:(h + 1) * HD, :], aT_lo[:, h * HD:(h + 1) * HD, :], HD, P, first=(h == 0), last=(h == 1))

            def turn_y(a, i):
                down_out.wait(pe, i * 2 + (KD + a + 1))
                y_out.wait(pe, i * 2 + (a - 1))
                for j, (c, n) in enumerate(TOK):
                    ins = pe.transpose(PM[a][0:n, j * P:(j + 1) * P], yT[a][:, c:c + n], ident[:, :])
                y_turned.up(ins)

            for f in range(2):
                if f == 0:
                    for j in range(4):
                        ff_piece(0, j, 0, first=(j == 0))
                    with pe.Fori(0, HF // 2 - 1) as i:
                        for j in range(4):
                            ff_piece(0, j, i + 1)
                else:
                    with pe.Fori(0, HF // 2) as i:
                        for j in range(4):
                            ff_piece(1, j, i)
                ff_split.wait(pe, (f + 1) * HF)
                if f == 0:
                    with pe.Fori(0, KD // 2) as i:
                        for j in range(4):
                            down_piece(0, j, i)
                else:
                    for j in range(4):
                        down_piece(1, j, 0)
                        if j >= 2 and j % 2:
                            turn_y(0, 0)
                    with pe.Fori(0, KD // 2 - 1) as i:
                        for j in range(4):
                            down_piece(1, j, i + 1)
                            if j == 1:
                                turn_y(1, i)
                            if j == 3:
                                turn_y(0, i + 1)
                    turn_y(1, KD // 2 - 1)


_INS = ["x_prompt", "x_sample", "cache_kv_latent", "cache_k_rope", "state_pool", "page_table", "w_mod", "b_mod", "norm1", "w_in",
        "q_a_norm", "w_q_b", "kv_a_norm", "w_kv_b", "q_norm_nope", "q_norm_rope", "k_norm_nope", "k_norm_rope", "w_pool", "b_pool",
        "pool_scale", "w_out", "norm2", "w_gate", "w_up", "w_down"]


def _constants(S, past, NT, NB, RP, heads):
    inv = np.float32(1.0) / (ROPE_THETA ** (np.arange(0, RP, 2) / RP)).astype(np.float32)
    pos = np.zeros((3, P), np.float32)
    pos[0], pos[1] = np.arange(P), np.arange(P, 2 * P)
    pos[2, 0:NB * NT] = past + np.tile(np.arange(NT), NB)
    ang = (pos[:, :, None] * inv).astype(np.float32).transpose(1, 0, 2).astype(np.float64)
    key, query = np.arange(P)[:, None], np.arange(2 * P)[None, :]
    ratio = np.ones((4, 16), np.float32)
    for g, w in enumerate(POOL_WINDOWS):
        ratio[g, 0:w - 1] = w / np.arange(1, w)
    return {
        "c_ident": np.eye(P, dtype=np.float32),
        "c_cos": np.ascontiguousarray(np.cos(ang), np.float32),
        "c_sin": np.ascontiguousarray(np.sin(ang), np.float32),
        "c_causal": np.where(key <= query, 0.0, NEG).astype(np.float32),
        "c_newmask": np.where(np.arange(NT)[None, :] <= np.arange(heads * NT)[:, None] % NT, 0.0, NEG).astype(np.float32),
        "c_ratio": np.ascontiguousarray(np.broadcast_to(ratio, (P, 4, 16))),
    }


def kernel(**inputs):
    import concourse.bacc as _bacc
    from concourse.bass_utils import run_bass_kernel_spmd as _run

    a = {n: np.ascontiguousarray(inputs[n]) for n in _INS}
    a["c_all"] = np.concatenate([np.asarray(inputs["c_prompt"]), np.asarray(inputs["c_sample"])], axis=0)
    B, S, D = a["x_prompt"].shape
    NB, NT = a["x_sample"].shape[:2]
    KVL, RP = a["cache_kv_latent"].shape[3], a["cache_k_rope"].shape[3]
    HIST, PW = a["state_pool"].shape[2:]
    past = a["page_table"].shape[1] * a["cache_kv_latent"].shape[2]
    heads = a["w_q_b"].shape[2] // (a["q_norm_nope"].shape[1] + RP)
    a.update(_constants(S, past, NT, NB, RP, heads))
    outs = {"y_p": (B, S, D), "y_s": (NB, NT, D), "lat_p": (1, B, S, KVL), "kr_p": (1, B, S, RP), "pool_p": (1, B, HIST, PW),
            "lat_s": (1, NB, NT, KVL), "kr_s": (1, NB, NT, RP), "pool_s": (1, NB, HIST, PW)}
    nc = _bacc.Bacc("TRN2", target_bir_lowering=False, num_devices=1)
    t = {n: nc.dram_tensor(f"in_{n}", v.shape, mybir.dt.from_np(v.dtype), kind="ExternalInput").ap() for n, v in a.items()}
    o = {n: nc.dram_tensor(f"out_{n}", s, F32, kind="ExternalOutput").ap() for n, s in outs.items()}
    hybrid_step(nc, t, o)
    r = _run(nc, [{f"in_{n}": v for n, v in a.items()}], core_ids=[0])
    return tuple(r.results[0][f"out_{n}"] for n in outs)
```
